# Optimizing a Trainium2 kernel written in Bass

```python
import jax, jax.numpy as jnp
from jax import lax
import numpy as np
import math

D_MODEL = 1024
BATCH = 1
SEQ = 256
DEPTH = 1

CHUNK = 64
EPS = 1e-6
D_MIX = D_MODEL
D_A = D_MIX // 2
A_HEADS = 4
A_HEAD_DIM = D_A // A_HEADS
GMLP_BLOCK = 128
D_B = D_MIX - D_A
B_HEADS = 4
B_KEY_DIM = D_B // B_HEADS
B_VAL_DIM = D_B // B_HEADS
D_BK = B_HEADS * B_KEY_DIM
D_BV = B_HEADS * B_VAL_DIM
D_IN = 2 * D_A + 2 * D_BK + 2 * D_BV
N_GROUPS = 4
EXPERTS_PER_GROUP = 8
N_EXPERTS = N_GROUPS * EXPERTS_PER_GROUP
TOP_K_IN_GROUP = 2
D_EXPERT = D_MODEL // 2
MOE_BLOCK = 256


def rms_norm(x, gain):
    xf = x.astype(jnp.float32)
    y = xf * lax.rsqrt(jnp.mean(xf * xf, axis=-1, keepdims=True) + EPS)
    return (y * gain.astype(jnp.float32)).astype(x.dtype)

def gmlp_mixer(u, v, v_gain, w_s, b_s):
    bn, s, _ = u.shape
    nb = s // GMLP_BLOCK
    vh = rms_norm(v.reshape(bn, s, A_HEADS, A_HEAD_DIM), v_gain.reshape(A_HEADS, A_HEAD_DIM))
    vh = vh.reshape(bn, nb, GMLP_BLOCK, A_HEADS, A_HEAD_DIM)
    chunk_id = jnp.arange(GMLP_BLOCK) // CHUNK
    mask = chunk_id[None, :] <= chunk_id[:, None]
    w = jnp.where(mask[None], w_s, jnp.zeros_like(w_s))
    mixed = jnp.einsum('gij,bnjgc->bnigc', w, vh) + jnp.transpose(b_s)[:, :, None]
    return u * mixed.reshape(bn, s, D_A).astype(u.dtype)

def hgrn2_mixer(q_raw, f_raw, i_raw, g_raw, lb, out_gain):
    bn, s, _ = q_raw.shape
    n = s // CHUNK
    f32 = jnp.float32
    q = jax.nn.silu(q_raw.astype(f32))
    f = lb + (1.0 - lb) * jax.nn.sigmoid(f_raw.astype(f32))
    k = 1.0 - f
    lf = jnp.log(f)

    def split(t, d):
        return t.reshape(bn, n, CHUNK, B_HEADS, d).transpose(0, 3, 1, 2, 4)

    q, k, lf = split(q, B_KEY_DIM), split(k, B_KEY_DIM), split(lf, B_KEY_DIM)
    v = split(i_raw.astype(f32), B_VAL_DIM)
    b = lax.cumsum(lf, axis=3)
    ref = b[:, :, :, CHUNK // 2 - 1:CHUNK // 2, :]
    qe = q * jnp.exp(b - ref)
    ke = k * jnp.exp(ref - b)
    causal = jnp.tril(jnp.ones((CHUNK, CHUNK), dtype=bool))
    scores = jnp.einsum('bhncd,bhnsd->bhncs', qe, ke)
    scores = jnp.where(causal, scores, 0.0)
    o_intra = jnp.einsum('bhncs,bhnse->bhnce', scores, v)
    b_last = b[:, :, :, -1:, :]
    u_state = jnp.einsum('bhnsd,bhnse->bhnde', k * jnp.exp(b_last - b), v)
    decay = jnp.exp(b_last[:, :, :, 0, :])

    def step(state, xs):
        dec, upd = xs
        return dec[..., None] * state + upd, state

    s0 = jnp.zeros((bn, B_HEADS, B_KEY_DIM, B_VAL_DIM), f32)
    _, s_prev = lax.scan(step, s0, (jnp.moveaxis(decay, 2, 0), jnp.moveaxis(u_state, 2, 0)))
    s_prev = jnp.moveaxis(s_prev, 0, 2)
    o_inter = jnp.einsum('bhncd,bhnde->bhnce', q * jnp.exp(b), s_prev)
    o = (o_intra + o_inter).transpose(0, 2, 3, 1, 4).reshape(bn, s, B_HEADS, B_VAL_DIM)
    o = rms_norm(o, out_gain.reshape(B_HEADS, B_VAL_DIM))
    o = o * jax.nn.silu(g_raw.reshape(bn, s, B_HEADS, B_VAL_DIM).astype(f32))
    return o.reshape(bn, s, D_BV).astype(q_raw.dtype)

def hier_moe(xn, w_gr, b_gr, w_er, b_er, w_gate, w_up, w_down):
    bn, s, d = xn.shape
    t = bn * s
    xt = xn.reshape(t, d)
    f32 = jnp.float32
    g_logits = (xt @ w_gr).astype(f32) + b_gr.astype(f32)
    g_probs = jax.nn.softmax(g_logits, axis=-1)
    g_idx = jnp.argmax(g_logits, axis=-1)
    g_prob = jnp.take_along_axis(g_probs, g_idx[:, None], axis=1)[:, 0]
    e_logits = ((xt @ w_er).astype(f32) + b_er.astype(f32)).reshape(t, N_GROUPS, EXPERTS_PER_GROUP)
    e_logits = jnp.take_along_axis(e_logits, g_idx[:, None, None], axis=1)[:, 0]
    top_v, top_i = lax.top_k(e_logits, TOP_K_IN_GROUP)
    wts = g_prob[:, None] * jax.nn.softmax(top_v, axis=-1)
    eid = (g_idx[:, None] * EXPERTS_PER_GROUP + top_i).reshape(-1).astype(jnp.int32)
    tok = jnp.repeat(jnp.arange(t, dtype=jnp.int32), TOP_K_IN_GROUP)
    wt = wts.reshape(-1)
    n_assign = t * TOP_K_IN_GROUP

    order = jnp.argsort(eid)
    se, stok, swt = eid[order], tok[order], wt[order]
    counts = jnp.bincount(eid, length=N_EXPERTS).astype(jnp.int32)
    padded = ((counts + MOE_BLOCK - 1) // MOE_BLOCK) * MOE_BLOCK
    pend = jnp.cumsum(padded)
    pstart = pend - padded
    start = jnp.cumsum(counts) - counts
    dest = pstart[se] + (jnp.arange(n_assign, dtype=jnp.int32) - start[se])
    n_blk = -(-n_assign // MOE_BLOCK) + N_EXPERTS
    rows = n_blk * MOE_BLOCK
    buf_tok = jnp.full((rows,), t, jnp.int32).at[dest].set(stok)
    buf_wt = jnp.zeros((rows,), f32).at[dest].set(swt)
    blk_expert = jnp.clip(jnp.searchsorted(pend, jnp.arange(n_blk) * MOE_BLOCK, side='right'),
                          0, N_EXPERTS - 1)
    xpad = jnp.concatenate([xt, jnp.zeros((1, d), xt.dtype)], axis=0)

    def expert_block(args):
        tok_b, e = args
        xb = xpad[tok_b]
        h = jax.nn.silu(xb @ w_gate[e]) * (xb @ w_up[e])
        return h @ w_down[e]

    out = lax.map(expert_block, (buf_tok.reshape(n_blk, MOE_BLOCK), blk_expert))
    out = out.reshape(rows, d) * buf_wt[:, None].astype(out.dtype)
    y = jnp.zeros((t + 1, d), out.dtype).at[buf_tok].add(out)[:t]
    return y.reshape(bn, s, d).astype(xn.dtype)

def first_inputs(seed: int = 0) -> dict:
    key = jax.random.key(seed)
    ks = jax.random.split(key, 20)
    nrm = jax.random.normal
    f32 = jnp.float32
    d = D_MODEL
    return {
        "x": nrm(ks[0], (BATCH, SEQ, d), f32),
        "norm1_gain": 1.0 + 0.05 * nrm(ks[1], (DEPTH, d), f32),
        "w_in": nrm(ks[2], (DEPTH, d, D_IN), f32) * d ** -0.5,
        "gmlp_v_gain": 1.0 + 0.05 * nrm(ks[3], (DEPTH, D_A), f32),
        "gmlp_w_s": nrm(ks[4], (DEPTH, A_HEADS, GMLP_BLOCK, GMLP_BLOCK), f32) * 0.5 * GMLP_BLOCK ** -0.5,
        "gmlp_b_s": 1.0 + 0.1 * nrm(ks[5], (DEPTH, A_HEADS, GMLP_BLOCK), f32),
        "hgrn_lower_bounds": 0.1 * nrm(ks[6], (DEPTH + 1, D_BK), f32),
        "hgrn_out_gain": 1.0 + 0.05 * nrm(ks[7], (DEPTH, D_BV), f32),
        "w_out": nrm(ks[8], (DEPTH, D_MIX, d), f32) * D_MIX ** -0.5,
        "norm2_gain": 1.0 + 0.05 * nrm(ks[9], (DEPTH, d), f32),
        "w_group_router": nrm(ks[10], (DEPTH, d, N_GROUPS), f32) * d ** -0.5,
        "b_group_router": 0.01 * nrm(ks[11], (DEPTH, N_GROUPS), f32),
        "w_expert_router": nrm(ks[12], (DEPTH, d, N_EXPERTS), f32) * d ** -0.5,
        "b_expert_router": 0.01 * nrm(ks[13], (DEPTH, N_EXPERTS), f32),
        "w_gate": nrm(ks[14], (DEPTH, N_EXPERTS, d, D_EXPERT), f32) * d ** -0.5,
        "w_up": nrm(ks[15], (DEPTH, N_EXPERTS, d, D_EXPERT), f32) * d ** -0.5,
        "w_down": nrm(ks[16], (DEPTH, N_EXPERTS, D_EXPERT, d), f32) * D_EXPERT ** -0.5,
        "final_gain": 1.0 + 0.05 * nrm(ks[17], (d,), f32),
    }

def first_block(x, norm1_gain, w_in, gmlp_v_gain, gmlp_w_s, gmlp_b_s, hgrn_lower_bounds,
              hgrn_out_gain, w_out, norm2_gain, w_group_router, b_group_router,
              w_expert_router, b_expert_router, w_gate, w_up, w_down, final_gain):
    lb_all = jnp.cumsum(jax.nn.softmax(hgrn_lower_bounds.astype(jnp.float32), axis=0), axis=0)
    split_at = [D_A, 2 * D_A, 2 * D_A + D_BK, 2 * D_A + 2 * D_BK, 2 * D_A + 2 * D_BK + D_BV]
    h = x
    for l in range(DEPTH):
        n1 = rms_norm(h, norm1_gain[l])
        proj = n1 @ w_in[l]
        u, v, q, f, i, g = jnp.split(proj, split_at, axis=-1)
        a_out = gmlp_mixer(jax.nn.gelu(u, approximate=False), jax.nn.gelu(v, approximate=False),
                           gmlp_v_gain[l], gmlp_w_s[l], gmlp_b_s[l])
        b_out = hgrn2_mixer(q, f, i, g, lb_all[l], hgrn_out_gain[l])
        h = h + jnp.concatenate([a_out, b_out], axis=-1) @ w_out[l]
        n2 = rms_norm(h, norm2_gain[l])
        h = h + hier_moe(n2, w_group_router[l], b_group_router[l], w_expert_router[l],
                         b_expert_router[l], w_gate[l], w_up[l], w_down[l])
    return rms_norm(h, final_gain)


DEPTH_2 = 2

N_MIXERS = 2
N_NSA_LAYERS = (DEPTH_2 + 1) // 2
N_DIFF_LAYERS = DEPTH_2 // 2
HEAD_DIM = 64
ROPE_DIM = HEAD_DIM // 4
ROPE_THETA = 500000.0
NSA_HEADS = D_MODEL // HEAD_DIM
NSA_GROUPS = 4
NSA_HPG = NSA_HEADS // NSA_GROUPS
CMP_BLOCK = 32
CMP_STRIDE = 16
CMP_HIDDEN = 2 * HEAD_DIM
SEL_BLOCK = 64
SEL_TOPK = 16
WINDOW = 512
NSA_Q_CHUNK = 64
NSA_Q_W = NSA_HEADS * HEAD_DIM
NSA_KV_W = NSA_GROUPS * HEAD_DIM
NSA_IN = NSA_Q_W + 6 * NSA_KV_W + 3 * NSA_HEADS
DIFF_HEADS = D_MODEL // (2 * HEAD_DIM)
DIFF_V_DIM = 2 * HEAD_DIM
DIFF_W = DIFF_HEADS * 2 * HEAD_DIM
DIFF_IN = 3 * DIFF_W
ATT_BLOCK = 128
D_FF = 4 * D_MODEL
NEG_INF = -1e30
SEL_FORCE = 1e6


def rms_norm_2(x, g):
    xf = x.astype(jnp.float32)
    y = xf * lax.rsqrt(jnp.mean(xf * xf, axis=-1, keepdims=True) + EPS)
    return (y * g.astype(jnp.float32)).astype(x.dtype)

def rope_tables(positions):
    inv = ROPE_THETA ** (-jnp.arange(0, ROPE_DIM, 2, dtype=jnp.float32) / ROPE_DIM)
    ang = positions.astype(jnp.float32)[..., None] * inv
    return jnp.cos(ang), jnp.sin(ang)

def apply_partial_rope(x, cos, sin):
    half = ROPE_DIM // 2
    shape = cos.shape[:2] + (1,) * (x.ndim - 3) + cos.shape[-1:]
    c = cos.reshape(shape)
    s = sin.reshape(shape)
    x1 = x[..., :half].astype(jnp.float32)
    x2 = x[..., half:ROPE_DIM].astype(jnp.float32)
    rot = jnp.concatenate([x1 * c - x2 * s, x2 * c + x1 * s], axis=-1).astype(x.dtype)
    return jnp.concatenate([rot, x[..., ROPE_DIM:]], axis=-1)

def masked_softmax(s, mask):
    return jax.nn.softmax(jnp.where(mask, s, NEG_INF), axis=-1) * mask

def compress_blocks(blk, pe, w1, w2):
    B, NC = blk.shape[:2]
    z = (blk + pe[:, None, :]).transpose(0, 1, 3, 2, 4).reshape(B, NC, NSA_GROUPS, CMP_BLOCK * HEAD_DIM)
    return jax.nn.silu(z @ w1) @ w2

def nsa_mixer(h, cos, sin, w_in, b_gate, q_gain, k_gain, pe_k, w_ck1, w_ck2, pe_v, w_cv1, w_cv2, w_out):
    B, S, _ = h.shape
    G, HPG, dh = NSA_GROUPS, NSA_HPG, HEAD_DIM
    scale = 1.0 / math.sqrt(dh)
    sizes = [NSA_Q_W] + [NSA_KV_W] * 6 + [3 * NSA_HEADS]
    q, kc, vc, ks, vs, kw, vw, gl = jnp.split(h @ w_in, list(np.cumsum(sizes)[:-1]), axis=-1)
    q = rms_norm_2(q.reshape(B, S, NSA_HEADS, dh), q_gain)
    q_rot = apply_partial_rope(q, cos, sin)
    q_cmp = q.reshape(B, S, G, HPG, dh).transpose(0, 2, 3, 1, 4)
    q_rot = q_rot.reshape(B, S, G, HPG, dh).transpose(0, 2, 3, 1, 4)
    gates = jax.nn.sigmoid(gl.astype(jnp.float32) + b_gate.astype(jnp.float32)).reshape(B, S, NSA_HEADS, 3)

    n_cmp = (S - CMP_BLOCK) // CMP_STRIDE + 1
    idx = jnp.arange(n_cmp)[:, None] * CMP_STRIDE + jnp.arange(CMP_BLOCK)[None, :]
    kc = kc.reshape(B, S, G, dh)
    vc = vc.reshape(B, S, G, dh)
    k_cmp = rms_norm_2(compress_blocks(kc[:, idx], pe_k, w_ck1, w_ck2), k_gain[0]).transpose(0, 2, 1, 3)
    v_cmp = compress_blocks(vc[:, idx], pe_v, w_cv1, w_cv2).transpose(0, 2, 1, 3)
    cmp_start = jnp.arange(n_cmp) * CMP_STRIDE
    cmp_end = cmp_start + CMP_BLOCK - 1
    n_sel = S // SEL_BLOCK
    top_n = min(SEL_TOPK, n_sel)
    sel_start = jnp.arange(n_sel) * SEL_BLOCK
    overlap = ((cmp_start[:, None] <= sel_start[None, :] + SEL_BLOCK - 1)
               & (cmp_end[:, None] >= sel_start[None, :])).astype(jnp.float32)

    ks = apply_partial_rope(rms_norm_2(ks.reshape(B, S, G, dh), k_gain[1]), cos, sin)
    ks_blk = ks.transpose(0, 2, 1, 3).reshape(B, G, n_sel, SEL_BLOCK, dh)
    vs_blk = vs.reshape(B, S, G, dh).transpose(0, 2, 1, 3).reshape(B, G, n_sel, SEL_BLOCK, dh)
    kw = apply_partial_rope(rms_norm_2(kw.reshape(B, S, G, dh), k_gain[2]), cos, sin)
    pad = ((0, 0), (0, 0), (WINDOW, 0), (0, 0))
    kw_pad = jnp.pad(kw.transpose(0, 2, 1, 3), pad)
    vw_pad = jnp.pad(vw.reshape(B, S, G, dh).transpose(0, 2, 1, 3), pad)
    b_idx = jnp.arange(B)[:, None, None, None]
    g_idx = jnp.arange(G)[None, :, None, None]
    blk_ids = jnp.arange(n_sel)
    QC = NSA_Q_CHUNK

    def chunk(ci):
        s0 = ci * QC
        t = s0 + jnp.arange(QC)
        qc_ = lax.dynamic_slice_in_dim(q_cmp, s0, QC, axis=3)
        qr_ = lax.dynamic_slice_in_dim(q_rot, s0, QC, axis=3)
        sc = jnp.einsum('bghqd,bgcd->bghqc', qc_, k_cmp).astype(jnp.float32) * scale
        pc = masked_softmax(sc, cmp_end[None, :] <= t[:, None])
        o_cmp = jnp.einsum('bghqc,bgcd->bghqd', pc.astype(v_cmp.dtype), v_cmp)
        imp = jnp.einsum('bghqc,cs->bgqs', pc, overlap)
        bt = (t // SEL_BLOCK)[:, None]
        valid = blk_ids[None, :] <= bt
        forced = (blk_ids[None, :] == 0) | (blk_ids[None, :] == bt) | (blk_ids[None, :] == bt - 1)
        imp = jnp.where(forced, SEL_FORCE, jnp.where(valid, imp, -1.0))
        _, sel = lax.top_k(imp, top_n)
        kg = ks_blk[b_idx, g_idx, sel]
        vg = vs_blk[b_idx, g_idx, sel]
        ss = jnp.einsum('bghqd,bgqnld->bghqnl', qr_, kg).astype(jnp.float32) * scale
        tok = sel[..., None] * SEL_BLOCK + jnp.arange(SEL_BLOCK)
        ms = (tok <= t[:, None, None])[:, :, None]
        shp = ss.shape
        ps = masked_softmax(ss.reshape(shp[:4] + (top_n * SEL_BLOCK,)),
                            ms.reshape(ms.shape[:4] + (top_n * SEL_BLOCK,))).reshape(shp)
        o_sel = jnp.einsum('bghqnl,bgqnld->bghqd', ps.astype(vg.dtype), vg)
        kw_ = lax.dynamic_slice_in_dim(kw_pad, s0, WINDOW + QC, axis=2)
        vw_ = lax.dynamic_slice_in_dim(vw_pad, s0, WINDOW + QC, axis=2)
        kpos = s0 - WINDOW + jnp.arange(WINDOW + QC)
        mw = (kpos[None, :] <= t[:, None]) & (kpos[None, :] > t[:, None] - WINDOW) & (kpos[None, :] >= 0)
        sw = jnp.einsum('bghqd,bgkd->bghqk', qr_, kw_).astype(jnp.float32) * scale
        o_win = jnp.einsum('bghqk,bgkd->bghqd', masked_softmax(sw, mw).astype(vw_.dtype), vw_)
        g = lax.dynamic_slice_in_dim(gates, s0, QC, axis=1)
        g = g.reshape(B, QC, G, HPG, 3).transpose(0, 2, 3, 1, 4).astype(o_win.dtype)
        o = g[..., 0:1] * o_cmp + g[..., 1:2] * o_sel + g[..., 2:3] * o_win
        return o.transpose(0, 3, 1, 2, 4).reshape(B, QC, NSA_Q_W)

    outs = lax.map(chunk, jnp.arange(S // QC))
    return outs.transpose(1, 0, 2, 3).reshape(B, S, NSA_Q_W) @ w_out

def diff_mixer(h, cos, sin, layer_depth, w_in, q_gain, k_gain, lq1, lk1, lq2, lk2, subln_g, w_out):
    B, S, _ = h.shape
    dh = HEAD_DIM
    scale = 1.0 / math.sqrt(dh)
    q, k, v = jnp.split(h @ w_in, [DIFF_W, 2 * DIFF_W], axis=-1)
    q = apply_partial_rope(rms_norm_2(q.reshape(B, S, DIFF_HEADS, 2, dh), q_gain), cos, sin)
    k = apply_partial_rope(rms_norm_2(k.reshape(B, S, DIFF_HEADS, 2, dh), k_gain), cos, sin)
    q = q.transpose(0, 2, 3, 1, 4)
    k = k.transpose(0, 2, 3, 1, 4)
    v = v.reshape(B, S, DIFF_HEADS, DIFF_V_DIM).transpose(0, 2, 1, 3)
    lam_init = 0.8 - 0.6 * math.exp(-0.3 * (layer_depth - 1))
    lam = (jnp.exp(jnp.sum(lq1.astype(jnp.float32) * lk1.astype(jnp.float32)))
           - jnp.exp(jnp.sum(lq2.astype(jnp.float32) * lk2.astype(jnp.float32))) + lam_init)
    kpos = jnp.arange(S)

    def block(bi):
        s0 = bi * ATT_BLOCK
        qb = lax.dynamic_slice_in_dim(q, s0, ATT_BLOCK, axis=3)
        s = jnp.einsum('bhcqd,bhckd->bhcqk', qb, k).astype(jnp.float32) * scale
        t = s0 + jnp.arange(ATT_BLOCK)
        p = masked_softmax(s, kpos[None, :] <= t[:, None])
        a = p[:, :, 0] - lam * p[:, :, 1]
        o = jnp.einsum('bhqk,bhkd->bhqd', a.astype(v.dtype), v)
        o = rms_norm_2(o, subln_g) * (1.0 - lam_init)
        return o.transpose(0, 2, 1, 3).reshape(B, ATT_BLOCK, DIFF_W)

    outs = lax.map(block, jnp.arange(S // ATT_BLOCK))
    return outs.transpose(1, 0, 2, 3).reshape(B, S, DIFF_W) @ w_out

def second_inputs(seed: int = 0) -> dict:
    key = jax.random.key(seed)
    ks = iter(jax.random.split(key, 32))
    D = D_MODEL

    def nrm(shape, scale):
        return jax.random.normal(next(ks), shape, jnp.float32) * scale

    def gain(shape):
        return 1.0 + nrm(shape, 0.02)

    x = nrm((BATCH, SEQ, D), 1.0)
    c = nrm((BATCH, D), 1.0)
    offsets = jax.random.randint(next(ks), (BATCH, 1), 0, 1024, dtype=jnp.int32)
    positions = (offsets + jnp.arange(SEQ, dtype=jnp.int32)[None, :]).astype(jnp.int32)
    NL, NDF = N_NSA_LAYERS, N_DIFF_LAYERS
    return {
        'x': x, 'c': c, 'positions': positions,
        'ln_mix_g': gain((DEPTH_2, D)), 'ln_mlp_g': gain((DEPTH_2, D)),
        'w_ada': nrm((DEPTH_2, D, 6 * D), D ** -0.5), 'b_ada': nrm((DEPTH_2, 6 * D), 0.01),
        'w_mlp_in': nrm((DEPTH_2, D, D_FF), D ** -0.5), 'w_mlp_out': nrm((DEPTH_2, D_FF, D), D_FF ** -0.5),
        'nsa_w_in': nrm((NL, D, NSA_IN), D ** -0.5), 'nsa_b_gate': nrm((NL, 3 * NSA_HEADS), 0.01),
        'nsa_q_gain': gain((NL, HEAD_DIM)), 'nsa_k_gain': gain((NL, 3, HEAD_DIM)),
        'nsa_pe_k': nrm((NL, CMP_BLOCK, HEAD_DIM), 0.1),
        'nsa_w_ck1': nrm((NL, CMP_BLOCK * HEAD_DIM, CMP_HIDDEN), (CMP_BLOCK * HEAD_DIM) ** -0.5),
        'nsa_w_ck2': nrm((NL, CMP_HIDDEN, HEAD_DIM), CMP_HIDDEN ** -0.5),
        'nsa_pe_v': nrm((NL, CMP_BLOCK, HEAD_DIM), 0.1),
        'nsa_w_cv1': nrm((NL, CMP_BLOCK * HEAD_DIM, CMP_HIDDEN), (CMP_BLOCK * HEAD_DIM) ** -0.5),
        'nsa_w_cv2': nrm((NL, CMP_HIDDEN, HEAD_DIM), CMP_HIDDEN ** -0.5),
        'nsa_w_out': nrm((NL, NSA_Q_W, D), NSA_Q_W ** -0.5),
        'diff_w_in': nrm((NDF, D, DIFF_IN), D ** -0.5),
        'diff_q_gain': gain((NDF, HEAD_DIM)), 'diff_k_gain': gain((NDF, HEAD_DIM)),
        'diff_lq1': nrm((NDF, HEAD_DIM), 0.1), 'diff_lk1': nrm((NDF, HEAD_DIM), 0.1),
        'diff_lq2': nrm((NDF, HEAD_DIM), 0.1), 'diff_lk2': nrm((NDF, HEAD_DIM), 0.1),
        'diff_subln_g': gain((NDF, DIFF_V_DIM)),
        'diff_w_out': nrm((NDF, DIFF_W, D), DIFF_W ** -0.5),
    }

def second_block(x, c, positions, ln_mix_g, ln_mlp_g, w_ada, b_ada, w_mlp_in, w_mlp_out,
              nsa_w_in, nsa_b_gate, nsa_q_gain, nsa_k_gain, nsa_pe_k, nsa_w_ck1, nsa_w_ck2,
              nsa_pe_v, nsa_w_cv1, nsa_w_cv2, nsa_w_out,
              diff_w_in, diff_q_gain, diff_k_gain, diff_lq1, diff_lk1, diff_lq2, diff_lk2,
              diff_subln_g, diff_w_out):
    cos, sin = rope_tables(positions)
    cond = jax.nn.silu(c)
    for i in range(DEPTH_2):
        mod = cond @ w_ada[i] + b_ada[i]
        sh1, sc1, g1, sh2, sc2, g2 = jnp.split(mod, 6, axis=-1)
        h = rms_norm_2(x, ln_mix_g[i]) * (1.0 + sc1[:, None, :]) + sh1[:, None, :]
        j = i // N_MIXERS
        if i % N_MIXERS == 0:
            y = nsa_mixer(h, cos, sin, nsa_w_in[j], nsa_b_gate[j], nsa_q_gain[j], nsa_k_gain[j],
                          nsa_pe_k[j], nsa_w_ck1[j], nsa_w_ck2[j], nsa_pe_v[j], nsa_w_cv1[j],
                          nsa_w_cv2[j], nsa_w_out[j])
        else:
            y = diff_mixer(h, cos, sin, i + 1, diff_w_in[j], diff_q_gain[j], diff_k_gain[j],
                           diff_lq1[j], diff_lk1[j], diff_lq2[j], diff_lk2[j], diff_subln_g[j],
                           diff_w_out[j])
        x = x + g1[:, None, :] * y
        h = rms_norm_2(x, ln_mlp_g[i]) * (1.0 + sc2[:, None, :]) + sh2[:, None, :]
        x = x + g2[:, None, :] * (jnp.square(jax.nn.relu(h @ w_mlp_in[i])) @ w_mlp_out[i])
    return x


def setup_inputs(seed=0):
    out = dict(first_inputs(seed))
    for name, value in second_inputs(seed + 1).items():
        if name != "x":
            out[name + "_2"] = value
    return out


def reference(
    x, norm1_gain, w_in, gmlp_v_gain, gmlp_w_s, gmlp_b_s, hgrn_lower_bounds, hgrn_out_gain,
    w_out, norm2_gain, w_group_router, b_group_router, w_expert_router, b_expert_router, w_gate,
    w_up, w_down, final_gain, c_2, positions_2, ln_mix_g_2, ln_mlp_g_2, w_ada_2, b_ada_2,
    w_mlp_in_2, w_mlp_out_2, nsa_w_in_2, nsa_b_gate_2, nsa_q_gain_2, nsa_k_gain_2, nsa_pe_k_2,
    nsa_w_ck1_2, nsa_w_ck2_2, nsa_pe_v_2, nsa_w_cv1_2, nsa_w_cv2_2, nsa_w_out_2, diff_w_in_2,
    diff_q_gain_2, diff_k_gain_2, diff_lq1_2, diff_lk1_2, diff_lq2_2, diff_lk2_2,
    diff_subln_g_2, diff_w_out_2,
):
    x = first_block(
        x, norm1_gain, w_in, gmlp_v_gain, gmlp_w_s, gmlp_b_s, hgrn_lower_bounds, hgrn_out_gain,
        w_out, norm2_gain, w_group_router, b_group_router, w_expert_router, b_expert_router,
        w_gate, w_up, w_down, final_gain,
    )
    return second_block(
        x, c_2, positions_2, ln_mix_g_2, ln_mlp_g_2, w_ada_2, b_ada_2, w_mlp_in_2, w_mlp_out_2,
        nsa_w_in_2, nsa_b_gate_2, nsa_q_gain_2, nsa_k_gain_2, nsa_pe_k_2, nsa_w_ck1_2,
        nsa_w_ck2_2, nsa_pe_v_2, nsa_w_cv1_2, nsa_w_cv2_2, nsa_w_out_2, diff_w_in_2,
        diff_q_gain_2, diff_k_gain_2, diff_lq1_2, diff_lk1_2, diff_lq2_2, diff_lk2_2,
        diff_subln_g_2, diff_w_out_2,
    )


_drawn_inputs = setup_inputs


def setup_inputs(seed=0):
    import zlib

    import numpy as np

    out = dict(_drawn_inputs(seed))
    spreads = {}
    factors = {'gmlp_v_gain': 2.845,
     'hgrn_lower_bounds': 5.428,
     'b_group_router': 8.0,
     'b_expert_router': 4.302,
     'ln_mix_g_2': 8.0,
     'ln_mlp_g_2': 2.899,
     'b_ada_2': 2.717,
     'nsa_b_gate_2': 8.0,
     'nsa_q_gain_2': 8.0,
     'nsa_k_gain_2': 8.0,
     'nsa_pe_k_2': 8.0,
     'nsa_pe_v_2': 3.435,
     'diff_q_gain_2': 8.0,
     'diff_k_gain_2': 8.0,
     'diff_lk1_2': 3.779,
     'diff_lq2_2': 8.0,
     'diff_lk2_2': 8.0,
     'diff_subln_g_2': 171.012}
    for name, (base, spread) in spreads.items():
        noise = np.random.default_rng([zlib.crc32(name.encode()), seed]).standard_normal(out[name].shape)
        drawn = base * np.exp(spread * noise) if base else spread * noise
        out[name] = __import__('jax').numpy.asarray(drawn.astype(out[name].dtype))
    for name, factor in factors.items():
        out[name] = (out[name] * factor).astype(out[name].dtype)
    return out
```

```python
import math
from contextlib import ExitStack

import concourse.bass as bass
import numpy as np
from concourse import mybir

F32 = mybir.dt.float32
BF16 = mybir.dt.bfloat16
I32 = mybir.dt.int32
U32 = mybir.dt.uint32
ALU = mybir.AluOpType
ACT = mybir.ActivationFunctionType
AX = mybir.AxisListType.X

P = 128
D = 1024
KC = D // P
S = 256
NT = S // P
NB = 512
SLAB = KC * NB
SLOTS = 6
EPS = 1e-6
NEG = -1e30

HA = 4
CH = 64
NE = 32
NG = 4
EPG = NE // NG
FE = 512
BT = 64
PAIRS = NE // 2
OVF = (2 * S) // BT
OVF_PAIRS = OVF // 2
BLOCKS = NE + OVF

DH = 64
QH = 16
GR = 4
RD = 8
THETA = 500000.0
NCMP = (S - 32) // 16 + 1
SCALE = DH ** -0.5
DFF = 4096
MC = DFF // NB
TWO_PI = 2.0 * math.pi
PI1 = 6.28125
PI2 = float(round((TWO_PI - PI1) * 2.0 ** 22)) / 2.0 ** 22
PI3 = TWO_PI - PI1 - PI2
ROUND = 1.5 * 2.0 ** 23
LAM0 = 0.8 - 0.6 * math.exp(-0.3)

ROWS = {}
_at = 0
for _name, _n in (("norm1", 8), ("norm2", 8), ("mix", 16), ("mlp", 16), ("hgain", 4), ("bs", 4),
                  ("subln", 1), ("pe_k", 16), ("pe_v", 16), ("c", 8)):
    ROWS[_name] = _at
    _at += _n
NROWS = _at
NADA = 2 * 6 * KC


SLABS = {}
_at = 0
for _name, _n in (("w_in", 6), ("ada", 24), ("w_out", 2), ("experts", 6 * PAIRS),
                  ("nsa_in", 5), ("nsa_cmp", 1), ("nsa_out", 2), ("mlp0", 16), ("diff_in", 6), ("diff_out", 2),
                  ("mlp1", 16)):
    SLABS[_name] = _at
    _at += _n


class Steps:

    def __init__(self, eng, sem, it=None, per=0):
        self.eng, self.sem, self.it, self.per, self.n = eng, sem, it, per, 0

    def value(self):
        return self.n if self.it is None else self.it * self.per + self.n

    def sig(self, ins):
        self.n += 1
        ins.then_inc(self.sem, 1)

    def then(self, ins):
        self.sig(ins)
        self.eng.wait_ge(self.sem, self.value())


class Ring:

    def __init__(self):
        self.n, self.last, self.loads = 0, [0] * SLOTS, [0] * SLOTS

    def take(self, slot):
        free = self.last[slot]
        self.n += 1
        self.last[slot] = self.n
        self.loads[slot] += 1
        return free, self.loads[slot]

    def skip(self, slots, rounds):
        for _ in range(rounds):
            for s in slots:
                self.take(s)


def build(nc, d, out):
    with ExitStack() as ctx:
        def sb(name, shape, dt=F32):
            return ctx.enter_context(nc.sbuf_tensor(name, shape, dt))

        def sem(name):
            return ctx.enter_context(nc.semaphore(name))

        ring = sb("ring", [P, SLOTS, SLAB])
        x = sb("x", [P, NT, D])
        xn = sb("xn", [P, NT, D])
        hT = sb("hT", [P, KC, S])
        proj = sb("proj", [P, NT, 6 * NB])
        mixT = sb("mixT", [P, KC, S])
        work = sb("work", [P, 11776])
        ident = sb("ident", [P, P])
        cum = sb("cum", [P, 3, P])
        same = sb("same", [P, 2])
        ones = sb("ones", [P, P])
        cols = sb("cols", [P, NROWS])
        acol = sb("acol", [P, NADA])
        mod = sb("mod", [P, NADA])
        sel4 = sb("sel4", [P, 1])
        gain_a = sb("gain_a", [P, 4, KC])
        epsc = sb("epsc", [P, 1])
        ss = sb("ss", [P, 64])
        rms = sb("rms", [P, 64])
        rstd = sb("rstd", [P, 64])
        zb = sb("zb", [P, NB], BF16)
        ps = [ctx.enter_context(nc.psum_tensor(f"bank{i}", [P, NB], F32)) for i in range(8)]

        def view(buf, at, *shape):
            n = math.prod(shape)
            flat = buf
            if len(buf.shape) == 3:
                flat = buf[:, :, :].rearrange("p a b -> p (a b)")
            else:
                flat = buf[:, :]
            v = flat[:, at:at + n]
            if len(shape) == 2:
                return v.rearrange("p (a b) -> p a b", b=shape[1])
            if len(shape) == 3:
                return v.rearrange("p (a b c) -> p a b c", b=shape[1], c=shape[2])
            return v

        rows = view(hT, 0, P)
        arow = view(hT, P, P)[0:NADA]
        hk = view(work, 0, NT, NB)
        lf = view(work, 1024, NT, NB)
        ex = view(work, 2048, 4, NT, NB)
        exT = view(work, 6144, 3, HA, S)
        scT = view(work, 9216, NT, NB)
        st = view(work, 10240, 3, NB)
        sq = view(work, 6144, NT, NB)
        lb_bc = view(mixT, 0, NB)
        lb1_bc = view(mixT, 512, NB)
        vg_bc = view(mixT, 1024, NB)
        wT = view(mixT, 1536, HA, P)
        ws = view(work, 8192, HA, P)
        crep = view(work, 7168, KC, 32)
        decay = sb("decay", [P, 16])
        ada_row = view(xn, 0, 2, NB)
        xgT = view(work, 0, KC, 2 * BT)
        pick = view(work, 1024, NT, 2 * BT)
        pickw = view(work, 1280, NT, 2 * BT)
        pickT = view(work, 1536, NT * P)
        sg = view(work, 1792, FE)
        eh = view(work, 2304, FE)
        ehT = view(work, 2816, FE // P, 2 * BT)
        eo = view(work, 3328, D)
        fg_bc = view(work, 4352, D)
        lg = view(work, 5376, NT, NG + NE)
        goh = view(work, 5456, NT, NG)
        gtmp = view(work, 5464, NT, NG)
        em = view(work, 5472, NT, NE)
        oh1 = view(work, 5536, NT, NE)
        oh2 = view(work, 5600, NT, NE)
        etmp = view(work, 5664, NT, NE)
        chosen = view(work, 5728, NT, NE)
        cwt = view(work, 5792, NT, NE)
        pos1 = view(work, 5856, NT, NE)
        tot = view(work, 5920, NE)
        more = view(work, 5952, NE)
        upto_e = view(work, 5984, NE)
        before_e = view(work, 6016, NE)
        own = view(work, 6048, OVF, NE)
        otmp = view(work, 6304, OVF, NE)
        obase = view(work, 6560, OVF)
        oexp = view(work, 6568, OVF)
        sm = view(work, 6576, 16, NT)
        sqn = view(work, 0, NT, 1536)
        E = [view(work, 1024 * i, 4, S) for i in range(2)]
        pT = [[view(work, 2048 + 1024 * i + 512 * k, 4, P) for k in range(2)] for i in range(2)]
        qcT = view(work, 4096, QH // 2, S)
        qrT = hT
        kT = view(work, 6144, 2, GR, S)
        kz = view(work, 8192, 2, GR, S)
        pcT = view(work, 8192, 2, 4, P)
        csc = view(work, 10240, 2, NT, 8 * 16)
        hc = view(work, 10752, 2, GR * NCMP)
        vcm = view(work, 10880, GR, DH)
        kcm = view(work, 11136, DH)
        kcT = view(work, 11200, GR * NCMP)
        pc = view(work, 11264, 2)
        rt = view(work, 11266, 2, NT * RD)
        kk = view(work, 11298, 2, NT * RD)
        nm = view(work, 11330, 2, 4)
        sums = view(work, 11338, 2, 4)
        gl = view(work, 11346, NT, 3 * QH)
        cmx = view(work, 11442, 64)
        csum = view(work, 11506, 64)
        cadd = view(work, 11570, NT, 16)
        wgl = view(mixT, 0, KC, 3 * QH)
        w2c = view(mixT, 384, 2, DH)
        bgl = view(mixT, 512, 3 * QH)
        qg = view(mixT, 560, DH)
        kg = view(mixT, 624, 3, DH)
        gbc = view(xn, 1024, D)
        rep = view(xn, 0, KC, P)
        dmask = cum[:, 2]
        cm01 = sb("cm01", [P, NT, 16])
        posi = sb("posi", [P, NT], I32)
        cossin = sb("cossin", [P, 2, NT * RD])
        inv = sb("inv", [P, RD])
        hid = [view(work, 1024 * i, 4, S) for i in range(2)]
        dqT = [qcT, view(work, 6144, 8, S)]
        dsq = view(work, 8192, NT, 1536)
        lamv = view(work, 11346, 4, DH)
        dl = view(work, 11602, 8)
        wr = sb("wr", [P, KC, NG + NE])
        router_b = sb("router_b", [P, NG + NE])
        iota = sb("iota", [P, BT])
        iotai = sb("iotai", [P, BT], I32)
        desc = sb("desc", [P, NE])
        before = sb("before", [P, P])
        posb = sb("posb", [P, BLOCKS + 2, NT])
        cwb = sb("cwb", [P, BLOCKS + 2, NT])
        oexp_i = sb("oexp_i", [P, OVF], I32)
        RMS_NORM = [1, 4, 5, 6, 9, 10, 13]

        x_in = sem("x_in")
        small_in = [sem(f"small_in{i}") for i in range(4)]
        landed = [sem(f"landed{i}") for i in range(SLOTS)]
        slabs_used = sem("slabs_used")
        const_ready = sem("const_ready")
        pool_step = sem("pool_step")
        dve_step = sem("dve_step")
        act_step = sem("act_step")
        dve_const = sem("dve_const")
        sum_ready = sem("sum_ready")
        rms_ready = sem("rms_ready")
        x_ready = sem("x_ready")
        xn_ready = sem("xn_ready")
        xnT_psum = sem("xnT_psum")
        hT_dve = sem("hT_dve")
        hT_act = sem("hT_act")
        small_psum = sem("small_psum")
        cols_ready = sem("cols_ready")
        crep_ready = sem("crep_ready")
        half_psum = sem("half_psum")
        proj_act = sem("proj_act")
        proj_dve = sem("proj_dve")
        ada_rows = sem("ada_rows")
        ada_cols = sem("ada_cols")
        mod_ready = sem("mod_ready")
        done = sem("done")

        f_ready = sem("f_ready")
        lf_ready = sem("lf_ready")
        cum_psum = sem("cum_psum")
        lb_diff = sem("lb_diff")
        fg_in = sem("fg_in")
        lb_exp = sem("lb_exp")
        exT_dve = sem("exT_dve")
        pe_step = sem("pe_step")
        ex_act = sem("ex_act")
        ex_ready = sem("ex_ready")
        exT_psum = sem("exT_psum")
        exT_ready = sem("exT_ready")
        sc_psum = sem("sc_psum")
        sc_ready = sem("sc_ready")
        u_psum = sem("u_psum")
        st_ready = sem("st_ready")
        o_psum = sem("o_psum")
        osq_ready = sem("osq_ready")
        vh_ready = sem("vh_ready")
        mixed_psum = sem("mixed_psum")
        mixed_taken = sem("mixed_taken")
        ab_ready = sem("ab_ready")
        abT_psum = sem("abT_psum")
        mixT_dve = sem("mixT_dve")
        mixT_act = sem("mixT_act")

        logit_psum = sem("logit_psum")
        router_dve = sem("router_dve")
        router_act = sem("router_act")
        chosen_ready = sem("chosen_ready")
        pos_psum = sem("pos_psum")
        blocks_ready = sem("blocks_ready")

        MSLOT = (4, 5, 0, 1)
        NSLOT = (2, 3, 4, 5, 0, 1)
        cv1_in = sem("cv1_in")
        nsa_in_sem = sem("nsa_small_in")
        rope_dve = sem("rope_dve")
        rope_act = sem("rope_act")
        rep_ready = sem("rep_ready")
        gate_psum = sem("gate_psum")
        gate_ready = sem("gate_ready")
        gl_psum = sem("gl_psum")
        gl_dve = sem("gl_dve")
        gl_ready = sem("gl_ready")
        sq_act = sem("sq_act")
        rows_ready = sem("rows_ready")
        heads_psum = sem("heads_psum")
        heads_act = sem("heads_act")
        heads_dve = sem("heads_dve")
        kz_psum = sem("kz_psum")
        kz_act = sem("kz_act")
        kz_dve = sem("kz_dve")
        cmp_psum = sem("cmp_psum")
        cmp_dve = sem("cmp_dve")
        cmp_act = sem("cmp_act")
        csc_psum = sem("csc_psum")
        cexp_dve = sem("cexp_dve")
        cexp_act = sem("cexp_act")
        cw_ready = sem("cw_ready")
        pcT_psum = sem("pcT_psum")
        pcT_ready = sem("pcT_ready")
        sc2_psum = sem("sc2_psum")
        nm_ready = sem("nm_ready")
        e_ready = sem("e_ready")
        p_ready = sem("p_ready")
        pT_psum = sem("pT_psum")
        pT_act = sem("pT_act")
        pT_dve = sem("pT_dve")
        ot_psum = sem("ot_psum")
        ot_ready = sem("ot_ready")
        hid_ready = sem("hid_ready")
        relu_ready = sem("relu_ready")
        diff_in_sem = sem("diff_small_in")
        res = view(work, 4096, 2, NT, NB)
        dgain = view(mixT, 0, 2, DH)
        lam_dve = sem("lam_dve")
        lam_act = sem("lam_act")
        orow_ready = sem("orow_ready")

        class Pairs:

            def __init__(self, tag, used, used0, landed, landed0, block0):
                self.used, self.used0, self.landed, self.landed0 = used, used0, landed, landed0
                self.block0 = block0
                self.pick_ready = sem(tag + "_pick_ready")
                self.pickw_ready = sem(tag + "_pickw_ready")
                self.gathered = sem(tag + "_gathered")
                self.xg_ready = sem(tag + "_xg_ready")
                self.sg_ready = sem(tag + "_sg_ready")
                self.h_ready = sem(tag + "_h_ready")
                self.hT_psum = sem(tag + "_hT_psum")
                self.hT_ready = sem(tag + "_hT_ready")
                self.pickT_psum = sem(tag + "_pickT_psum")
                self.pickT_ready = sem(tag + "_pickT_ready")
                self.down = sem(tag + "_down")
                self.o_act = sem(tag + "_o_act")
                self.o_dve = sem(tag + "_o_dve")
                self.scattered = sem(tag + "_scattered")

            def wait_used(self, eng, q, k):
                eng.wait_ge(self.used, q * 6 + (self.used0 + k))

            def wait_landed(self, eng, q, k):
                eng.wait_ge(self.landed[k], q * 16 + (self.landed0[k] + 16))

        walk = Ring()
        walk.skip(range(SLOTS), 5)
        walk.skip(range(2), 1)
        ESLOT = (2, 3, 4, 5, 0, 1)
        main = Pairs("main", slabs_used, SLABS["experts"], [landed[s] for s in ESLOT],
                     [16 * walk.loads[s] for s in ESLOT], 0)
        ovf = Pairs("ovf", sem("ovf_used"), 0, [sem(f"ovf_landed{k}") for k in range(6)], [0] * 6, NE)

        block = ctx.enter_context(nc.Block())

        def bank_done(eng, name, s, t, half):
            if t == 0:
                eng.wait_ge(half_psum, half + 1)
            else:
                eng.wait_ge(slabs_used, SLABS[name] + s + 1)

        def k_slab(w, n0):
            return w.rearrange("(c p) n -> p c n", p=P)[:, :, n0:n0 + NB]

        def slab(slot):
            return ring[:, slot].rearrange("p (c n) -> p c n", n=NB)

        @block.sync
        def _(sp):
            r = Ring()

            def load(slot, src, dst=None):
                free, _ = r.take(slot)
                if free > 0:
                    sp.wait_ge(slabs_used, free)
                sp.dma_start(slab(slot) if dst is None else dst, src).then_inc(landed[slot], 16)

            sp.dma_start(x[:, :, :], d["x"].rearrange("(t p) n -> p t n", p=P)).then_inc(x_in, 16)
            for s in range(6):
                load(s, k_slab(d["w_in"], s * NB))
            adav = d["w_ada_2"].rearrange("l (c p) (s n) -> l s p c n", p=P, n=NB)
            for s in range(6):
                load(s, adav[0, s])
            n0 = r.n
            with sp.Fori(1, 4) as it:
                for s in range(6):
                    sp.wait_ge(slabs_used, it * 6 + (n0 - 12 + s + 1))
                    src = adav[bass.ds(it // 2, 1), bass.ds((it % 2) * 6 + s, 1)]
                    sp.dma_start(slab(s), src.rearrange("l s p c n -> (l s p) c n")).then_inc(landed[s], 16)
            r.skip(range(6), 3)
            for s in range(2):
                load(s, k_slab(d["w_out"], s * NB))

            def mlp_load(l):
                win = d["w_mlp_in_2"][l].rearrange("(c p) (j n) -> j p c n", p=P, n=NB)
                wout = d["w_mlp_out_2"][l].rearrange("(j c p) n -> j p c n", p=P, c=NB // P)

                def one(n, j, second):
                    w = wout if second else win
                    dst = ring[:, MSLOT[n % 4]].rearrange("p (c n) -> p c n", n=D if second else NB)
                    return dst, w[bass.ds(j, 1)].rearrange("j p c n -> (j p) c n")

                def fixed(n):
                    k, second = ((n + 1) // 2, n % 2 == 0) if 0 < n < 15 else (0 if n == 0 else 8, n == 15)
                    dst, src = one(n, k - 1 if second else k, second)
                    load(MSLOT[n % 4], src, dst)

                for n in range(4):
                    fixed(n)
                n0 = r.n - 4
                with sp.Fori(1, 3) as i:
                    for m in range(4):
                        dst, src = one(m, i * 2 + (-1, 1, 0, 2)[m], m % 2 == 0)
                        sp.wait_ge(slabs_used, i * 4 + (n0 + m - 3))
                        sp.dma_start(dst, src).then_inc(landed[MSLOT[m]], 16)
                r.skip(MSLOT, 2)
                for n in range(12, 16):
                    fixed(n)

            def expert(w, e, k, halves):
                return (w[bass.ds(e, 1)].rearrange("e (c p) n -> (e p) c n", p=P),
                        ring[:, ESLOT[k]].rearrange("p (c n) -> p c n", n=halves * NB))

            PARTS = ((d["w_gate"], 1), (d["w_up"], 1), (d["w_down"], 2))
            for k in range(6):
                src, dst = expert(PARTS[k // 2][0], k % 2, k, PARTS[k // 2][1])
                load(ESLOT[k], src, dst)
            with sp.Fori(1, PAIRS) as q:
                for k in range(6):
                    src, dst = expert(PARTS[k // 2][0], q * 2 + k % 2, k, PARTS[k // 2][1])
                    main.wait_used(sp, q - 1, k + 1)
                    sp.dma_start(dst, src).then_inc(main.landed[k], 16)
            r.skip(ESLOT, PAIRS - 1)
            sp.wait_ge(blocks_ready, 1)
            for q in range(OVF_PAIRS):
                e = [sp.value_load(oexp_i[0:1, 2 * q + k:2 * q + k + 1], min_val=0, max_val=NE - 1) for k in range(2)]
                for k in range(6):
                    src, dst = expert(PARTS[k // 2][0], e[k % 2], k, PARTS[k // 2][1])
                    if q == 0:
                        main.wait_used(sp, PAIRS - 1, k + 1)
                    else:
                        ovf.wait_used(sp, q - 1, k + 1)
                    sp.dma_start(dst, src).then_inc(ovf.landed[k], 16)
            ovf.wait_used(sp, OVF_PAIRS - 1, 6)
            for s in range(5):
                load(NSLOT[s], k_slab(d["nsa_w_in_2"], s * NB))
            cmp_w = ring[:, NSLOT[5]].rearrange("p (w j m) -> p w j m", w=2, m=P)
            load(NSLOT[5], d["nsa_w_ck1_2"].rearrange("(j p) m -> p j m", p=P), cmp_w[:, 0])
            sp.dma_start(cmp_w[:, 1], d["nsa_w_cv1_2"].rearrange("(j p) m -> p j m", p=P)).then_inc(cv1_in, 16)
            for s in range(2):
                load(NSLOT[s], k_slab(d["nsa_w_out_2"], s * NB))
            mlp_load(0)
            for s in range(6):
                load(NSLOT[s], k_slab(d["diff_w_in_2"], s * NB))
            for s in range(2):
                load(NSLOT[s], k_slab(d["diff_w_out_2"], s * NB))
            mlp_load(1)
            sp.wait_ge(x_ready, 28)
            sp.dma_start(out.rearrange("(t p) n -> p t n", p=P), x[:, :, :]).then_inc(done, 16)
            sp.wait_ge(done, 16)

        @block.gpsimd
        def _(pool):
            step = Steps(pool, pool_step)
            step.sig(pool.memset(ident[:, :], 0.0))
            step.sig(pool.memset(cum[:, :, :], 1.0))
            step.sig(pool.memset(same[:, :], 0.0))
            step.sig(pool.memset(sel4[:, :], 0.0))
            step.sig(pool.memset(ones[:, :], 1.0))
            step.sig(pool.memset(epsc[:, :], EPS))
            step.sig(pool.memset(before[:, :], 1.0))
            step.sig(pool.memset(cm01[:, :, :], 1.0))
            for i in range(RD):
                step.sig(pool.memset(inv[:, i:i + 1], float(np.float32(THETA) ** np.float32(-i / RD))))
            step.sig(pool.memset(posb[:, :, :], -1.0))
            step.sig(pool.memset(cwb[:, :, :], 0.0))
            step.then(pool.memset(zb[:, :], 0.0))

            def keep(ap, base, pattern, cm, fill, op=ALU.is_ge):
                step.then(pool.affine_select(out=ap, in_=ap, compare_op=op, fill=fill, base=base,
                                             pattern=pattern, channel_multiplier=cm))

            keep(ident[:, :], 0, [[-1, P]], 1, 1.0, ALU.not_equal)
            for h in range(2):
                a = slice(CH * h, CH * h + CH)
                if h == 0:
                    keep(same[:, 0:1], -CH, [[0, 1]], 1, 1.0)
                else:
                    keep(same[:, 1:2], CH - 1, [[0, 1]], -1, 1.0)
                keep(cum[:, 0, a], CH * h, [[1, CH]], -1, 0.0)
                keep(cum[:, 0, a], -CH * h, [[0, CH]], 1, 0.0)
                keep(cum[:, 2, a], -CH * h - 1, [[-1, CH]], 1, 0.0)
                keep(cum[:, 2, a], CH * h + CH - 1, [[0, CH]], -1, 0.0)
                keep(cum[:, 1, a], CH * h + CH // 2 - 1, [[0, CH]], -1, 0.0)
                keep(cum[:, 1, a], -CH * h, [[0, CH]], 1, 0.0)
            for j in range(4):
                keep(sel4[:, :], -32 * j, [[0, 1]], 1, 1.0, ALU.not_equal)
            keep(before[:, :], -1, [[1, P]], -1, 0.0)
            for t in range(NT):
                keep(cm01[:, t], t * P - 31, [[-16, 16]], 1, 0.0)
            step.sig(pool.iota(iotai[:, :], pattern=[[1, BT]], base=0, channel_multiplier=0))
            step.then(pool.tensor_tensor(cum[:, 1], cum[:, 0], cum[:, 1], ALU.subtract))
            pool.sem_inc(const_ready, 1)

        @block.scalar
        def _(act):
            step = Steps(act, act_step)
            n_hT = 0
            bc = lambda ap, n: ap.rearrange("(a n) -> a n", a=1).broadcast_to([P, n])

            def small(name, src):
                act.dma_start(rows[ROWS[name]:ROWS[name] + src.shape[0], :], src).then_inc(small_in[0], 16)

            def rowsof(ap, n):
                return ap.rearrange("(r q) -> r q", q=P)

            small("norm1", rowsof(d["norm1_gain"], 8))
            small("norm2", rowsof(d["norm2_gain"], 8))
            small("mix", rowsof(d["ln_mix_g_2"].rearrange("l n -> (l n)"), 16))
            small("mlp", rowsof(d["ln_mlp_g_2"].rearrange("l n -> (l n)"), 16))
            small("hgain", rowsof(d["hgrn_out_gain"], 4))
            small("bs", d["gmlp_b_s"])
            small("subln", rowsof(d["diff_subln_g_2"], 1))
            small("pe_k", rowsof(d["nsa_pe_k_2"].rearrange("l n -> (l n)"), 16))
            small("pe_v", rowsof(d["nsa_pe_v_2"].rearrange("l n -> (l n)"), 16))
            small("c", rowsof(d["c_2"], 8))
            act.dma_start(arow[:, :], rowsof(d["b_ada_2"].rearrange("l n -> (l n)"), NADA)).then_inc(small_in[0], 16)
            act.dma_start(lb_bc, bc(d["hgrn_lower_bounds"][0], NB)).then_inc(small_in[1], 16)
            act.dma_start(lb1_bc, bc(d["hgrn_lower_bounds"][1], NB)).then_inc(small_in[1], 16)
            act.dma_start(vg_bc, bc(d["gmlp_v_gain"], NB)).then_inc(small_in[1], 16)
            act.dma_start(ws, d["gmlp_w_s"].rearrange("g i j -> i g j")).then_inc(small_in[2], 16)

            act.dma_start(wr[:, :, 0:NG], d["w_group_router"].rearrange("(c p) n -> p c n", p=P)).then_inc(small_in[3], 16)
            act.dma_start(wr[:, :, NG:], d["w_expert_router"].rearrange("(c p) n -> p c n", p=P)).then_inc(small_in[3], 16)
            act.dma_start(router_b[:, 0:NG], bc(d["b_group_router"], NG)).then_inc(small_in[3], 16)
            act.dma_start(router_b[:, NG:], bc(d["b_expert_router"], NE)).then_inc(small_in[3], 16)

            def norm(i):
                act.wait_ge(x_ready, 4 * i) if i else act.wait_ge(x_in, 16)
                for t in range(NT):
                    step.sig(act.activation(xn[:, t], x[:, t], ACT.Square, accum_out=ss[:, t:t + 1]))
                act.wait_ge(act_step, step.n)
                act.activation(rms[:, 0:NT], ss[:, 0:NT], ACT.Sqrt, bias=epsc[:, 0:1], scale=1.0 / D).then_inc(rms_ready, 1)

            def norm_out(i, gain, bias=None):
                act.wait_ge(xnT_psum, i + 1)
                for c in range(4, KC):
                    kw = {} if bias is None else {"bias": bias(c)}
                    act.activation(hT[:, c], ps[4 + c // 2][:, (c % 2) * S:(c % 2) * S + S], ACT.Identity,
                                   scale=gain(c), **kw).then_inc(hT_act, 1)

            act.wait_ge(const_ready, 1)
            norm(0)
            act.wait_ge(cols_ready, 1)
            step.then(act.activation(crep[:, :, 0], cols[:, ROWS["c"]:ROWS["c"] + KC], ACT.Silu))
            for c in range(KC):
                act.activation(crep[:, c, 1:32], ones[:, 0:31], ACT.Copy, scale=crep[:, c, 0:1]).then_inc(crep_ready, 1)
            norm_out(0, lambda c: cols[:, ROWS["norm1"] + c:ROWS["norm1"] + c + 1])
            act.wait_ge(lb_diff, 1)
            act.activation(lb_bc, lb_bc, ACT.Exp).then_inc(lb_exp, 1)

            for s, f in ((0, ACT.Gelu), (1, ACT.Gelu), (2, ACT.Silu), (3, ACT.Sigmoid), (5, ACT.Silu)):
                for t in range(NT):
                    bank_done(act, "w_in", s, t, s)
                    act.activation(proj[:, t, s * NB:(s + 1) * NB], ps[(s % 2) * 2 + t][:, :], f).then_inc(proj_act, 1)
            act.wait_ge(f_ready, 1)
            act.activation(lf, proj[:, :, 3 * NB:4 * NB], ACT.Ln).then_inc(lf_ready, 1)
            act.wait_ge(sum_ready, 1)
            act.activation(rms[:, 0:8], ss[:, 0:8], ACT.Sqrt, bias=epsc[:, 0:1], scale=1.0 / P).then_inc(rms_ready, 1)

            with act.Fori(0, 4) as it:
                for s in range(6):
                    act.wait_ge(slabs_used, it * 6 + (SLABS["ada"] + s + 1))
                    if s >= 2:
                        act.wait_ge(ada_cols, it * 6 + s)
                    else:
                        act.wait_ge(ada_cols, it * 6 + 1)
                    act.activation(ada_row[:, s % 2], ps[4 + s % 2][:, :], ACT.Copy).then_inc(ada_rows, 1)
            act.wait_ge(cum_psum, 1)
            for t in range(NT):
                for j, (m, sc) in enumerate(((1, 1.0), (1, -1.0), (0, 1.0), (2, 1.0))):
                    act.activation(ex[:, j, t], ps[3 * t + m][:, :], ACT.Exp, scale=sc).then_inc(ex_act, 1)
            act.activation(decay[:, :], ps[6][:, 0:16], ACT.Exp).then_inc(ex_act, 1)
            for j in range(3):
                act.wait_ge(exT_psum, 2 * j + 2)
                act.activation(exT[:, j, :, P:2 * P], ps[2 * j + 1][:, :].rearrange("p (h c) -> p h c", h=HA),
                               ACT.Copy).then_inc(exT_ready, 1)
            act.wait_ge(o_psum, 1)
            for t in range(NT):
                act.activation(sq[:, t], ps[5 + t][:, :], ACT.Square).then_inc(osq_ready, 1)
            act.wait_ge(sum_ready, 2)
            act.activation(rms[:, 0:8], ss[:, 0:8], ACT.Sqrt, bias=epsc[:, 0:1], scale=1.0 / P).then_inc(rms_ready, 1)
            for c in range(4, KC):
                act.wait_ge(abT_psum, c // 2 + 1)
                act.activation(mixT[:, c], ps[c // 2][:, (c % 2) * S:(c % 2) * S + S], ACT.Copy,
                               scale=cols[:, ROWS["hgain"] + c - 4:ROWS["hgain"] + c - 3]).then_inc(mixT_act, 1)
            norm(1)
            def mid(name, dst, src, **kw):
                act.dma_start(dst, src, **kw).then_inc(nsa_in_sem, 16)

            mid("gate weights", wgl, d["nsa_w_in_2"].rearrange("(c p) n -> p c n", p=P)[:, :, 5 * NB:])
            mid("ck2", w2c[:, 0], d["nsa_w_ck2_2"])
            mid("cv2", w2c[:, 1], d["nsa_w_cv2_2"])
            mid("gate bias", bgl, bc(d["nsa_b_gate_2"], 3 * QH))
            mid("q gain", qg, bc(d["nsa_q_gain_2"], DH))
            for k in range(3):
                mid("k gain", kg[:, k], bc(d["nsa_k_gain_2"][k], DH))
            mid("positions", posi[:, :], d["positions_2"].rearrange("(t p) -> p t", p=P), allow_slow_non_contiguous=True)
            act.dma_start(fg_bc, bc(d["final_gain"], D)).then_inc(fg_in, 16)
            norm_out(1, lambda c: cols[:, ROWS["norm2"] + c:ROWS["norm2"] + c + 1])
            act.wait_ge(router_dve, 1)
            act.activation(gtmp, gtmp, ACT.Exp).then_inc(router_act, 1)
            act.wait_ge(router_dve, 2)
            act.activation(sm[:, 2], sm[:, 2], ACT.Exp).then_inc(router_act, 1)

            def pair(m, q):
                m.wait_used(act, q, 4)
                act.activation(sg, ps[4][:, :], ACT.Silu).then_inc(m.sg_ready, 1)
                act.wait_ge(m.hT_psum, q + 1)
                act.activation(ehT, ps[6][:, :].rearrange("p (c s) -> p c s", c=FE // P), ACT.Copy).then_inc(m.hT_ready, 1)
                act.wait_ge(m.down, q + 1)
                act.activation(eo[:, 0:NB], ps[4][:, :], ACT.Copy).then_inc(m.o_act, 1)

            for m, n in ((main, PAIRS), (ovf, OVF_PAIRS)):
                act.sem_inc(m.hT_ready, 1)
                act.sem_inc(m.o_act, 1)
                with act.Fori(0, n) as q:
                    pair(m, q)
            norm(2)
            def norm2(i, j, l, which):
                norm(i)
                norm_out(j, lambda c: gain_a[:, 2 * l + which, c:c + 1],
                         lambda c: mod[:, (l * 6 + 3 * which) * KC + c:(l * 6 + 3 * which) * KC + c + 1])

            def gate_rows(k):
                act.wait_ge(gate_psum, k + 1)
                for n in range(2):
                    act.activation(gbc[:, n * NB:n * NB + NB], ps[4 + n][:, :], ACT.Copy).then_inc(gate_ready, 1)

            def projections(name, half, parts):
                for s in parts:
                    for t in range(NT):
                        src = ps[(s % 2) * 2 + t]
                        bank_done(act, name, s, t, half + s)
                        w, at = parts[s]
                        if w:
                            step.sig(act.activation(sqn[:, t, at:at + w], src[:, 0:w], ACT.Square))
                        act.activation(proj[:, t, s * NB:(s + 1) * NB], src[:, :], ACT.Copy).then_inc(proj_act, 1)

            def unit_exp(u, nk):
                act.wait_ge(nm_ready, u + 1)
                for i in range(4):
                    src = ps[2 * (u % 2) + i // 2][:, (i % 2) * S:(i % 2) * S + nk]
                    act.activation(E[u % 2][:, i, 0:nk], src, ACT.Exp, bias=nm[:, u % 2, i:i + 1], scale=SCALE,
                                   accum_out=sums[:, u % 2, i:i + 1]).then_inc(e_ready, 1)

            act.wait_ge(rope_dve, 1)
            act.activation(cossin[:, :, :], rt, ACT.Sin).then_inc(rope_act, 1)
            norm2(3, 2, 0, 0)
            gate_rows(0)
            projections("nsa_in", 8, {0: (512, 0), 1: (512, 512), 3: (256, 1024), 4: (256, 1280)})
            act.wait_ge(gl_dve, 1)
            act.activation(gl, gl, ACT.Sigmoid).then_inc(gl_ready, 1)
            act.wait_ge(sum_ready, 3)
            act.activation(rms[:, 0:48], ss[:, 0:48], ACT.Sqrt, bias=epsc[:, 0:1], scale=1.0 / DH).then_inc(rms_ready, 1)
            for gp in range(2):
                act.wait_ge(kz_psum, gp + 1)
                for o in range(2):
                    src = ps[gp][DH * o:DH * o + DH, 0:S]
                    act.activation(kz[0:DH, 0, 2 * gp + o], src, ACT.Copy).then_inc(kz_act, 1)
                    act.activation(kz[DH:P, 0, 2 * gp + o, 0:S - 1], src[:, 1:S], ACT.Copy).then_inc(kz_act, 1)
            for w in range(2):
                act.wait_ge(cmp_dve, w + 1)
                act.activation(hc[:, w], ps[4 + w][:, 0:GR * NCMP], ACT.Silu, bias=pc[:, w:w + 1]).then_inc(cmp_act, 1)
            act.wait_ge(cmp_psum, 3)
            act.activation(kcm[0:GR * NCMP], ps[6][0:GR * NCMP, 0:DH], ACT.Square, accum_out=ss[0:GR * NCMP, 48:49]).then_inc(cmp_act, 1)
            act.wait_ge(cmp_act, 3)
            act.activation(rms[0:GR * NCMP, 48:49], ss[0:GR * NCMP, 48:49], ACT.Sqrt, bias=epsc[0:GR * NCMP, 0:1], scale=1.0 / DH).then_inc(rms_ready, 1)
            act.wait_ge(heads_psum, 1)
            for k in range(2):
                act.activation(qcT[:, 4 * k:4 * k + 4, 0:P], ps[k][:, :].rearrange("p (h q) -> p h q", h=4), ACT.Copy).then_inc(heads_act, 1)
            act.wait_ge(heads_psum, 3)
            for t in range(NT):
                for o in range(2):
                    act.activation(kT[DH * o:DH * o + DH, 0, :, t * P:t * P + P],
                                   ps[t][0:DH, :].rearrange("p (g q) -> p g q", g=GR), ACT.Copy).then_inc(heads_act, 1)
            act.wait_ge(heads_psum, 5)
            for k in range(2):
                act.activation(qrT[:, 4 * k:4 * k + 4, 0:P], ps[4 + k][:, :].rearrange("p (h q) -> p h q", h=4), ACT.Copy).then_inc(heads_act, 1)
            act.wait_ge(cexp_dve, 1)
            act.activation(csc, csc, ACT.Exp).then_inc(cexp_act, 1)

            unit_exp(0, P)
            u = 0
            for t in range(NT):
                for g in range(GR):
                    n = t * GR + g
                    act.wait_ge(pcT_psum, n + 1)
                    act.activation(pcT[0:NCMP, n % 2], ps[7][0:NCMP, :].rearrange("p (h q) -> p h q", h=4), ACT.Copy).then_inc(pcT_ready, 1)
                    for br in range(2):
                        if u + 1 < 2 * NT * GR:
                            if u:
                                act.wait_ge(pT_psum, u)
                            unit_exp(u + 1, ((u + 1) // 8 + 1) * P)
                        act.wait_ge(pT_psum, u + 1)
                        act.activation(pT[u % 2][0], ps[4][:, :].rearrange("p (h q) -> p h q", h=4), ACT.Copy).then_inc(pT_act, 1)
                        u += 1
                    act.wait_ge(ot_psum, n + 1)
                    act.activation(mixT[:, 2 * g:2 * g + 2, t * P:t * P + P], ps[6][:, 0:S].rearrange("p (j q) -> p j q", j=2),
                                   ACT.Copy).then_inc(ot_ready, 1)
            def mlp(l):
                norm2(4 + 2 * l, 3 + 2 * l, l, 1)
                gate_rows(1 + 2 * l)

                def relu2(k, par, first=0):
                    for n in range(2):
                        act.wait_ge(slabs_used, k * 2 + (SLABS[f"mlp{l}"] + first))
                        o = hid[par][:, 2 * n:2 * n + 2]
                        act.activation(o, ps[4 + n][:, :].rearrange("p (m q) -> p m q", m=2), ACT.Relu).then_inc(relu_ready, 1)
                        act.wait_ge(relu_ready, k * 2 + (l * 2 * MC + n + 1))
                        act.activation(o, o, ACT.Square).then_inc(hid_ready, 1)

                relu2(0, 0, 1)
                with act.Fori(0, 3) as i:
                    relu2(i * 2 + 1, 1)
                    relu2(i * 2 + 2, 0)
                relu2(7, 1)

            act.wait_ge(x_ready, 16)
            for k, name in enumerate(("diff_lq1_2", "diff_lk1_2", "diff_lq2_2", "diff_lk2_2")):
                act.dma_start(lamv[:, k], bc(d[name], DH)).then_inc(diff_in_sem, 16)
            for k, name in enumerate(("diff_q_gain_2", "diff_k_gain_2")):
                act.dma_start(dgain[:, k], bc(d[name], DH)).then_inc(diff_in_sem, 16)
            mlp(0)
            norm2(5, 4, 1, 0)
            gate_rows(2)
            projections("diff_in", 15, {0: (512, 0), 1: (512, 512)})
            for s in (2, 3):
                for t in range(NT):
                    src = ps[(s % 2) * 2 + t]
                    bank_done(act, "diff_in", s, t, 15 + s)
                    step.sig(act.activation(dsq[:, t, (s - 2) * NB:(s - 1) * NB], src[:, :], ACT.Square))
                    act.activation(proj[:, t, s * NB:(s + 1) * NB], src[:, :], ACT.Copy).then_inc(proj_act, 1)
            act.wait_ge(lam_dve, 1)
            act.activation(lamv[:, 0, 0:2], lamv[:, 0, 0:2], ACT.Exp).then_inc(lam_act, 1)
            act.wait_ge(sum_ready, 4)
            act.activation(rms[:, 0:64], ss[:, 0:64], ACT.Sqrt, bias=epsc[:, 0:1], scale=1.0 / DH).then_inc(rms_ready, 1)
            for w in range(2):
                act.wait_ge(heads_psum, 7 + 2 * w)
                for k in range(2):
                    act.activation(dqT[w][:, 4 * k:4 * k + 4, 0:P], ps[4 * w + k][:, :].rearrange("p (h q) -> p h q", h=4), ACT.Copy).then_inc(heads_act, 1)
            unit_exp(16, P)
            for u in range(8):
                t = u // 4
                if u < 7:
                    act.wait_ge(pT_psum, 16 + u)
                    unit_exp(17 + u, ((u + 1) // 4 + 1) * P)
                act.wait_ge(ot_psum, 8 + u + 1)
                act.activation(proj[:, t, (u % 4) * S:(u % 4) * S + S], ps[6 + u % 2][:, 0:S], ACT.Copy).then_inc(ot_ready, 1)
            act.wait_ge(ot_ready, 16)
            for t in range(NT):
                act.activation(work[:, t * D:(t + 1) * D], proj[:, t, 0:D], ACT.Square).then_inc(sq_act, 1)
            act.wait_ge(sum_ready, 5)
            act.activation(rms[:, 0:16], ss[:, 0:16], ACT.Sqrt, bias=epsc[:, 0:1], scale=1.0 / P).then_inc(rms_ready, 1)
            act.wait_ge(abT_psum, 8)
            for c in range(4, KC):
                act.activation(mixT[:, c], ps[c // 2][:, (c % 2) * S:(c % 2) * S + S], ACT.Copy, scale=lamv[:, 1, 0:1]).then_inc(mixT_act, 1)
            mlp(1)

        @block.vector
        def _(v):
            step = Steps(v, dve_step)

            def norm(i):
                v.wait_ge(rms_ready, RMS_NORM[i])
                step.then(v.reciprocal(rstd[:, 0:NT], rms[:, 0:NT]))
                for t in range(NT):
                    v.tensor_scalar(xn[:, t], x[:, t], rstd[:, t:t + 1], None, ALU.mult).then_inc(xn_ready, 1)

            def norm_out(i, gain, bias=None):
                v.wait_ge(xnT_psum, i + 1)
                for c in range(0, 4):
                    src = ps[4 + c // 2][:, (c % 2) * S:(c % 2) * S + S]
                    if bias is None:
                        ins = v.tensor_scalar(hT[:, c], src, gain(c), None, ALU.mult)
                    else:
                        ins = v.tensor_scalar(hT[:, c], src, gain(c), bias(c), ALU.mult, ALU.add)
                    ins.then_inc(hT_dve, 1)

            def head_sums(sq3, n):
                for t in range(NT):
                    step.sig(v.tensor_reduce(ss[:, n * t:n * t + n], sq3[:, t].rearrange("p (h e) -> p h e", e=P), AX, ALU.add))

            v.wait_ge(small_psum, 1)
            step.sig(v.tensor_copy(cols[:, :], ps[0][:, 0:NROWS]))
            v.tensor_copy(acol[:, :], ps[0][:, P:P + NADA]).then_inc(cols_ready, 1)
            v.wait_ge(cols_ready, 1)
            v.wait_ge(dve_step, step.n)
            step.sig(v.memset(wT[CH:P, :, 0:CH], 0.0))
            step.sig(v.tensor_copy(wT[0:CH], ps[1][0:CH, :].rearrange("p (h i) -> p h i", h=HA)))
            step.then(v.tensor_copy(wT[CH:P, :, CH:P], ps[1][CH:P, :].rearrange("p (h i) -> p h i", h=HA)[:, :, CH:P]))
            norm(0)
            norm_out(0, lambda c: cols[:, ROWS["norm1"] + c:ROWS["norm1"] + c + 1])
            v.wait_ge(small_in[1], 48)
            step.then(v.tensor_tensor(lb_bc, lb1_bc, lb_bc, ALU.subtract))
            v.sem_inc(lb_diff, 1)
            v.wait_ge(lb_exp, 1)
            step.then(v.tensor_scalar(lb_bc, lb_bc, 1.0, None, ALU.add))
            step.then(v.reciprocal(lb_bc, lb_bc))
            step.then(v.tensor_scalar(lb1_bc, lb_bc, -1.0, 1.0, ALU.mult, ALU.add))
            v.wait_ge(proj_act, 4)
            for t in range(NT):
                step.sig(v.tensor_tensor(sq[:, t], proj[:, t, NB:2 * NB], proj[:, t, NB:2 * NB], ALU.mult))
            v.wait_ge(dve_step, step.n)
            head_sums(sq, 4)
            v.wait_ge(dve_step, step.n)
            v.sem_inc(sum_ready, 1)
            v.wait_ge(proj_act, 8)
            for t in range(NT):
                f = proj[:, t, 3 * NB:4 * NB]
                step.then(v.tensor_tensor(f, f, lb1_bc, ALU.mult))
                step.then(v.tensor_tensor(f, f, lb_bc, ALU.add))
                step.then(v.tensor_scalar(hk[:, t], f, -1.0, 1.0, ALU.mult, ALU.add))
            v.sem_inc(f_ready, 1)
            for t in range(NT):
                bank_done(v, "w_in", 4, t, 4)
                v.tensor_copy(proj[:, t, 4 * NB:5 * NB], ps[t][:, :]).then_inc(proj_dve, 1)
            v.wait_ge(rms_ready, 2)
            step.then(v.reciprocal(rstd[:, 0:8], rms[:, 0:8]))
            for t in range(NT):
                vv = proj[:, t, NB:2 * NB].rearrange("p (h e) -> p h e", e=P)
                v.tensor_tensor(vv, vv, rstd[:, 4 * t:4 * t + 4].unsqueeze(2).to_broadcast([P, HA, P]),
                                ALU.mult).then_inc(vh_ready, 1)
            for t in range(NT):
                v.wait_ge(mixed_psum, t + 1)
                v.tensor_tensor(sq[:, t], ps[6 + t][:, :], vg_bc, ALU.mult).then_inc(mixed_taken, 1)
                v.wait_ge(mixed_taken, t + 1)
                for g in range(HA):
                    a = slice(g * P, g * P + P)
                    step.sig(v.scalar_tensor_tensor(proj[:, t, a], sq[:, t, a], cols[:, ROWS["bs"] + g:ROWS["bs"] + g + 1],
                                                    proj[:, t, a], ALU.add, ALU.mult))
            v.wait_ge(dve_step, step.n)
            step.then(v.memset(scT, 0.0))
            v.sem_inc(mod_ready, 1)
            with v.Fori(0, 4) as it:
                v.wait_ge(ada_cols, it * 6 + 7)
                v.tensor_tensor(mod[:, bass.ds(it * 24, 24)], ps[6][:, 0:24], acol[:, bass.ds(it * 24, 24)], ALU.add).then_inc(mod_ready, 1)
            q, g = proj[:, :, 2 * NB:3 * NB], proj[:, :, 5 * NB:6 * NB]
            for t in range(NT):
                for j, m in enumerate((q[:, t], hk[:, t], q[:, t], hk[:, t])):
                    v.wait_ge(ex_act, 4 * t + j + 1)
                    v.tensor_tensor(ex[:, j, t], ex[:, j, t], m, ALU.mult).then_inc(ex_ready, 1)
            for j in range(3):
                v.wait_ge(exT_psum, 2 * j + 1)
                v.tensor_copy(exT[:, j, :, 0:P], ps[2 * j][:, :].rearrange("p (h c) -> p h c", h=HA)).then_inc(exT_dve, 1)
            for t in range(NT):
                v.wait_ge(sc_psum, t + 1)
                v.copy_predicated(scT[:, t].rearrange("p (h c) -> p h c", h=HA),
                                  cum[:, 0].bitcast(U32).unsqueeze(1).to_broadcast([P, HA, P]),
                                  ps[t][:, :].rearrange("p (h c) -> p h c", h=HA)).then_inc(sc_ready, 1)
            v.wait_ge(ex_act, 9)
            v.wait_ge(u_psum, 1)
            step.then(v.tensor_copy(st[:, 0], ps[2][:, :]))
            for n in (1, 2):
                for h in range(HA):
                    a = slice(h * P, h * P + P)
                    step.sig(v.scalar_tensor_tensor(st[:, n, a], st[:, n - 1, a], decay[:, 4 * n + h:4 * n + h + 1],
                                                    ps[2 + n][:, a], ALU.mult, ALU.add))
                v.wait_ge(dve_step, step.n)
            v.sem_inc(st_ready, 1)
            v.wait_ge(osq_ready, 2)
            head_sums(sq, 4)
            v.wait_ge(dve_step, step.n)
            v.sem_inc(sum_ready, 1)
            v.wait_ge(rms_ready, 3)
            step.then(v.reciprocal(rstd[:, 0:8], rms[:, 0:8]))
            for t in range(NT):
                gg = g[:, t].rearrange("p (h e) -> p h e", e=P)
                step.then(v.tensor_tensor(gg, gg, rstd[:, 4 * t:4 * t + 4].unsqueeze(2).to_broadcast([P, HA, P]), ALU.mult))
                v.tensor_tensor(g[:, t], g[:, t], ps[5 + t][:, :], ALU.mult).then_inc(ab_ready, 1)
            for c in range(0, 4):
                v.wait_ge(abT_psum, c // 2 + 1)
                v.tensor_copy(mixT[:, c], ps[c // 2][:, (c % 2) * S:(c % 2) * S + S]).then_inc(mixT_dve, 1)
            for s in range(2):
                for t in range(NT):
                    bank_done(v, "w_out", s, t, 6 + s)
                    a = slice(s * NB, s * NB + NB)
                    v.tensor_tensor(x[:, t, a], x[:, t, a], ps[4 + 2 * s + t][:, :], ALU.add).then_inc(x_ready, 1)
            norm(1)
            norm_out(1, lambda c: cols[:, ROWS["norm2"] + c:ROWS["norm2"] + c + 1])

            def bcast(ap, n):
                return ap.unsqueeze(2).to_broadcast([P, ap.shape[1], n])

            step.sig(v.tensor_copy(iota[:, :], iotai[:, :]))
            step.then(v.tensor_scalar(desc[:, :], iotai[:, 0:NE], -1.0, float(NE), ALU.mult, ALU.add))
            v.wait_ge(small_in[3], 64)
            v.wait_ge(logit_psum, 1)
            step.then(v.tensor_tensor(lg, ps[0][:, 0:NT * (NG + NE)].rearrange("p (t n) -> p t n", t=NT),
                                      router_b[:, :].unsqueeze(1).to_broadcast([P, NT, NG + NE]), ALU.add))
            g_log, e_log = lg[:, :, 0:NG], lg[:, :, NG:]
            gmax, gprob, e2, w1, w2, key, v1, v2 = (sm[:, i] for i in (0, 1, 2, 3, 4, 5, 6, 7))

            def first(oh, vals, top, n):
                step.then(v.tensor_tensor(oh, vals, bcast(top, n), ALU.is_equal))
                step.then(v.tensor_tensor(oh, oh, desc[:, 0:n].unsqueeze(1).to_broadcast([P, NT, n]), ALU.mult))
                step.then(v.tensor_reduce(key, oh, AX, ALU.max))
                step.then(v.tensor_tensor(oh, oh, bcast(key, n), ALU.is_equal))

            step.then(v.tensor_reduce(gmax, g_log, AX, ALU.max))
            step.then(v.tensor_tensor(gtmp, g_log, bcast(gmax, NG), ALU.subtract))
            v.sem_inc(router_dve, 1)
            first(goh, g_log, gmax, NG)
            v.wait_ge(router_act, 1)
            step.then(v.tensor_reduce(gprob, gtmp, AX, ALU.add))
            step.then(v.reciprocal(gprob, gprob))
            step.then(v.tensor_scalar(gtmp, goh, -1.0, -NEG, ALU.add, ALU.mult))
            em4 = em.rearrange("p t (g e) -> p (t g) e", e=EPG)
            gohf = goh.rearrange("p t g -> p (t g)")
            gtf = gtmp.rearrange("p t g -> p (t g)")
            for t in range(NT):
                step.sig(v.tensor_tensor(em[:, t].rearrange("p (g e) -> p g e", e=EPG), e_log[:, t].rearrange("p (g e) -> p g e", e=EPG),
                                         bcast(goh[:, t], EPG), ALU.mult))
            v.wait_ge(dve_step, step.n)
            step.then(v.tensor_tensor(em4, em4, bcast(gtf, EPG), ALU.add))
            step.then(v.tensor_reduce(v1, em, AX, ALU.max))
            first(oh1, em, v1, NE)
            step.then(v.scalar_tensor_tensor(em, oh1, NEG, em, ALU.mult, ALU.add))
            step.then(v.tensor_reduce(v2, em, AX, ALU.max))
            step.then(v.tensor_tensor(e2, v2, v1, ALU.subtract))
            v.sem_inc(router_dve, 1)
            first(oh2, em, v2, NE)
            step.then(v.tensor_tensor(chosen, oh1, oh2, ALU.add))
            v.sem_inc(chosen_ready, 1)
            v.wait_ge(router_act, 2)
            step.then(v.tensor_scalar(w1, e2, 1.0, None, ALU.add))
            step.then(v.reciprocal(w1, w1))
            step.then(v.tensor_tensor(w1, w1, gprob, ALU.mult))
            step.then(v.tensor_tensor(w2, w1, e2, ALU.mult))
            step.then(v.tensor_tensor(oh1, oh1, bcast(w1, NE), ALU.mult))
            step.then(v.tensor_tensor(oh2, oh2, bcast(w2, NE), ALU.mult))
            step.then(v.tensor_tensor(cwt, oh1, oh2, ALU.add))
            v.wait_ge(pos_psum, 1)
            step.then(v.tensor_scalar(pos1, ps[1][:, 0:NT * NE].rearrange("p (t e) -> p t e", e=NE), 1.0, None, ALU.add))
            step.then(v.tensor_tensor(pos1, pos1, chosen, ALU.mult))
            step.sig(v.tensor_copy(tot, ps[1][:, NT * NE:(NT + 1) * NE]))
            for t in range(NT):
                step.sig(v.tensor_scalar(posb[:, 0:NE, t], pos1[:, t], -1.0, None, ALU.add))
                step.sig(v.tensor_copy(cwb[:, 0:NE, t], cwt[:, t]))
            v.wait_ge(dve_step, step.n)
            step.then(v.tensor_scalar(more, tot, float(BT), None, ALU.is_gt))
            for k in range(2, S // BT):
                step.then(v.scalar_tensor_tensor(more, tot, float(k * BT), more, ALU.is_gt, ALU.add))
            step.then(v.tensor_tensor_scan(upto_e, ones[:, 0:NE], more, 0.0, ALU.mult, ALU.add))
            step.then(v.tensor_tensor(before_e, upto_e, more, ALU.subtract))

            def over_e(ap):
                return ap.unsqueeze(1).to_broadcast([P, OVF, NE])

            j_of = bcast(iota[:, 0:OVF], NE)
            step.then(v.tensor_tensor(own, over_e(before_e), j_of, ALU.is_le))
            step.then(v.tensor_tensor(otmp, over_e(upto_e), j_of, ALU.is_gt))
            step.then(v.tensor_tensor(own, own, otmp, ALU.mult))
            step.then(v.tensor_tensor(otmp, j_of, over_e(before_e), ALU.subtract))
            step.then(v.scalar_tensor_tensor(otmp, otmp, 1.0, own, ALU.add, ALU.mult))
            step.then(v.tensor_reduce(obase, otmp, AX, ALU.add))
            step.then(v.tensor_scalar(obase, obase, float(BT), 1.0, ALU.mult, ALU.add))
            step.then(v.tensor_tensor(otmp, own, over_e(iota[:, 0:NE]), ALU.mult))
            step.then(v.tensor_reduce(oexp, otmp, AX, ALU.add))
            step.then(v.tensor_copy(oexp_i[:, :], oexp))
            for t in range(NT):
                step.then(v.tensor_tensor(otmp, own, over_e(pos1[:, t]), ALU.mult))
                step.then(v.tensor_reduce(posb[:, NE:BLOCKS, t], otmp, AX, ALU.add))
                step.then(v.tensor_tensor(posb[:, NE:BLOCKS, t], posb[:, NE:BLOCKS, t], obase, ALU.subtract))
                step.then(v.tensor_tensor(otmp, own, over_e(cwt[:, t]), ALU.mult))
                step.then(v.tensor_reduce(cwb[:, NE:BLOCKS, t], otmp, AX, ALU.add))
            v.sem_inc(blocks_ready, 1)

            def build_pick(m, q, weighted):
                for e in range(2):
                    for t in range(NT):
                        b = q * 2 + (m.block0 + e)
                        at = posb[:, bass.ds(b, 1), t]
                        dst = (pickw if weighted else pick)[:, t, e * BT:e * BT + BT]
                        if weighted:
                            ins = v.tensor_scalar(dst, iota[:, :], at, cwb[:, bass.ds(b, 1), t], ALU.is_equal, ALU.mult)
                        else:
                            ins = v.tensor_scalar(dst, iota[:, :], at, None, ALU.is_equal)
                ins.then_inc(m.pickw_ready if weighted else m.pick_ready, 1)

            def take_gathered(m, n):
                for k in range(2):
                    v.wait_ge(m.gathered, n + (k + 1))
                    c = 4 * k
                    v.tensor_tensor(xgT[:, c:c + 4], ps[6 + k][:, :].rearrange("p (c s) -> p c s", c=4),
                                    bcast(cols[:, ROWS["norm2"] + c:ROWS["norm2"] + c + 4], 2 * BT),
                                    ALU.mult).then_inc(m.xg_ready, 1)

            def pairs(m, n):
                v.sem_inc(m.pickT_ready, 1)
                v.sem_inc(m.o_dve, 1)
                build_pick(m, 0, False)
                take_gathered(m, 0)
                with v.Fori(0, n) as q:
                    v.wait_ge(m.gathered, q * 2 + 2)
                    build_pick(m, q + 1, False)
                    v.wait_ge(m.pickT_psum, q + 1)
                    build_pick(m, q, True)
                    v.wait_ge(m.sg_ready, q + 1)
                    v.tensor_tensor(eh, sg, ps[5][:, :], ALU.mult).then_inc(m.h_ready, 1)
                    take_gathered(m, q * 2 + 2)
                    v.wait_ge(m.pickT_psum, q + 2)
                    v.tensor_copy(pickT, ps[7][:, 0:NT * P]).then_inc(m.pickT_ready, 1)
                    m.wait_used(v, q, 6)
                    v.tensor_copy(eo[:, NB:D], ps[5][:, :]).then_inc(m.o_dve, 1)

            pairs(main, PAIRS)
            pairs(ovf, OVF_PAIRS)
            v.wait_ge(ovf.scattered, OVF_PAIRS)
            for s in range(2):
                for t in range(NT):
                    a = slice(s * NB, s * NB + NB)
                    v.tensor_tensor(x[:, t, a], x[:, t, a], ps[2 * t + s][:, :], ALU.add).then_inc(x_ready, 1)
            v.wait_ge(x_ready, 8)
            norm(2)
            v.wait_ge(xn_ready, 6)
            v.wait_ge(fg_in, 16)
            for t in range(NT):
                v.tensor_tensor(x[:, t], xn[:, t], fg_bc, ALU.mult).then_inc(x_ready, 2)
            v.wait_ge(mod_ready, 5)
            for l in range(2):
                for w, (name, part) in enumerate((("mix", 1), ("mlp", 4))):
                    sc = mod[:, (l * 6 + part) * KC:(l * 6 + part + 1) * KC]
                    g = cols[:, ROWS[name] + l * KC:ROWS[name] + (l + 1) * KC]
                    step.sig(v.scalar_tensor_tensor(gain_a[:, 2 * l + w], sc, 1.0, g, ALU.add, ALU.mult))
            step.sig(v.tensor_scalar(dmask, before[:, :], NEG, None, ALU.mult))
            step.sig(v.tensor_scalar(cadd, cm01[:, :, :], -1.0, -NEG, ALU.add, ALU.mult))
            v.wait_ge(nsa_in_sem, 9 * 16)
            step.then(v.tensor_copy(kk[:, 0, 0:NT], posi[:, :]))
            step.then(v.tensor_tensor(rt[:, 1].rearrange("p (t i) -> p t i", t=NT), bcast(kk[:, 0, 0:NT], RD),
                                      inv[:, :].unsqueeze(1).to_broadcast([P, NT, RD]), ALU.mult))
            step.then(v.tensor_scalar(kk[:, 0], rt[:, 1], 1.0 / TWO_PI, 0.25, ALU.mult, ALU.add))
            step.then(v.tensor_scalar(kk[:, 1], rt[:, 1], 1.0 / TWO_PI, None, ALU.mult))
            step.then(v.tensor_scalar(kk, kk, ROUND, None, ALU.add))
            step.then(v.tensor_scalar(kk, kk, ROUND, None, ALU.subtract))
            step.then(v.tensor_copy(rt[:, 0], rt[:, 1]))
            for part in (PI1, PI2, PI3):
                step.then(v.scalar_tensor_tensor(rt, kk, -part, rt, ALU.mult, ALU.add))
            step.then(v.tensor_scalar(rt[:, 0], rt[:, 0], math.pi / 2, None, ALU.add))
            step.then(v.tensor_scalar(rt, rt, 3.1415925, -3.1415925, ALU.min, ALU.max))
            v.sem_inc(rope_dve, 1)
            cos = cossin[:, 0].rearrange("p (t i) -> p t i", t=NT)
            sin = cossin[:, 1].rearrange("p (t i) -> p t i", t=NT)

            def norm2(i, j, l, which):
                norm(i)
                norm_out(j, lambda c: gain_a[:, 2 * l + which, c:c + 1],
                         lambda c: mod[:, (l * 6 + 3 * which) * KC + c:(l * 6 + 3 * which) * KC + c + 1])

            def gate_cols(k, l, part):
                for c in range(KC):
                    ins = v.tensor_scalar(rep[:, c], ones[:, :], mod[:, (l * 6 + part) * KC + c:(l * 6 + part) * KC + c + 1],
                                          None, ALU.mult)
                ins.then_inc(rep_ready, 1)

            def rope(first, heads):
                h = proj[:, :, first:first + heads * DH].rearrange("p t (h e) -> p t h e", e=DH)
                a, b = h[:, :, :, 0:RD], h[:, :, :, RD:2 * RD]
                w = lambda i: rope_s[:, i, 0:NT * heads * RD].rearrange("p (t h i) -> p t h i", t=NT, i=RD)
                over = lambda ap: ap.unsqueeze(2).to_broadcast([P, NT, heads, RD])
                step.sig(v.tensor_tensor(w(0), a, over(cos), ALU.mult))
                step.sig(v.tensor_tensor(w(1), b, over(sin), ALU.mult))
                step.sig(v.tensor_tensor(w(2), b, over(cos), ALU.mult))
                step.then(v.tensor_tensor(w(3), a, over(sin), ALU.mult))
                step.sig(v.tensor_tensor(a, w(0), w(1), ALU.subtract))
                step.then(v.tensor_tensor(b, w(2), w(3), ALU.add))

            def scaled(first, heads, r0, per, gain):
                for t in range(NT):
                    h = proj[:, t, first:first + heads * DH].rearrange("p (h e) -> p h e", e=DH)
                    step.then(v.tensor_tensor(h, h, bcast(rstd[:, r0 + per * t:r0 + per * t + heads], DH), ALU.mult))
                    step.then(v.tensor_tensor(h, h, gain.unsqueeze(1).to_broadcast([P, heads, DH]), ALU.mult))

            def unit_max(u, nk):
                v.wait_ge(sc2_psum, u + 1)
                v.wait_ge(e_ready, 4 * (u - 1)) if u > 1 else None
                for k in range(2):
                    b = ps[2 * (u % 2) + k][:, :].rearrange("p (h k) -> p h k", h=2)
                    dg = b[:, :, nk - P:nk]
                    step.sig(v.tensor_tensor(dg, dg, dmask.unsqueeze(1).to_broadcast([P, 2, P]), ALU.add))
                v.wait_ge(dve_step, step.n)
                for k in range(2):
                    b = ps[2 * (u % 2) + k][:, :].rearrange("p (h k) -> p h k", h=2)
                    step.sig(v.tensor_reduce(nm[:, u % 2, 2 * k:2 * k + 2], b[:, :, 0:nk], AX, ALU.max))
                v.wait_ge(dve_step, step.n)
                v.tensor_scalar(nm[:, u % 2], nm[:, u % 2], -SCALE, None, ALU.mult).then_inc(nm_ready, 1)

            def residual(name, half, gate, banks):
                v.wait_ge(gate_ready, 2 * gate + 2)
                for s in range(2):
                    for t in range(NT):
                        if name:
                            bank_done(v, name, s, t, half + s)
                        a = slice(s * NB, s * NB + NB)
                        step.then(v.tensor_tensor(res[:, s, t], ps[banks(s, t)][:, :], gbc[:, a], ALU.mult))
                        v.tensor_tensor(x[:, t, a], x[:, t, a], res[:, s, t], ALU.add).then_inc(x_ready, 1)

            norm2(3, 2, 0, 0)
            gate_cols(0, 0, 2)
            for t in range(NT):
                bank_done(v, "nsa_in", 2, t, 10)
                v.tensor_copy(proj[:, t, 2 * NB:3 * NB], ps[t][:, :]).then_inc(proj_dve, 1)
            v.wait_ge(gl_psum, 1)
            v.tensor_tensor(gl, ps[7][:, 0:NT * 3 * QH].rearrange("p (t n) -> p t n", t=NT),
                            bgl.unsqueeze(1).to_broadcast([P, NT, 3 * QH]), ALU.add).then_inc(gl_dve, 1)
            for gp in range(2):
                v.wait_ge(kz_psum, 3 + gp)
                for o in range(2):
                    src = ps[2 + gp][DH * o:DH * o + DH, 0:S]
                    v.tensor_copy(kz[0:DH, 1, 2 * gp + o], src).then_inc(kz_dve, 1)
                    v.tensor_copy(kz[DH:P, 1, 2 * gp + o, 0:S - 1], src[:, 1:S]).then_inc(kz_dve, 1)
            v.wait_ge(proj_act, 10 + 8)
            for t in range(NT):
                step.sig(v.tensor_reduce(ss[:, 24 * t:24 * t + 24], sqn[:, t].rearrange("p (h e) -> p h e", e=DH), AX, ALU.add))
            v.wait_ge(dve_step, step.n)
            v.sem_inc(sum_ready, 1)
            for w in range(2):
                v.wait_ge(cmp_psum, w + 1)
                v.tensor_copy(pc[:, w:w + 1], ps[4 + w][:, 64:65]).then_inc(cmp_dve, 1)
            v.wait_ge(rms_ready, 7)
            step.then(v.reciprocal(rstd[:, 0:48], rms[:, 0:48]))
            scaled(0, QH, 0, 24, qg)
            v.sem_inc(rows_ready, 1)
            v.wait_ge(rms_ready, 8)
            G15 = GR * NCMP
            step.then(v.reciprocal(rstd[0:G15, 48:49], rms[0:G15, 48:49]))
            v.scalar_tensor_tensor(kcm[0:G15], ps[6][0:G15, 0:DH], rstd[0:G15, 48:49], kg[0:G15, 0], ALU.mult, ALU.mult).then_inc(cmp_dve, 1)
            v.wait_ge(cmp_psum, 4)
            v.tensor_copy(vcm[0:NCMP], ps[7][0:NCMP, 0:GR * DH].rearrange("p (g e) -> p g e", e=DH)).then_inc(cmp_dve, 1)
            scaled(1536, GR, 16, 24, kg[:, 1])
            v.wait_ge(rope_act, 1)
            rope_s = view(work, 8192, 4, 256)
            v.wait_ge(cmp_psum, 2)
            rope(1536, GR)
            v.sem_inc(rows_ready, 1)
            v.wait_ge(cmp_psum, 5)
            for o in range(2):
                v.tensor_copy(kcT[DH * o:DH * o + DH], ps[6][0:DH, 64:64 + G15]).then_inc(cmp_dve, 1)
            v.wait_ge(heads_psum, 2)
            for k in range(2):
                v.tensor_copy(qcT[:, 4 * k:4 * k + 4, P:S], ps[2 + k][:, :].rearrange("p (h q) -> p h q", h=4)).then_inc(heads_dve, 1)
            scaled(2048, GR, 20, 24, kg[:, 2])
            rope(2048, GR)
            v.sem_inc(rows_ready, 1)
            rope(0, QH)
            v.sem_inc(rows_ready, 1)
            v.wait_ge(heads_psum, 4)
            for t in range(NT):
                for o in range(2):
                    v.tensor_copy(kT[DH * o:DH * o + DH, 1, :, t * P:t * P + P],
                                  ps[2 + t][0:DH, :].rearrange("p (g q) -> p g q", g=GR)).then_inc(heads_dve, 1)
            v.wait_ge(heads_psum, 6)
            for k in range(2):
                v.tensor_copy(qrT[:, 4 * k:4 * k + 4, P:S], ps[6 + k][:, :].rearrange("p (h q) -> p h q", h=4)).then_inc(heads_dve, 1)
            v.wait_ge(csc_psum, 1)
            c16 = lambda ap: ap.rearrange("p (h c) -> p h c", c=16)[:, :, 0:NCMP]
            step.then(v.memset(csc, 0.0))
            for o in range(2):
                for t in range(NT):
                    step.sig(v.scalar_tensor_tensor(c16(csc[:, o, t]), c16(ps[o][:, t * P:t * P + P]), SCALE,
                                                    cadd[:, t, 0:NCMP].unsqueeze(1).to_broadcast([P, 8, NCMP]), ALU.mult, ALU.add))
            v.wait_ge(dve_step, step.n)
            call = csc.rearrange("p o t n -> p (o t n)").rearrange("p (h c) -> p h c", c=16)[:, :, 0:NCMP]
            step.then(v.tensor_reduce(cmx[:, 0:32], call, AX, ALU.max))
            step.then(v.tensor_tensor(call, call, bcast(cmx[:, 0:32], NCMP), ALU.subtract))
            v.sem_inc(cexp_dve, 1)
            v.wait_ge(cexp_act, 1)
            step.then(v.tensor_reduce(csum[:, 0:32], call, AX, ALU.add))
            step.then(v.reciprocal(csum[:, 0:32], csum[:, 0:32]))
            v.wait_ge(gl_ready, 1)
            for o in range(2):
                for t in range(NT):
                    gate = gl[:, t].rearrange("p (h w) -> p h w", w=6)[:, :, 3 * o]
                    at = (o * NT + t) * 8
                    step.then(v.tensor_tensor(csum[:, at:at + 8], csum[:, at:at + 8], gate, ALU.mult))
                    step.then(v.tensor_tensor(c16(csc[:, o, t]), c16(csc[:, o, t]),
                                              cm01[:, t, 0:NCMP].unsqueeze(1).to_broadcast([P, 8, NCMP]), ALU.mult))
                    step.then(v.tensor_tensor(c16(csc[:, o, t]), c16(csc[:, o, t]), bcast(csum[:, at:at + 8], NCMP), ALU.mult))
            v.sem_inc(cw_ready, 1)
            nu = 2 * NT * GR

            def unit_weights(u, t, g, br):
                nk = (t + 1) * P
                v.wait_ge(e_ready, 4 * (u + 1))
                s4 = sums[:, u % 2]
                step.then(v.reciprocal(s4, s4))
                gate = gl[:, t, 12 * g:12 * g + 12].rearrange("p (j o w) -> p o j w", j=2, w=3)[:, :, :, 1 + br]
                s22 = s4.rearrange("p (o j) -> p o j", j=2)
                step.then(v.tensor_tensor(s22, s22, gate, ALU.mult))
                v.tensor_tensor(E[u % 2][:, :, 0:nk], E[u % 2][:, :, 0:nk], bcast(s4, nk), ALU.mult).then_inc(p_ready, 1)

            unit_max(0, P)
            for u in range(nu):
                t, g, br = u // 8, (u // 2) % GR, u % 2
                if u + 1 < nu:
                    unit_max(u + 1, ((u + 1) // 8 + 1) * P)
                unit_weights(u, t, g, br)
                if t:
                    v.wait_ge(pT_psum, u + 1)
                    v.tensor_copy(pT[u % 2][1], ps[5][:, :].rearrange("p (h q) -> p h q", h=4)).then_inc(pT_dve, 1)
            residual("nsa_out", 13, 0, lambda s, t: 2 * s + t)
            def mlp(l):
                norm2(4 + 2 * l, 3 + 2 * l, l, 1)
                gate_cols(1 + 2 * l, l, 5)
                v.wait_ge(slabs_used, SLABS[f"mlp{l}"] + 16)
                residual(None, 0, 1 + 2 * l, lambda s, t: 2 * t + s)

            mlp(0)
            norm2(5, 4, 1, 0)
            gate_cols(2, 1, 2)
            v.wait_ge(diff_in_sem, 6 * 16)
            for k in range(2):
                step.then(v.tensor_tensor(lamv[:, 2 * k], lamv[:, 2 * k], lamv[:, 2 * k + 1], ALU.mult))
            for k in range(2):
                step.then(v.tensor_reduce(dl[:, k:k + 1], lamv[:, 2 * k], AX, ALU.add))
            step.then(v.tensor_copy(lamv[:, 0, 0:2], dl[:, 0:2]))
            v.sem_inc(lam_dve, 1)
            for s in (4, 5):
                for t in range(NT):
                    bank_done(v, "diff_in", s, t, 15 + s)
                    v.tensor_copy(proj[:, t, s * NB:(s + 1) * NB], ps[(s % 2) * 2 + t][:, :]).then_inc(proj_dve, 1)
            v.wait_ge(lam_act, 1)
            step.then(v.tensor_tensor(dl[:, 0:1], lamv[:, 0, 1:2], lamv[:, 0, 0:1], ALU.subtract))
            step.sig(v.tensor_scalar(dl[:, 0:1], dl[:, 0:1], -LAM0, None, ALU.add))
            step.then(v.tensor_scalar(lamv[:, 1, 0:1], cols[:, ROWS["subln"]:ROWS["subln"] + 1], 1.0 - LAM0, None, ALU.mult))
            v.wait_ge(proj_act, 18 + 8)
            for t in range(NT):
                step.sig(v.tensor_reduce(ss[:, 32 * t:32 * t + 16], sqn[:, t, 0:1024].rearrange("p (h e) -> p h e", e=DH), AX, ALU.add))
                step.sig(v.tensor_reduce(ss[:, 32 * t + 16:32 * t + 32], dsq[:, t, 0:1024].rearrange("p (h e) -> p h e", e=DH), AX, ALU.add))
            v.wait_ge(dve_step, step.n)
            v.sem_inc(sum_ready, 1)
            v.wait_ge(rms_ready, 11)
            step.then(v.reciprocal(rstd[:, 0:64], rms[:, 0:64]))
            rope_s = view(work, 0, 4, 256)
            for w in range(2):
                scaled(1024 * w, QH, 16 * w, 32, dgain[:, w])
                rope(1024 * w, QH)
                v.sem_inc(rows_ready, 1)
                v.wait_ge(heads_psum, 8 + 2 * w)
                for k in range(2):
                    v.tensor_copy(dqT[w][:, 4 * k:4 * k + 4, P:S], ps[4 * w + 2 + k][:, :].rearrange("p (h q) -> p h q", h=4)).then_inc(heads_dve, 1)

            def diff_weights(u, nk):
                v.wait_ge(e_ready, 4 * (u + 1))
                s4 = sums[:, u % 2]
                step.then(v.reciprocal(s4, s4))
                step.then(v.tensor_scalar(s4[:, 2:4], s4[:, 2:4], dl[:, 0:1], None, ALU.mult))
                for j in range(2):
                    step.sig(v.tensor_scalar(E[u % 2][:, 2 + j, 0:nk], E[u % 2][:, 2 + j, 0:nk], s4[:, 2 + j:3 + j], None, ALU.mult))
                v.wait_ge(dve_step, step.n)
                for j in range(2):
                    v.scalar_tensor_tensor(E[u % 2][:, j, 0:nk], E[u % 2][:, j, 0:nk], s4[:, j:j + 1], E[u % 2][:, 2 + j, 0:nk],
                                           ALU.mult, ALU.add).then_inc(p_ready, 1)

            unit_max(nu, P)
            for u in range(8):
                nk = (u // 4 + 1) * P
                if u < 7:
                    unit_max(nu + u + 1, ((u + 1) // 4 + 1) * P)
                diff_weights(nu + u, nk)
                v.wait_ge(pT_psum, nu + u + 1)
                v.tensor_copy(pT[u % 2][0][:, 0:2 * (u // 4 + 1)], ps[4 + u % 2][:, 0:2 * nk].rearrange("p (h q) -> p h q", q=P)).then_inc(pT_dve, 1)
            v.wait_ge(sq_act, 2)
            for t in range(NT):
                step.sig(v.tensor_reduce(ss[:, 8 * t:8 * t + 8], work[:, t * D:(t + 1) * D].rearrange("p (h e) -> p h e", e=P), AX, ALU.add))
            v.wait_ge(dve_step, step.n)
            v.sem_inc(sum_ready, 1)
            v.wait_ge(rms_ready, 12)
            step.then(v.reciprocal(rstd[:, 0:16], rms[:, 0:16]))
            for t in range(NT):
                o = proj[:, t, 0:D].rearrange("p (h e) -> p h e", e=P)
                v.tensor_tensor(o, o, bcast(rstd[:, 8 * t:8 * t + 8], P), ALU.mult).then_inc(orow_ready, 1)
            v.wait_ge(abT_psum, 6)
            for c in range(0, 4):
                v.tensor_scalar(mixT[:, c], ps[c // 2][:, (c % 2) * S:(c % 2) * S + S], lamv[:, 1, 0:1], None, ALU.mult).then_inc(mixT_dve, 1)
            residual("diff_out", 21, 2, lambda s, t: 4 + 2 * s + t)
            mlp(1)

        @block.tensor
        def _(pe):
            r = Ring()
            step = Steps(pe, pe_step)

            def arrived(slot):
                _, loads = r.take(slot)
                pe.wait_ge(landed[slot], 16 * loads)

            def norm_T(i):
                for t in range(NT):
                    pe.wait_ge(xn_ready, 2 * i + t + 1)
                    for c in range(KC):
                        m = pe.transpose(ps[4 + c // 2][:, (c % 2) * S + t * P:(c % 2) * S + t * P + P],
                                         xn[:, t, c * P:c * P + P], ident[:, :])
                m.then_inc(xnT_psum, 1)

            def product(bank, lhs, t, slot):
                w = slab(slot)
                for c in range(KC):
                    m = pe.matmul(bank[:, :], lhs[:, c, t * P:t * P + P], w[:, c, :], start=(c == 0), stop=(c == KC - 1))
                return m

            pe.wait_ge(const_ready, 1)
            pe.wait_ge(small_in[0], 16 * 11)
            pe.transpose(ps[0][:, 0:NROWS], rows[0:NROWS, :], ident[0:NROWS, 0:NROWS])
            pe.transpose(ps[0][:, P:P + NADA], arow[:, :], ident[0:NADA, 0:NADA])
            pe.wait_ge(small_in[2], 16)
            for g in range(HA):
                m = pe.transpose(ps[1][:, g * P:g * P + P], ws[:, g], ident[:, :])
            m.then_inc(small_psum, 1)
            norm_T(0)
            pe.wait_ge(hT_dve, 4)
            pe.wait_ge(hT_act, 4)
            pe.wait_ge(cols_ready, 1)
            pe.wait_ge(dve_step, 4)
            for s in range(6):
                arrived(s)
                for t in range(NT):
                    if s >= 2:
                        pe.wait_ge(proj_act, 2 * (s - 2) + t + 1)
                    product(ps[(s % 2) * 2 + t], hT, t, s).then_inc(slabs_used if t else half_psum, 1)
            for t in range(NT):
                pe.wait_ge(vh_ready, t + 1)
                for g in range(HA):
                    m = pe.matmul(ps[6 + t][:, g * P:g * P + P], wT[:, g], proj[:, t, NB + g * P:NB + g * P + P],
                                  start=True, stop=True)
                m.then_inc(mixed_psum, 1)
            pe.wait_ge(crep_ready, KC)
            pe.wait_ge(mixed_taken, 1)
            pe.sem_inc(ada_cols, 1)
            with pe.Fori(0, 4) as it:
                def to_cols(s):
                    pe.wait_ge(ada_rows, it * 6 + s + 1)
                    for c in range(4):
                        m = pe.matmul(ps[6][:, 4 * s + c:4 * s + c + 1], ada_row[:, s % 2, c * P:c * P + P], sel4[:, :],
                                      start=True, stop=True)
                    m.then_inc(ada_cols, 1)

                for s in range(6):
                    pe.wait_ge(landed[s], it * 16 + 16 * (r.loads[s] + 1))
                    for c in range(KC):
                        j = c % 4
                        m = pe.matmul(ps[4 + s % 2][32 * j:32 * j + 32, :], crep[:, c], slab(s)[:, c, :],
                                      start=(c < 4), stop=(c >= 4), skip_group_check=True)
                    m.then_inc(slabs_used, 1)
                    if s >= 1:
                        if s == 1:
                            pe.wait_ge(mod_ready, it + 1)
                        to_cols(s - 1)
                to_cols(5)
            r.skip(range(6), 4)
            pe.wait_ge(lf_ready, 1)
            for t in range(NT):
                for m_ in range(3):
                    pe.matmul(ps[3 * t + m_][:, :], cum[:, m_], lf[:, t], start=True, stop=True)
            pe.wait_ge(mod_ready, 5)
            for t in range(NT):
                for h in range(HA):
                    m = pe.matmul(ps[6][:, 8 * t + h:8 * t + h + 5:4], lf[:, t, h * P:h * P + P], same[:, :], start=True, stop=True)
            m.then_inc(cum_psum, 1)
            for j in range(3):
                for t in range(NT):
                    pe.wait_ge(ex_act, 9)
                    pe.wait_ge(ex_ready, 4 * t + j + 1)
                    for h in range(HA):
                        m = pe.transpose(ps[2 * j + t][:, h * P:h * P + P], ex[:, j, t, h * P:h * P + P], ident[:, :])
                    m.then_inc(exT_psum, 1)
            pe.wait_ge(exT_dve, 3)
            pe.wait_ge(exT_ready, 3)
            for t in range(NT):
                a = slice(t * P, t * P + P)
                for h in range(HA):
                    m = pe.matmul(ps[t][:, h * P:h * P + P], exT[:, 1, h, a], exT[:, 0, h, a], start=True, stop=True)
                m.then_inc(sc_psum, 1)
            pe.wait_ge(ex_ready, 8)
            pe.wait_ge(proj_dve, 2)
            for n in range(3):
                t, b = n // 2, CH * (n % 2)
                for h in range(HA):
                    a = slice(h * P, h * P + P)
                    m = pe.matmul(ps[2 + n][:, a], ex[b:b + CH, 3, t, a], proj[b:b + CH, t, 4 * NB + h * P:4 * NB + h * P + P],
                                  start=True, stop=True)
            m.then_inc(u_psum, 1)
            for t in range(NT):
                pe.wait_ge(sc_ready, t + 1)
                for h in range(HA):
                    a = slice(h * P, h * P + P)
                    pe.matmul(ps[5 + t][:, a], scT[:, t, a], proj[:, t, 4 * NB + h * P:4 * NB + h * P + P],
                              start=(h == 0), stop=False, skip_group_check=True)
            pe.wait_ge(st_ready, 1)
            for n in (1, 2, 3):
                t, b = n // 2, CH * (n % 2)
                for h in range(HA):
                    a = slice(h * P, h * P + P)
                    m = pe.matmul(ps[5 + t][b:b + CH, a], exT[:, 2, h, n * CH:n * CH + CH], st[:, n - 1, a],
                                  start=False, stop=True, skip_group_check=True)
            m.then_inc(o_psum, 1)
            pe.wait_ge(ab_ready, 2)
            for c in range(KC):
                for t in range(NT):
                    src = c * P if c < 4 else 5 * NB + (c - 4) * P
                    m = pe.transpose(ps[c // 2][:, (c % 2) * S + t * P:(c % 2) * S + t * P + P], proj[:, t, src:src + P], ident[:, :])
                if c % 2:
                    m.then_inc(abT_psum, 1)
            pe.wait_ge(mixT_dve, 4)
            pe.wait_ge(mixT_act, 4)
            for s in range(2):
                arrived(s)
                for t in range(NT):
                    product(ps[4 + 2 * s + t], mixT, t, s).then_inc(slabs_used if t else half_psum, 1)
            norm_T(1)
            pe.wait_ge(hT_dve, 8)
            pe.wait_ge(hT_act, 8)
            pe.wait_ge(small_in[3], 64)
            for t in range(NT):
                for c in range(KC):
                    m = pe.matmul(ps[0][:, t * (NG + NE):(t + 1) * (NG + NE)], hT[:, c, t * P:t * P + P], wr[:, c, :],
                                  start=(c == 0), stop=(c == KC - 1))
            m.then_inc(logit_psum, 1)
            pe.wait_ge(chosen_ready, 1)
            for t in range(NT):
                for u in range(t + 1):
                    pe.matmul(ps[1][:, t * NE:(t + 1) * NE], before[:, :] if u == t else ones[:, :], chosen[:, u],
                              start=(u == 0), stop=(u == t))
            for u in range(NT):
                m = pe.matmul(ps[1][:, NT * NE:(NT + 1) * NE], ones[:, :], chosen[:, u], start=(u == 0), stop=(u == NT - 1))
            m.then_inc(pos_psum, 1)

            def gather(m):
                for k in range(2):
                    for c in range(4 * k, 4 * k + 4):
                        for t in range(NT):
                            ins = pe.matmul(ps[6 + k][:, (c % 4) * 2 * BT:(c % 4 + 1) * 2 * BT], xn[:, t, c * P:c * P + P],
                                            pick[:, t], start=(t == 0), stop=(t == NT - 1))
                    ins.then_inc(m.gathered, 1)

            def pair(m, q):
                pe.wait_ge(m.xg_ready, q * 2 + 2)
                pe.wait_ge(m.o_act, q + 1)
                pe.wait_ge(m.o_dve, q + 1)
                for part in range(2):
                    m.wait_landed(pe, q, 2 * part)
                    m.wait_landed(pe, q, 2 * part + 1)
                    for c in range(KC):
                        for e in range(2):
                            ins = pe.matmul(ps[4 + part][BT * e:BT * e + BT, :], xgT[:, c, BT * e:BT * e + BT],
                                            slab(ESLOT[2 * part + e])[:, c, :], start=(c == 0), stop=(c == KC - 1),
                                            skip_group_check=True)
                    ins.then_inc(m.used, 2)
                pe.wait_ge(m.pick_ready, q + 2)
                pe.wait_ge(m.hT_ready, q + 1)
                pe.wait_ge(m.pickT_ready, q + 1)
                gather(m)
                pe.wait_ge(m.h_ready, q + 1)
                pe.wait_ge(m.xg_ready, q * 2 + 3)
                for c in range(FE // P):
                    ins = pe.transpose(ps[6][:, c * P:c * P + P], eh[:, c * P:c * P + P], ident[:, :])
                ins.then_inc(m.hT_psum, 1)
                pe.wait_ge(m.pickw_ready, q + 1)
                pe.wait_ge(m.xg_ready, q * 2 + 4)
                for t in range(NT):
                    ins = pe.transpose(ps[7][:, t * P:t * P + P], pickw[:, t], ident[:, :])
                ins.then_inc(m.pickT_psum, 1)
                pe.wait_ge(m.hT_ready, q + 2)
                m.wait_landed(pe, q, 4)
                m.wait_landed(pe, q, 5)
                for n in range(2):
                    for c in range(FE // P):
                        for e in range(2):
                            w = ring[:, ESLOT[4 + e]].rearrange("p (c n) -> p c n", n=D)
                            ins = pe.matmul(ps[4 + n][BT * e:BT * e + BT, :], ehT[:, c, BT * e:BT * e + BT],
                                            w[:, c, n * NB:n * NB + NB], start=(c == 0), stop=(c == FE // P - 1),
                                            skip_group_check=True)
                    if n == 0:
                        ins.then_inc(m.down, 1)
                    else:
                        ins.then_inc(m.used, 2)
                pe.wait_ge(m.pickT_ready, q + 2)
                pe.wait_ge(m.o_act, q + 2)
                pe.wait_ge(m.o_dve, q + 2)
                for t in range(NT):
                    for n in range(2):
                        ins = pe.matmul(ps[2 * t + n][:, :], pickT[:, t * P:t * P + P], eo[:, n * NB:n * NB + NB],
                                        start=False, stop=True, skip_group_check=True)
                ins.then_inc(m.scattered, 1)

            pe.wait_ge(blocks_ready, 1)
            for i in range(4):
                pe.matmul(ps[i][:, :], zb[:, 0:P], zb[:, :], start=True, stop=True, skip_group_check=True)
            pe.wait_ge(main.pick_ready, 1)
            gather(main)
            pe.sem_inc(main.pickT_psum, 1)
            with pe.Fori(0, PAIRS) as q:
                pair(main, q)
            r.skip(ESLOT, PAIRS)
            pe.wait_ge(ovf.pick_ready, 1)
            pe.wait_ge(main.hT_ready, PAIRS + 1)
            pe.wait_ge(main.pickT_ready, PAIRS + 1)
            pe.wait_ge(main.xg_ready, 2 * PAIRS + 2)
            gather(ovf)
            pe.sem_inc(ovf.pickT_psum, 1)
            with pe.Fori(0, OVF_PAIRS) as q:
                pair(ovf, q)
            def norm2(i, j):
                norm_T(i)
                pe.wait_ge(hT_dve, 4 * (j + 1))
                pe.wait_ge(hT_act, 4 * (j + 1))

            def gate_rows(k):
                pe.wait_ge(rep_ready, k + 1)
                for c in range(KC):
                    ins = pe.matmul(ps[4 + c // 4][:, (c % 4) * P:(c % 4) * P + P], rep[:, c], ident[:, :], start=True, stop=True)
                ins.then_inc(gate_psum, 1)

            def head_T(first, n, banks):
                def do(t):
                    for c in range(n):
                        ins = pe.transpose(ps[banks + c // 4][:, (c % 4) * P:(c % 4) * P + P],
                                           proj[:, t, first + c * P:first + c * P + P], ident[:, :])
                    ins.then_inc(heads_psum, 1)
                return do

            pe.wait_ge(x_ready, 8)
            norm2(3, 2)
            gate_rows(0)
            for s in range(5):
                arrived(NSLOT[s])
                for t in range(NT):
                    if s >= 2:
                        if s == 4:
                            pe.wait_ge(proj_dve, 2 + t + 1)
                        else:
                            pe.wait_ge(proj_act, 10 + 2 * (s - 2) + t + 1)
                    product(ps[(s % 2) * 2 + t], hT, t, NSLOT[s]).then_inc(slabs_used if t else half_psum, 1)
            pe.wait_ge(nsa_in_sem, 9 * 16)
            for t in range(NT):
                for c in range(KC):
                    ins = pe.matmul(ps[7][:, t * 3 * QH:(t + 1) * 3 * QH], hT[:, c, t * P:t * P + P], wgl[:, c], start=(c == 0), stop=(c == KC - 1))
            ins.then_inc(gl_psum, 1)
            pe.wait_ge(proj_dve, 4)
            pe.wait_ge(proj_act, 18)
            for w in range(2):
                for gp in range(2):
                    for t in range(NT):
                        at = 2 * NB + w * 256 + gp * P
                        ins = pe.transpose(ps[2 * w + gp][:, t * P:t * P + P], proj[:, t, at:at + P], ident[:, :])
                    ins.then_inc(kz_psum, 1)
            arrived(NSLOT[5])
            pe.wait_ge(cv1_in, 16)
            cw1 = ring[:, NSLOT[5]].rearrange("p (w j m) -> p w j m", w=2, m=P)
            pe.wait_ge(gate_ready, 2)
            for w in range(2):
                pe.wait_ge(kz_dve if w else kz_act, 8)
                for j in range(16):
                    pe.matmul(ps[4 + w][:, 0:GR * NCMP], cw1[:, w, j], kz[:, w, :, 2 * j:2 * j + 16 * NCMP - 15:16],
                              start=(j == 0), stop=(j == 15))
                pcol = ROWS["pe_v" if w else "pe_k"]
                for j in range(16):
                    ins = pe.matmul(ps[4 + w][:, 64:65], cw1[:, w, j], cols[:, pcol + j:pcol + j + 1], start=(j == 0), stop=(j == 15))
                ins.then_inc(cmp_psum, 1)
            pe.wait_ge(cmp_act, 1)
            pe.matmul(ps[6][0:GR * NCMP, 0:DH], hc[:, 0], w2c[:, 0], start=True, stop=True).then_inc(cmp_psum, 1)
            pe.wait_ge(cmp_act, 2)
            pe.sem_inc(slabs_used, 1)
            pe.wait_ge(gl_dve, 1)
            for g in range(GR):
                ins = pe.matmul(ps[7][0:NCMP, g * DH:g * DH + DH], hc[:, 1, g * NCMP:(g + 1) * NCMP], w2c[:, 1], start=True, stop=True)
            ins.then_inc(cmp_psum, 1)
            pe.wait_ge(rows_ready, 1)
            pe.wait_ge(kz_act, 8)
            pe.wait_ge(kz_dve, 8)
            for t in range(NT):
                head_T(0, 8, 2 * t)(t)
            pe.wait_ge(cmp_dve, 3)
            pe.transpose(ps[6][0:DH, 64:64 + GR * NCMP], kcm[0:GR * NCMP], ident[0:GR * NCMP, 0:GR * NCMP]).then_inc(cmp_psum, 1)
            for br in range(2):
                pe.wait_ge(rows_ready, 2 + br)
                if br:
                    pe.wait_ge(heads_dve, 2)
                else:
                    pe.wait_ge(heads_act, 2)
                for t in range(NT):
                    for g in range(GR):
                        at = 1536 + 512 * br + g * DH
                        ins = pe.transpose(ps[2 * br + t][0:DH, g * P:g * P + P], proj[:, t, at:at + DH], ident[:, :])
                ins.then_inc(heads_psum, 1)
            pe.wait_ge(rows_ready, 4)
            pe.wait_ge(cmp_dve, 6)
            for t in range(NT):
                head_T(0, 8, 4 + 2 * t)(t)
            pe.wait_ge(heads_act, 6)
            for t in range(NT):
                for h in range(QH):
                    o = h % 2
                    at = t * P + (h // 2) * 16
                    g = h // 4
                    ins = pe.matmul(ps[o][:, at:at + NCMP], qcT[DH * o:DH * o + DH, h // 2, t * P:t * P + P],
                                    kcT[DH * o:DH * o + DH, g * NCMP:(g + 1) * NCMP], start=True, stop=True)
            ins.then_inc(csc_psum, 1)
            pe.wait_ge(heads_dve, 8)
            pe.wait_ge(heads_act, 8)
            pe.wait_ge(cw_ready, 1)
            nu = 2 * NT * GR

            def scores(u, t, g, br):
                if u >= 2:
                    pe.wait_ge(e_ready, 4 * (u - 1))
                nk = (t + 1) * P
                for j in range(2):
                    for o in range(2):
                        c = 2 * g + j
                        ins = pe.matmul(ps[2 * (u % 2) + o][:, j * S:j * S + nk], qrT[DH * o:DH * o + DH, c, t * P:t * P + P],
                                        kT[DH * o:DH * o + DH, br, g, 0:nk], start=True, stop=True)
                ins.then_inc(sc2_psum, 1)

            scores(0, 0, 0, 0)
            for n in range(NT * GR):
                t, g = n // GR, n % GR
                if n:
                    pe.wait_ge(pcT_ready, n)
                for o in range(2):
                    for j in range(2):
                        c = 2 * g + j
                        ins = pe.transpose(ps[7][0:NCMP, (2 * o + j) * P:(2 * o + j + 1) * P], csc[:, o, t, c * 16:c * 16 + NCMP], ident[:, :])
                ins.then_inc(pcT_psum, 1)
                for br in range(2):
                    u = 2 * n + br
                    if u + 1 < nu:
                        scores(u + 1, (u + 1) // 8, ((u + 1) // 2) % GR, (u + 1) % 2)
                    pe.wait_ge(p_ready, u + 1)
                    if u >= 1:
                        pe.wait_ge(pT_act, u)
                        if u > 8:
                            pe.wait_ge(pT_dve, u - 8)
                    for kb in range(t + 1):
                        for i in range(4):
                            ins = pe.transpose(ps[4 + kb][:, i * P:i * P + P], E[u % 2][:, i, kb * P:kb * P + P], ident[:, :])
                    ins.then_inc(pT_psum, 1)
                    if br == 0:
                        if n:
                            pe.wait_ge(ot_ready, n)
                        pe.wait_ge(pcT_ready, n + 1)
                        for o in range(2):
                            pe.matmul(ps[6][DH * o:DH * o + DH, 0:S], vcm[0:NCMP, g], pcT[0:NCMP, n % 2, 2 * o:2 * o + 2],
                                      start=True, stop=False, skip_group_check=True)
                    pe.wait_ge(pT_act, u + 1)
                    if t:
                        pe.wait_ge(pT_dve, u - 7)
                    for kb in range(t + 1):
                        at = 1792 + 512 * br + g * DH
                        for o in range(2):
                            ins = pe.matmul(ps[6][DH * o:DH * o + DH, 0:S], proj[:, kb, at:at + DH], pT[u % 2][kb][:, 2 * o:2 * o + 2],
                                            start=False, stop=(br == 1 and kb == t), skip_group_check=True)
                    if br:
                        ins.then_inc(ot_psum, 1)
            pe.wait_ge(ot_ready, 8)
            pe.wait_ge(e_ready, 4 * nu)
            for s in range(2):
                arrived(NSLOT[s])
                for t in range(NT):
                    product(ps[2 * s + t], mixT, t, NSLOT[s]).then_inc(slabs_used if t else half_psum, 1)
            def mlp(l):
                norm2(4 + 2 * l, 3 + 2 * l)
                gate_rows(1 + 2 * l)
                pe.wait_ge(x_ready, 16 + 8 * l)
                pe.wait_ge(gate_ready, 4 + 4 * l)
                for i in range(4):
                    pe.matmul(ps[i][:, :], zb[:, 0:P], zb[:, :], start=True, stop=True, skip_group_check=True)
                base = [16 * r.loads[s] for s in MSLOT]

                def hidden(k, slot):
                    if not isinstance(k, int) or k + l > 0:
                        pe.wait_ge(hid_ready, k * 2 + l * 2 * MC)
                    w = slab(slot)
                    for m in range(4):
                        for c in range(KC):
                            ins = pe.matmul(ps[4 + m // 2][:, (m % 2) * S:(m % 2) * S + S], w[:, c, m * P:m * P + P], hT[:, c],
                                            start=(c == 0), stop=(c == KC - 1))
                    ins.then_inc(slabs_used, 1)

                def output(k, par, slot):
                    pe.wait_ge(hid_ready, k * 2 + (l * 2 * MC + 2))
                    w = ring[:, slot].rearrange("p (c n) -> p c n", n=D)
                    for t in range(NT):
                        for n in range(2):
                            for c in range(4):
                                ins = pe.matmul(ps[2 * t + n][:, :], hid[par][:, c, t * P:t * P + P], w[:, c, n * NB:n * NB + NB],
                                                start=False, stop=(c == 3), skip_group_check=True)
                    ins.then_inc(slabs_used, 1)

                def wait_slab(i, n):
                    q, m = n // 4, n % 4
                    pe.wait_ge(landed[MSLOT[m]], i * 16 + (base[m] + 16 + 16 * q))

                zero = 0
                wait_slab(zero, 0)
                hidden(zero, MSLOT[0])
                with pe.Fori(0, 3) as i:
                    wait_slab(i, 1)
                    hidden(i * 2 + 1, MSLOT[1])
                    wait_slab(i, 2)
                    output(i * 2, 0, MSLOT[2])
                    wait_slab(i, 3)
                    hidden(i * 2 + 2, MSLOT[3])
                    wait_slab(i, 4)
                    output(i * 2 + 1, 1, MSLOT[0])
                wait_slab(3, 1)
                hidden(7, MSLOT[1])
                wait_slab(3, 2)
                output(6, 0, MSLOT[2])
                wait_slab(3, 3)
                output(7, 1, MSLOT[3])
                r.skip(MSLOT, 4)

            mlp(0)
            norm2(5, 4)
            gate_rows(2)
            pe.wait_ge(x_ready, 20)
            for s in range(6):
                arrived(NSLOT[s])
                for t in range(NT):
                    if s >= 2:
                        pe.wait_ge(proj_act, 18 + 2 * (s - 2) + t + 1)
                    product(ps[(s % 2) * 2 + t], hT, t, NSLOT[s]).then_inc(slabs_used if t else half_psum, 1)
            pe.wait_ge(proj_dve, 4 + 4)
            pe.wait_ge(proj_act, 26)
            pe.wait_ge(gate_ready, 6)
            for w in range(2):
                pe.wait_ge(rows_ready, 5 + w)
                for t in range(NT):
                    head_T(1024 * w, 8, (4 * w + 2 * t))(t)
            pe.wait_ge(heads_act, 12)
            pe.wait_ge(heads_dve, 12)

            def dscores(u):
                t, hp = u // 4, u % 4
                if u >= 2:
                    pe.wait_ge(e_ready, 4 * (nu + u - 1))
                nk = (t + 1) * P
                for j in range(2):
                    for o in range(2):
                        h = 2 * hp + j
                        ins = pe.matmul(ps[2 * (u % 2) + o][:, j * S:j * S + nk], dqT[0][DH * o:DH * o + DH, h, t * P:t * P + P],
                                        dqT[1][DH * o:DH * o + DH, h, 0:nk], start=True, stop=True)
                ins.then_inc(sc2_psum, 1)

            dscores(0)
            for u in range(8):
                t, hp = u // 4, u % 4
                if u < 7:
                    dscores(u + 1)
                pe.wait_ge(p_ready, nu + 2 * u + 2)
                if u >= 2:
                    pe.wait_ge(pT_dve, 8 + u - 1)
                for kb in range(t + 1):
                    for j in range(2):
                        ins = pe.transpose(ps[4 + u % 2][:, (2 * kb + j) * P:(2 * kb + j + 1) * P], E[u % 2][:, j, kb * P:kb * P + P], ident[:, :])
                ins.then_inc(pT_psum, 1)
                pe.wait_ge(pT_dve, 8 + u + 1)
                if u >= 2:
                    pe.wait_ge(ot_ready, 8 + u - 1)
                for j in range(2):
                    h = 2 * hp + j
                    for kb in range(t + 1):
                        ins = pe.matmul(ps[6 + u % 2][:, j * P:j * P + P], pT[u % 2][0][:, 2 * kb + j], proj[:, kb, 2048 + h * P:2048 + h * P + P],
                                        start=(kb == 0), stop=(kb == t))
                ins.then_inc(ot_psum, 1)
            pe.wait_ge(orow_ready, 2)
            for c in range(KC):
                for t in range(NT):
                    ins = pe.transpose(ps[c // 2][:, (c % 2) * S + t * P:(c % 2) * S + t * P + P], proj[:, t, c * P:c * P + P], ident[:, :])
                if c % 2:
                    ins.then_inc(abT_psum, 1)
            pe.wait_ge(mixT_dve, 8)
            pe.wait_ge(mixT_act, 8)
            for s in range(2):
                arrived(NSLOT[s])
                for t in range(NT):
                    product(ps[4 + 2 * s + t], mixT, t, NSLOT[s]).then_inc(slabs_used if t else half_psum, 1)
            mlp(1)


_INS = ["x", "norm1_gain", "w_in", "gmlp_v_gain", "gmlp_w_s", "gmlp_b_s", "hgrn_lower_bounds", "hgrn_out_gain",
        "w_out", "norm2_gain", "w_group_router", "b_group_router", "w_expert_router", "b_expert_router",
        "w_gate", "w_up", "w_down", "final_gain", "c_2", "positions_2", "ln_mix_g_2", "ln_mlp_g_2", "w_ada_2",
        "b_ada_2", "w_mlp_in_2", "w_mlp_out_2", "nsa_w_in_2", "nsa_b_gate_2", "nsa_q_gain_2", "nsa_k_gain_2",
        "nsa_pe_k_2", "nsa_w_ck1_2", "nsa_w_ck2_2", "nsa_pe_v_2", "nsa_w_cv1_2", "nsa_w_cv2_2", "nsa_w_out_2",
        "diff_w_in_2", "diff_q_gain_2", "diff_k_gain_2", "diff_lq1_2", "diff_lk1_2", "diff_lq2_2", "diff_lk2_2",
        "diff_subln_g_2", "diff_w_out_2"]
_KEEP = {"hgrn_lower_bounds", "final_gain", "ln_mix_g_2", "ln_mlp_g_2", "w_ada_2", "b_ada_2", "w_mlp_in_2",
         "w_mlp_out_2"}


def kernel(**inputs):
    import numpy as np
    import concourse.bacc as bacc
    from concourse.bass_utils import run_bass_kernel_spmd

    nc = bacc.Bacc("TRN2", target_bir_lowering=False, num_devices=1)
    arrays, d = {}, {}
    for name in _INS:
        a = np.ascontiguousarray(inputs[name])
        if name not in _KEEP:
            a = a[0]
        arrays[f"in_{name}"] = a
        d[name] = nc.dram_tensor(f"in_{name}", a.shape, mybir.dt.from_np(a.dtype), kind="ExternalInput").ap()
    out = nc.dram_tensor("out", (S, D), F32, kind="ExternalOutput").ap()
    build(nc, d, out)
    r = run_bass_kernel_spmd(nc, [arrays], core_ids=[0])
    return r.results[0]["out"].reshape(1, S, D)
```

```python
import math
from contextlib import ExitStack

import concourse.bass as bass
import numpy as np
from concourse import mybir

F32 = mybir.dt.float32
F32R = mybir.dt.float32r
BF16 = mybir.dt.bfloat16
I32 = mybir.dt.int32
U32 = mybir.dt.uint32
ALU = mybir.AluOpType
ACT = mybir.ActivationFunctionType
AX = mybir.AxisListType.X

P = 128
D = 1024
KC = D // P
S = 256
NT = S // P
NB = 512
SLAB = KC * NB
SLOTS = 6
EPS = 1e-6
NEG = -1e30

HA = 4
CH = 64
NE = 32
NG = 4
EPG = NE // NG
FE = 512
BT = 64
PAIRS = NE // 2
OVF = (2 * S) // BT
OVF_PAIRS = OVF // 2
BLOCKS = NE + OVF

DH = 64
QH = 16
GR = 4
RD = 8
THETA = 500000.0
NCMP = (S - 32) // 16 + 1
SCALE = DH ** -0.5
DFF = 4096
MC = DFF // NB
TWO_PI = 2.0 * math.pi
PI1 = 6.28125
PI2 = float(round((TWO_PI - PI1) * 2.0 ** 22)) / 2.0 ** 22
PI3 = TWO_PI - PI1 - PI2
ROUND = 1.5 * 2.0 ** 23
LAM0 = 0.8 - 0.6 * math.exp(-0.3)

ROWS = {}
_at = 0
for _name, _n in (("norm1", 8), ("norm2", 8), ("mix", 16), ("mlp", 16), ("hgain", 4), ("bs", 4),
                  ("subln", 1), ("pe_k", 16), ("pe_v", 16), ("c", 8)):
    ROWS[_name] = _at
    _at += _n
NROWS = _at
ADA = 2 * 6 * D // NB
NADA = 2 * 6 * KC


SLABS = {}
_at = 0
for _name, _n in (("in_and_ada", 30), ("w_out", 2), ("experts", 6 * PAIRS),
                  ("nsa_in", 5), ("nsa_cmp", 1), ("nsa_out", 2), ("mlp0", 16), ("diff_in", 6), ("diff_out", 2),
                  ("mlp1", 16)):
    SLABS[_name] = _at
    _at += _n


def in_slab(s):
    return 3 * s + 1


def ada_slab(n):
    return 3 * (n // 2) + 2 * (n % 2) if n < ADA // 2 else n + 6


class Steps:

    def __init__(self, eng, sem, it=None, per=0):
        self.eng, self.sem, self.it, self.per, self.n = eng, sem, it, per, 0

    def value(self):
        return self.n if self.it is None else self.it * self.per + self.n

    def sig(self, ins):
        self.n += 1
        ins.then_inc(self.sem, 1)

    def then(self, ins):
        self.sig(ins)
        self.eng.wait_ge(self.sem, self.value())


class Ring:

    def __init__(self):
        self.n, self.last, self.loads = 0, [0] * SLOTS, [0] * SLOTS

    def take(self, slot):
        free = self.last[slot]
        self.n += 1
        self.last[slot] = self.n
        self.loads[slot] += 1
        return free, self.loads[slot]

    def skip(self, slots, rounds):
        for _ in range(rounds):
            for s in slots:
                self.take(s)


def build(nc, d, out):
    with ExitStack() as ctx:
        def sb(name, shape, dt=F32):
            return ctx.enter_context(nc.sbuf_tensor(name, shape, dt))

        def sem(name):
            return ctx.enter_context(nc.semaphore(name))

        def sb_twice(name, shape):
            at = -(-nc.sbuf_base // 32) * 32
            buf = sb(name, shape)
            return buf, nc.alloc_sbuf_tensor_at(name + "_r", shape, F32R, offset=at)

        ring, ring_r = sb_twice("ring", [P, SLOTS, SLAB])
        x = sb("x", [P, NT, D])
        xn = sb("xn", [P, NT, D])
        hT, hT_r = sb_twice("hT", [P, KC, S])
        proj = sb("proj", [P, NT, 6 * NB])
        mixT, mixT_r = sb_twice("mixT", [P, KC, S])
        work_at = -(-nc.sbuf_base // 32) * 32
        work, work_r = sb_twice("work", [P, 11776])
        ident = sb("ident", [P, P])
        cum = sb("cum", [P, 3, P])
        same = sb("same", [P, 2])
        ones = sb("ones", [P, P])
        cols = sb("cols", [P, NROWS])
        acol = sb("acol", [P, NADA])
        mod = sb("mod", [P, NADA])
        sel4 = sb("sel4", [P, 1])
        gain_a = sb("gain_a", [P, 4, KC])
        epsc = sb("epsc", [P, 1])
        scrap = sb("scrap", [P, 1])
        ss = sb("ss", [P, 64])
        rms = sb("rms", [P, 64])
        rstd = sb("rstd", [P, 64])
        zb = sb("zb", [P, NB], BF16)
        ps = [ctx.enter_context(nc.psum_tensor(f"bank{i}", [P, NB], F32)) for i in range(8)]

        def view(buf, at, *shape):
            n = math.prod(shape)
            flat = buf
            if len(buf.shape) == 3:
                flat = buf[:, :, :].rearrange("p a b -> p (a b)")
            else:
                flat = buf[:, :]
            v = flat[:, at:at + n]
            if len(shape) == 2:
                return v.rearrange("p (a b) -> p a b", b=shape[1])
            if len(shape) == 3:
                return v.rearrange("p (a b c) -> p a b c", b=shape[1], c=shape[2])
            return v

        rows = view(hT, 0, P)
        arow = view(hT, P, P)[0:NADA]
        hk = view(work, 0, NT, NB)
        lf = view(work, 1024, NT, NB)
        ex = view(work, 2048, 4, NT, NB)
        exT = view(work, 6144, 3, HA, S)
        scT = view(work, 9216, NT, NB)
        st = view(work, 10240, 3, NB)
        sq = view(work, 6144, NT, NB)
        lb_bc = view(mixT, 0, NB)
        lb1_bc = view(mixT, 512, NB)
        vg_bc = view(mixT, 1024, NB)
        wT = view(mixT, 1536, HA, P)
        ws = view(work, 8192, HA, P)
        decay = sb("decay", [P, 16])
        ada_row = view(xn, 0, 2, NB)
        crep = view(xn, 1024, KC, 32)
        xgT = view(work, 0, KC, 2 * BT)
        pick = view(work, 1024, NT, 2 * BT)
        pickw = view(work, 1280, NT, 2 * BT)
        pickT = view(work, 1536, NT * P)
        sg = view(work, 1792, FE)
        eh = view(work, 2304, FE)
        ehT = view(work, 2816, FE // P, 2 * BT)
        eo = view(work, 3328, D)
        fg_bc = view(work, 4352, D)
        lg = view(work, 5376, NT, NG + NE)
        goh = view(work, 5456, NT, NG)
        gtmp = view(work, 5464, NT, NG)
        em = view(work, 5472, NT, NE)
        oh1 = view(work, 5536, NT, NE)
        oh2 = view(work, 5600, NT, NE)
        chosen = view(work, 5728, NT, NE)
        cwt = view(work, 5792, NT, NE)
        pos1 = view(work, 5856, NT, NE)
        tot = view(work, 5920, NE)
        more = view(work, 5952, NE)
        upto_e = view(work, 5984, NE)
        before_e = view(work, 6016, NE)
        own = view(work, 6048, OVF, NE)
        otmp = view(work, 6304, OVF, NE)
        obase = view(work, 6560, OVF)
        oexp = view(work, 6568, OVF)
        sm = view(work, 6576, 16, NT)
        sqn = view(work, 0, NT, 1536)
        E = [view(work, at, 4, S) for at in (0, 1024, 9216)]
        pT = [[view(work, 2048 + 1024 * i + 512 * k, 4, P) for k in range(2)] for i in range(2)]
        qcT = view(work, 4096, QH // 2, S)
        qrT = hT
        kT = view(work, 6144, 2, GR, S)
        kz = view(work, 8192, 2, GR, S)
        pcT = view(work, 8192, 2, 4, P)
        csc = view(work, 10240, 2, NT, 8 * 16)
        hc = view(work, 10752, 2, GR * NCMP)
        vcm = view(work, 10880, GR, DH)
        kcm = view(work, 11136, DH)
        kcT = view(work, 11610, GR, 32)
        pc = view(work, 11264, 2)
        rt = view(work, 11266, 2, NT * RD)
        kk = view(work, 11298, 2, NT * RD)
        nm = view(work, 11330, 2, 4)
        sums = view(work, 11338, 2, 4)
        gl = view(work, 11346, NT, 3 * QH)
        cmx = view(work, 11442, 64)
        csum = view(work, 11506, 64)
        cadd = view(work, 11570, NT, 16)
        wgl = view(mixT, 0, KC, 3 * QH)
        w2c = view(mixT, 384, 2, DH)
        bgl = view(mixT, 512, 3 * QH)
        pe_sum = view(mixT, 1024, 2, P)
        pe_term = view(mixT, 1280, 2, P)
        qg = view(mixT, 560, DH)
        kg = view(mixT, 624, 3, DH)
        gbc = view(xn, 1024, D)
        rep = view(xn, 0, KC, P)
        dmask = cum[:, 2]
        cm01 = sb("cm01", [P, NT, 16])
        posi = sb("posi", [P, NT], I32)
        cossin = sb("cossin", [P, 2, NT * RD])
        inv = sb("inv", [P, RD])
        hid = [view(work, 1024 * i, 4, S) for i in range(2)]
        hid_lo = [view(work_r, 1024 * i, 4, S) for i in range(2)]
        hid_hi_r = [view(work_r, 2048 + 1024 * i, 4, S) for i in range(2)]
        h_hi_nsa = view(ring_r, SLAB, KC, S)
        h_hi_r = mixT_r
        dqT = [qcT, view(work, 6144, 8, S)]
        dsq = sqn
        lamv = view(work, 11346, 4, DH)
        dl = view(work, 11602, 8)
        wr = sb("wr", [P, KC, NG + NE])
        router_b = sb("router_b", [P, NG + NE])
        iota = sb("iota", [P, BT])
        iotai = sb("iotai", [P, BT], I32)
        desc = sb("desc", [P, NE])
        before = sb("before", [P, P])
        posb = sb("posb", [P, BLOCKS + 2, NT])
        cwb = sb("cwb", [P, BLOCKS + 2, NT])
        oexp_i = sb("oexp_i", [P, OVF + 1], I32)
        RMS_NORM = [1, 4, 5, 6, 10, 11, 15]

        x_in = sem("x_in")
        small_in = [sem(f"small_in{i}") for i in range(4)]
        landed = [sem(f"landed{i}") for i in range(SLOTS)]
        slabs_used = sem("slabs_used")
        const_ready = sem("const_ready")
        pool_step = sem("pool_step")
        dve_step = sem("dve_step")
        act_step = sem("act_step")
        sum_ready = sem("sum_ready")
        rms_ready = sem("rms_ready")
        x_ready = sem("x_ready")
        xn_ready = sem("xn_ready")
        xnT_psum = sem("xnT_psum")
        hT_dve = sem("hT_dve")
        hT_act = sem("hT_act")
        small_psum = sem("small_psum")
        cols_ready = sem("cols_ready")
        crep_ready = sem("crep_ready")
        half_psum = sem("half_psum")
        proj_act = sem("proj_act")
        proj_dve = sem("proj_dve")
        ada_rows = sem("ada_rows")
        ada_cols = sem("ada_cols")
        mod_ready = sem("mod_ready")
        done = sem("done")

        f_ready = sem("f_ready")
        lf_ready = sem("lf_ready")
        cum_psum = sem("cum_psum")
        lb_diff = sem("lb_diff")
        fg_in = sem("fg_in")
        lb_exp = sem("lb_exp")
        exT_dve = sem("exT_dve")
        pe_step = sem("pe_step")
        ex_act = sem("ex_act")
        ex_ready = sem("ex_ready")
        exT_psum = sem("exT_psum")
        exT_ready = sem("exT_ready")
        sc_psum = sem("sc_psum")
        sc_ready = sem("sc_ready")
        u_psum = sem("u_psum")
        st_ready = sem("st_ready")
        o_psum = sem("o_psum")
        osq_ready = sem("osq_ready")
        vh_ready = sem("vh_ready")
        mixed_psum = sem("mixed_psum")
        mixed_taken = sem("mixed_taken")
        ab_ready = sem("ab_ready")
        abT_psum = sem("abT_psum")
        mixT_dve = sem("mixT_dve")
        mixT_act = sem("mixT_act")

        logit_psum = sem("logit_psum")
        router_dve = sem("router_dve")
        router_act = sem("router_act")
        chosen_ready = sem("chosen_ready")
        pos_psum = sem("pos_psum")
        blocks_ready = sem("blocks_ready")
        overflow_ready = sem("overflow_ready")

        NSLOT = (2, 3, 4, 5, 0, 2)
        DSLOT = (4, 5, 0, 1, 2, 3)
        MSLOT = ((4, 5, 0, 1), (0, 1, 2, 3))
        HSLOT = ((2, 3), (4, 5))
        SPLIT = {"nsa_in": 0, "mlp0": 5, "diff_in": 5 + 16, "mlp1": 5 + 16 + 6}
        PHI = {"nsa_in": (7168, 3072), "diff_in": (6656, 2560)}
        high_places = {name: [nc.alloc_sbuf_tensor_at(f"high_{name}{k}", [P, SLAB], F32R, offset=work_at + 4 * at)
                              for k, at in enumerate(ats)] for name, ats in PHI.items()}
        cv1_in = sem("cv1_in")
        nsa_in_sem = sem("nsa_small_in")
        rope_dve = sem("rope_dve")
        rope_act = sem("rope_act")
        rep_ready = sem("rep_ready")
        gate_psum = sem("gate_psum")
        gate_ready = sem("gate_ready")
        gl_psum = sem("gl_psum")
        gl_dve = sem("gl_dve")
        gl_ready = sem("gl_ready")
        sq_act = sem("sq_act")
        rows_ready = sem("rows_ready")
        heads_psum = sem("heads_psum")
        heads_act = sem("heads_act")
        heads_dve = sem("heads_dve")
        kz_psum = sem("kz_psum")
        kz_act = sem("kz_act")
        kz_dve = sem("kz_dve")
        cmp_psum = sem("cmp_psum")
        pe_sum_ready = sem("pe_sum_ready")
        cmp_dve = sem("cmp_dve")
        cmp_act = sem("cmp_act")
        csc_psum = sem("csc_psum")
        cexp_dve = sem("cexp_dve")
        cexp_act = sem("cexp_act")
        cw_ready = sem("cw_ready")
        pcT_psum = sem("pcT_psum")
        pcT_ready = sem("pcT_ready")
        sc2_psum = sem("sc2_psum")
        nm_ready = sem("nm_ready")
        e_ready = sem("e_ready")
        p_ready = sem("p_ready")
        pT_psum = sem("pT_psum")
        pT_act = sem("pT_act")
        pT_dve = sem("pT_dve")
        ot_psum = sem("ot_psum")
        ot_ready = sem("ot_ready")
        hid_ready = sem("hid_ready")
        hid_hi_ready = sem("hid_hi_ready")
        sq_ready = sem("sq_ready")
        hi_ready = sem("hi_ready")
        lo_ready = sem("lo_ready")
        h_hi_ready = sem("h_hi_ready")
        h_lo_ready = sem("h_lo_ready")
        relu_ready = sem("relu_ready")
        diff_in_sem = sem("diff_small_in")
        res = view(work, 4096, 2, NT, NB)
        dgain = view(work, 11610, 2, DH)
        lam_dve = sem("lam_dve")
        lam_act = sem("lam_act")
        orow_ready = sem("orow_ready")

        class Pairs:

            def __init__(self, tag, used, used0, landed, landed0, block0):
                self.used, self.used0, self.landed, self.landed0 = used, used0, landed, landed0
                self.block0 = block0
                self.pick_ready = sem(tag + "_pick_ready")
                self.pickw_ready = sem(tag + "_pickw_ready")
                self.gathered = sem(tag + "_gathered")
                self.xg_ready = sem(tag + "_xg_ready")
                self.sg_ready = sem(tag + "_sg_ready")
                self.h_ready = sem(tag + "_h_ready")
                self.hT_psum = sem(tag + "_hT_psum")
                self.hT_ready = sem(tag + "_hT_ready")
                self.pickT_psum = sem(tag + "_pickT_psum")
                self.pickT_ready = sem(tag + "_pickT_ready")
                self.down = sem(tag + "_down")
                self.o_act = sem(tag + "_o_act")
                self.o_dve = sem(tag + "_o_dve")
                self.scattered = sem(tag + "_scattered")

            def wait_used(self, eng, q, k):
                eng.wait_ge(self.used, q * 6 + (self.used0 + k))

            def wait_landed(self, eng, q, k):
                eng.wait_ge(self.landed[k], q * 16 + (self.landed0[k] + 16))

        def ring_at(name):
            w = Ring()
            for at, slots, rounds in (("", range(SLOTS), 5), ("", range(2), 1), ("", ESLOT, PAIRS),
                                      ("nsa_in", NSLOT, 1), ("", NSLOT[0:2], 1), ("mlp0", MSLOT[0], 4),
                                      ("diff_in", DSLOT, 1), ("", DSLOT[0:2], 1), ("mlp1", (), 0)):
                if at == name:
                    return w.loads
                w.skip(slots, rounds)

        def high_place(name, k):
            return high_places[name][k % 2][:, :]

        def wait_mlp_slab(eng, l, i, n):
            slot = MSLOT[l][n % 4]
            eng.wait_ge(landed[slot], i * 16 + 16 * (ring_at(f"mlp{l}")[slot] + 1 + n // 4))

        def wait_mlp_used(eng, l, i, n):
            eng.wait_ge(slabs_used, i * 4 + (SLABS[f"mlp{l}"] + n + 1))

        walk = Ring()
        walk.skip(range(SLOTS), 5)
        walk.skip(range(2), 1)
        ESLOT = (2, 3, 4, 5, 0, 1)
        main = Pairs("main", slabs_used, SLABS["experts"], [landed[s] for s in ESLOT],
                     [16 * walk.loads[s] for s in ESLOT], 0)
        ovf = Pairs("ovf", sem("ovf_used"), 0, [sem(f"ovf_landed{k}") for k in range(6)], [0] * 6, NE)

        NU = 2 * NT * GR
        NUD = 4 * NT
        OBANK = (5, 0)
        MIXBANK = (4, 5, 2, 3)

        block = ctx.enter_context(nc.Block())

        def heads(buf, per, first, n):
            return buf[:, 0:NT * per].rearrange("p (t h) -> p t h", t=NT)[:, :, first:first + n]

        def any_overflow(eng):
            eng.wait_ge(overflow_ready, 1)
            return eng.value_load(oexp_i[0:1, OVF:OVF + 1], min_val=0, max_val=OVF)

        def bank_done(eng, name, s, t, half):
            if t == 0:
                eng.wait_ge(half_psum, half + 1)
            else:
                eng.wait_ge(slabs_used, (in_slab(s) if name == "w_in" else SLABS[name] + s) + 1)

        def k_slab(w, n0):
            return w.rearrange("(c p) n -> p c n", p=P)[:, :, n0:n0 + NB]

        def slab(slot):
            return ring[:, slot].rearrange("p (c n) -> p c n", n=NB)

        @block.sync
        def _(sp):
            r = Ring()

            def load(slot, src, dst=None):
                free, _ = r.take(slot)
                if free > 0:
                    sp.wait_ge(slabs_used, free)
                sp.dma_start(slab(slot) if dst is None else dst, src).then_inc(landed[slot], 16)

            sp.dma_start(x[:, :, :], d["x"].rearrange("(t p) n -> p t n", p=P)).then_inc(x_in, 16)
            sp.wait_ge(small_in[0], 16 * 11)
            sp.wait_ge(small_in[2], 16)
            win_j = d["w_in"].rearrange("(c p) (j n) -> j p c n", p=P, n=NB)
            ada_ls = d["w_ada_2"].rearrange("l (c p) (s n) -> l s p c n", p=P, n=NB)

            def mixed_slab(i, k):
                if k % 3 == 1:
                    return win_j[bass.ds(i * 2 + k // 3, 1)].rearrange("j p c n -> (j p) c n")
                return ada_ls[0, bass.ds(i * 4 + 2 * (k // 3) + (k % 3) // 2, 1)].rearrange("s p c n -> (s p) c n")

            for k in (1, 0, 2, 4, 3, 5):
                sp.dma_start(slab(k), mixed_slab(0, k)).then_inc(landed[k], 16)
            for first, last in ((1, 3), (3, 5)):
                with sp.Fori(first, last) as i:
                    for k in range(6):
                        sp.wait_ge(slabs_used, i * 6 + (k - 5))
                        if first == 1:
                            src = mixed_slab(i, k)
                        else:
                            src = ada_ls[1, bass.ds(i * 6 + (k - 18), 1)].rearrange("s p c n -> (s p) c n")
                        sp.dma_start(slab(k), src).then_inc(landed[k], 16)
            r.skip(range(6), 5)
            for s in range(2):
                load(s, k_slab(d["w_out"], s * NB))

            def mlp_load(l):
                slots = MSLOT[l]
                win = d["w_mlp_in_2"][l].rearrange("(c p) (j n) -> j p c n", p=P, n=NB)
                wout = d["w_mlp_out_2"][l].rearrange("(j c p) n -> j p c n", p=P, c=NB // P)

                def one(n, j, second):
                    w = wout if second else win
                    dst = ring[:, slots[n % 4]].rearrange("p (c n) -> p c n", n=D if second else NB)
                    return dst, w[bass.ds(j, 1)].rearrange("j p c n -> (j p) c n")

                def fixed(n):
                    k, second = ((n + 1) // 2, n % 2 == 0) if 0 < n < 15 else (0 if n == 0 else 8, n == 15)
                    dst, src = one(n, k - 1 if second else k, second)
                    load(slots[n % 4], src, dst)

                for n in range(4):
                    fixed(n)
                n0 = r.n - 4
                with sp.Fori(1, 3) as i:
                    for m in range(4):
                        dst, src = one(m, i * 2 + (-1, 1, 0, 2)[m], m % 2 == 0)
                        sp.wait_ge(slabs_used, i * 4 + (n0 + m - 3))
                        sp.dma_start(dst, src).then_inc(landed[slots[m]], 16)
                r.skip(slots, 2)
                for n in range(12, 16):
                    fixed(n)
                for k in range(2):
                    r.last[HSLOT[l][k]] = r.n - 1 + k

            def expert(w, e, k, halves):
                return (w[bass.ds(e, 1)].rearrange("e (c p) n -> (e p) c n", p=P),
                        ring[:, ESLOT[k]].rearrange("p (c n) -> p c n", n=halves * NB))

            PARTS = ((d["w_gate"], 1), (d["w_up"], 1), (d["w_down"], 2))
            for k in range(6):
                src, dst = expert(PARTS[k // 2][0], k % 2, k, PARTS[k // 2][1])
                load(ESLOT[k], src, dst)
            with sp.Fori(1, PAIRS) as q:
                for k in range(6):
                    src, dst = expert(PARTS[k // 2][0], q * 2 + k % 2, k, PARTS[k // 2][1])
                    main.wait_used(sp, q - 1, k + 1)
                    sp.dma_start(dst, src).then_inc(main.landed[k], 16)
            r.skip(ESLOT, PAIRS - 1)
            with sp.If(any_overflow(sp) > 0):
                for q in range(OVF_PAIRS):
                    e = [sp.value_load(oexp_i[0:1, 2 * q + k:2 * q + k + 1], min_val=0, max_val=NE - 1) for k in range(2)]
                    for k in range(6):
                        src, dst = expert(PARTS[k // 2][0], e[k % 2], k, PARTS[k // 2][1])
                        if q == 0:
                            main.wait_used(sp, PAIRS - 1, k + 1)
                        else:
                            ovf.wait_used(sp, q - 1, k + 1)
                        sp.dma_start(dst, src).then_inc(ovf.landed[k], 16)
                ovf.wait_used(sp, OVF_PAIRS - 1, 6)
            for s in range(5):
                load(NSLOT[s], k_slab(d["nsa_w_in_2"], s * NB))
            r.last[1] = r.n
            cmp_w = ring[:, NSLOT[5]].rearrange("p (w j m) -> p w j m", w=2, m=P)
            load(NSLOT[5], d["nsa_w_ck1_2"].rearrange("(j p) m -> p j m", p=P), cmp_w[:, 0])
            sp.dma_start(cmp_w[:, 1], d["nsa_w_cv1_2"].rearrange("(j p) m -> p j m", p=P)).then_inc(cv1_in, 16)
            for s in range(2):
                load(NSLOT[s], k_slab(d["nsa_w_out_2"], s * NB))
            mlp_load(0)
            for s in range(6):
                load(DSLOT[s], k_slab(d["diff_w_in_2"], s * NB))
            for s in range(2):
                load(DSLOT[s], k_slab(d["diff_w_out_2"], s * NB))
            mlp_load(1)
            sp.wait_ge(x_ready, 28)
            sp.dma_start(out.rearrange("(t p) n -> p t n", p=P), x[:, :, :]).then_inc(done, 16)
            sp.wait_ge(done, 16)

        @block.gpsimd
        def _(pool):
            step = Steps(pool, pool_step)
            step.sig(pool.memset(ident[:, :], 0.0))
            step.sig(pool.memset(cum[:, :, :], 1.0))
            step.sig(pool.memset(same[:, :], 0.0))
            step.sig(pool.memset(sel4[:, :], 0.0))
            step.sig(pool.memset(ones[:, :], 1.0))
            step.sig(pool.memset(epsc[:, :], EPS))
            step.sig(pool.memset(before[:, :], 1.0))
            step.sig(pool.memset(cm01[:, :, :], 1.0))
            for i in range(RD):
                step.sig(pool.memset(inv[:, i:i + 1], float(np.float32(THETA) ** np.float32(-i / RD))))
            step.sig(pool.memset(posb[:, :, :], -1.0))
            step.sig(pool.memset(cwb[:, :, :], 0.0))
            step.then(pool.memset(zb[:, :], 0.0))

            def keep(ap, base, pattern, cm, fill, op=ALU.is_ge):
                step.then(pool.affine_select(out=ap, in_=ap, compare_op=op, fill=fill, base=base,
                                             pattern=pattern, channel_multiplier=cm))

            keep(ident[:, :], 0, [[-1, P]], 1, 1.0, ALU.not_equal)
            for h in range(2):
                a = slice(CH * h, CH * h + CH)
                if h == 0:
                    keep(same[:, 0:1], -CH, [[0, 1]], 1, 1.0)
                else:
                    keep(same[:, 1:2], CH - 1, [[0, 1]], -1, 1.0)
                keep(cum[:, 0, a], CH * h, [[1, CH]], -1, 0.0)
                keep(cum[:, 0, a], -CH * h, [[0, CH]], 1, 0.0)
                keep(cum[:, 2, a], -CH * h - 1, [[-1, CH]], 1, 0.0)
                keep(cum[:, 2, a], CH * h + CH - 1, [[0, CH]], -1, 0.0)
                keep(cum[:, 1, a], CH * h + CH // 2 - 1, [[0, CH]], -1, 0.0)
                keep(cum[:, 1, a], -CH * h, [[0, CH]], 1, 0.0)
            for j in range(4):
                keep(sel4[:, :], -32 * j, [[0, 1]], 1, 1.0, ALU.not_equal)
            keep(before[:, :], -1, [[1, P]], -1, 0.0)
            for t in range(NT):
                keep(cm01[:, t], t * P - 31, [[-16, 16]], 1, 0.0)
            step.sig(pool.iota(iotai[:, :], pattern=[[1, BT]], base=0, channel_multiplier=0))
            step.then(pool.tensor_tensor(cum[:, 1], cum[:, 0], cum[:, 1], ALU.subtract))
            pool.sem_inc(const_ready, 1)
            pool.wait_ge(cols_ready, 1)
            pool.wait_ge(landed[NSLOT[5]], 16 * (ring_at("nsa_in")[NSLOT[5]] + 2))
            pool.wait_ge(cv1_in, 16)
            cw1 = ring[:, NSLOT[5]].rearrange("p (w j m) -> p w j m", w=2, m=P)
            for j in range(16):
                for w in range(2):
                    pcol = ROWS["pe_v" if w else "pe_k"] + j
                    dst = pe_term if j else pe_sum
                    step.sig(pool.tensor_scalar(dst[:, w], cw1[:, w, j], cols[:, pcol:pcol + 1], None, ALU.mult))
                pool.wait_ge(pool_step, step.n)
                if j:
                    step.then(pool.tensor_tensor(pe_sum, pe_sum, pe_term, ALU.add))
            pool.sem_inc(pe_sum_ready, 1)

        @block.scalar
        def _(act):
            step = Steps(act, act_step)
            bc = lambda ap, n: ap.rearrange("(a n) -> a n", a=1).broadcast_to([P, n])

            def small(name, src):
                act.dma_start(rows[ROWS[name]:ROWS[name] + src.shape[0], :], src).then_inc(small_in[0], 16)

            def rowsof(ap, n):
                return ap.rearrange("(r q) -> r q", q=P)

            small("norm1", rowsof(d["norm1_gain"], 8))
            small("norm2", rowsof(d["norm2_gain"], 8))
            small("mix", rowsof(d["ln_mix_g_2"].rearrange("l n -> (l n)"), 16))
            small("mlp", rowsof(d["ln_mlp_g_2"].rearrange("l n -> (l n)"), 16))
            small("hgain", rowsof(d["hgrn_out_gain"], 4))
            small("bs", d["gmlp_b_s"])
            small("subln", rowsof(d["diff_subln_g_2"], 1))
            small("pe_k", rowsof(d["nsa_pe_k_2"].rearrange("l n -> (l n)"), 16))
            small("pe_v", rowsof(d["nsa_pe_v_2"].rearrange("l n -> (l n)"), 16))
            small("c", rowsof(d["c_2"], 8))
            act.dma_start(arow[:, :], rowsof(d["b_ada_2"].rearrange("l n -> (l n)"), NADA)).then_inc(small_in[0], 16)
            act.dma_start(lb_bc, bc(d["hgrn_lower_bounds"][0], NB)).then_inc(small_in[1], 16)
            act.dma_start(lb1_bc, bc(d["hgrn_lower_bounds"][1], NB)).then_inc(small_in[1], 16)
            act.dma_start(vg_bc, bc(d["gmlp_v_gain"], NB)).then_inc(small_in[1], 16)
            act.dma_start(ws, d["gmlp_w_s"].rearrange("g i j -> i g j")).then_inc(small_in[2], 16)

            act.dma_start(wr[:, :, 0:NG], d["w_group_router"].rearrange("(c p) n -> p c n", p=P)).then_inc(small_in[3], 16)
            act.dma_start(wr[:, :, NG:], d["w_expert_router"].rearrange("(c p) n -> p c n", p=P)).then_inc(small_in[3], 16)
            act.dma_start(router_b[:, 0:NG], bc(d["b_group_router"], NG)).then_inc(small_in[3], 16)
            act.dma_start(router_b[:, NG:], bc(d["b_expert_router"], NE)).then_inc(small_in[3], 16)

            def norm(i):
                act.activation(scrap[:, :], epsc[:, :], ACT.Sqrt)
                for t in range(NT):
                    early = 1 if i in (3, 5) and t == 0 else 0
                    act.wait_ge(x_ready, 4 * i - 1 + t - early) if i else act.wait_ge(x_in, 16)
                    step.sig(act.activation(xn[:, t], x[:, t], ACT.Square, accum_out=ss[:, t:t + 1]))
                act.wait_ge(act_step, step.n)
                act.activation(rms[:, 0:NT], ss[:, 0:NT], ACT.Sqrt, bias=epsc[:, 0:1], scale=1.0 / D).then_inc(rms_ready, 1)

            def norm_out(i, gain, bias=None):
                for c in range(4, KC):
                    if c % 2 == 0:
                        act.wait_ge(xnT_psum, 4 * i + (2 if c == 4 else 4))
                    kw = {} if bias is None else {"bias": bias(c)}
                    act.activation(hT[:, c], ps[4 + c // 2][:, (c % 2) * S:(c % 2) * S + S], ACT.Identity,
                                   scale=gain(c), **kw).then_inc(hT_act, 1)

            act.wait_ge(const_ready, 1)
            norm(0)
            act.wait_ge(cols_ready, 1)
            norm_out(0, lambda c: cols[:, ROWS["norm1"] + c:ROWS["norm1"] + c + 1])
            step.then(act.activation(crep[:, :, 0], cols[:, ROWS["c"]:ROWS["c"] + KC], ACT.Silu))
            for c in range(KC):
                act.activation(crep[:, c, 1:32], ones[:, 0:31], ACT.Copy, scale=crep[:, c, 0:1]).then_inc(crep_ready, 1)
            act.wait_ge(lb_diff, 1)
            act.activation(lb_bc, lb_bc, ACT.Exp).then_inc(lb_exp, 1)


            def ada_out(first, last):
                for n in range(first, last):
                    act.wait_ge(slabs_used, ada_slab(n) + 1)
                    if n >= 2:
                        act.wait_ge(ada_cols, n - 1)
                    act.activation(ada_row[:, n % 2], ps[7][:, :], ACT.Copy).then_inc(ada_rows, 1)

            for s, f in enumerate((ACT.Gelu, ACT.Gelu, ACT.Silu, ACT.Sigmoid, None, ACT.Silu)):
                for t in range(NT):
                    if f is not None:
                        bank_done(act, "w_in", s, t, s)
                        act.activation(proj[:, t, s * NB:(s + 1) * NB], ps[(s % 2) * 2 + t][:, :], f).then_inc(proj_act, 1)
                    ada_out(2 * s + t, 2 * s + t + 1)
            act.wait_ge(f_ready, 1)
            act.activation(lf, proj[:, :, 3 * NB:4 * NB], ACT.Ln).then_inc(lf_ready, 1)
            act.wait_ge(sum_ready, 1)
            act.activation(rms[:, 0:8], ss[:, 0:8], ACT.Sqrt, bias=epsc[:, 0:1], scale=1.0 / P).then_inc(rms_ready, 1)
            ada_out(12, 14)
            act.wait_ge(cum_psum, 1)
            for t in range(NT):
                for j, (m, sc) in enumerate(((1, 1.0), (1, -1.0), (0, 1.0), (2, 1.0))):
                    act.activation(ex[:, j, t], ps[3 * t + m][:, :], ACT.Exp, scale=sc).then_inc(ex_act, 1)
            ada_out(14, 16)
            act.wait_ge(cum_psum, 2)
            act.activation(decay[:, :], ps[0][:, 0:16], ACT.Exp).then_inc(ex_act, 1)
            for j in range(3):
                act.wait_ge(exT_psum, 2 * j + 2)
                act.activation(exT[:, j, :, P:2 * P], ps[2 * j + 1][:, :].rearrange("p (h c) -> p h c", h=HA),
                               ACT.Copy).then_inc(exT_ready, 1)
            ada_out(16, 20)
            act.wait_ge(o_psum, 1)
            for t in range(NT):
                act.activation(sq[:, t], ps[OBANK[t]][:, :], ACT.Square).then_inc(osq_ready, 1)
            ada_out(20, 21)
            act.wait_ge(sum_ready, 2)
            act.activation(rms[:, 0:8], ss[:, 0:8], ACT.Sqrt, bias=epsc[:, 0:1], scale=1.0 / P).then_inc(rms_ready, 1)
            ada_out(21, 24)
            for c in range(4, KC):
                act.wait_ge(abT_psum, c // 2 + 1)
                act.activation(mixT[:, c], ps[c // 2][:, (c % 2) * S:(c % 2) * S + S], ACT.Copy,
                               scale=cols[:, ROWS["hgain"] + c - 4:ROWS["hgain"] + c - 3]).then_inc(mixT_act, 1)
            norm(1)
            def mid(name, dst, src, **kw):
                act.dma_start(dst, src, **kw).then_inc(nsa_in_sem, 16)

            mid("gate weights", wgl, d["nsa_w_in_2"].rearrange("(c p) n -> p c n", p=P)[:, :, 5 * NB:])
            mid("ck2", w2c[:, 0], d["nsa_w_ck2_2"])
            mid("cv2", w2c[:, 1], d["nsa_w_cv2_2"])
            mid("gate bias", bgl, bc(d["nsa_b_gate_2"], 3 * QH))
            mid("q gain", qg, bc(d["nsa_q_gain_2"], DH))
            for k in range(3):
                mid("k gain", kg[:, k], bc(d["nsa_k_gain_2"][k], DH))
            mid("positions", posi[:, :], d["positions_2"].rearrange("(t p) -> p t", p=P), allow_slow_non_contiguous=True)
            act.dma_start(fg_bc, bc(d["final_gain"], D)).then_inc(fg_in, 16)
            norm_out(1, lambda c: cols[:, ROWS["norm2"] + c:ROWS["norm2"] + c + 1])
            act.wait_ge(router_dve, 1)
            act.activation(gtmp, gtmp, ACT.Exp).then_inc(router_act, 1)
            act.wait_ge(router_dve, 2)
            act.activation(sm[:, 2], sm[:, 2], ACT.Exp).then_inc(router_act, 1)

            def pair(m, q):
                m.wait_used(act, q, 4)
                act.activation(sg, ps[4][:, :], ACT.Silu).then_inc(m.sg_ready, 1)
                act.wait_ge(m.hT_psum, q + 1)
                act.activation(ehT, ps[6][:, :].rearrange("p (c s) -> p c s", c=FE // P), ACT.Copy).then_inc(m.hT_ready, 1)
                act.wait_ge(m.down, q + 1)
                act.activation(eo[:, 0:NB], ps[4][:, :], ACT.Copy).then_inc(m.o_act, 1)

            def pairs(m, n):
                act.sem_inc(m.hT_ready, 1)
                act.sem_inc(m.o_act, 1)
                with act.Fori(0, n) as q:
                    pair(m, q)

            pairs(main, PAIRS)
            with act.If(any_overflow(act) > 0):
                pairs(ovf, OVF_PAIRS)

            def high_in(name, k, slots):
                slot = slots[k]
                act.wait_ge(landed[slot], 16 * (ring_at(name)[slot] + 1))
                if k >= 2:
                    act.wait_ge(slabs_used, SLABS[name] + k - 1)
                act.activation(high_place(name, k), ring[:, slot], ACT.Copy).then_inc(hi_ready, 1)

            def high_h(j, dst):
                act.wait_ge(hT_act, 4 * (3 + j))
                act.activation(dst[:, 4:KC], hT[:, 4:KC], ACT.Copy).then_inc(h_hi_ready, 1)

            high_in("nsa_in", 0, NSLOT)
            norm(2)


            def norm2(i, j, l, which):
                norm(i)
                norm_out(j, lambda c: gain_a[:, 2 * l + which, c:c + 1],
                         lambda c: mod[:, (l * 6 + 3 * which) * KC + c:(l * 6 + 3 * which) * KC + c + 1])

            def gate_rows(k, bank):
                act.wait_ge(gate_psum, k + 1)
                for n in range(2):
                    act.activation(gbc[:, n * NB:n * NB + NB], ps[bank + n][:, :], ACT.Copy).then_inc(gate_ready, 1)

            def projections(name, half, parts):
                for s in parts:
                    for t in range(NT):
                        src = ps[(s % 2) * 2 + t]
                        bank_done(act, name, s, t, half + s)
                        w, at = parts[s]
                        if w:
                            step.sig(act.activation(sqn[:, t, at:at + w], src[:, 0:w], ACT.Square))
                        act.activation(proj[:, t, s * NB:(s + 1) * NB], src[:, :], ACT.Copy).then_inc(proj_act, 1)

            def unit_exp(u, nk):
                act.wait_ge(nm_ready, u + 1)
                for i in range(4):
                    src = ps[2 * (u % 2) + i // 2][:, (i % 2) * S:(i % 2) * S + nk]
                    act.activation(E[u % 3][:, i, 0:nk], src, ACT.Exp, bias=nm[:, u % 2, i:i + 1], scale=SCALE,
                                   accum_out=sums[:, u % 2, i:i + 1]).then_inc(e_ready, 1)

            def head_roots(k, per, first, n):
                act.wait_ge(sum_ready, k)
                act.activation(heads(rms, per, first, n), heads(ss, per, first, n), ACT.Sqrt, bias=epsc[:, 0:1],
                               scale=1.0 / DH).then_inc(rms_ready, 1)

            norm2(3, 2, 0, 0)
            high_h(0, h_hi_nsa)
            high_in("nsa_in", 1, NSLOT)
            projections("nsa_in", 8, {0: (512, 0)})
            high_in("nsa_in", 2, NSLOT)
            gate_rows(0, 4)
            projections("nsa_in", 8, {1: (512, 512)})
            high_in("nsa_in", 3, NSLOT)
            head_roots(3, 24, 0, QH)
            act.wait_ge(rope_dve, 1)
            act.activation(cossin[:, :, :], rt, ACT.Sin).then_inc(rope_act, 1)
            high_in("nsa_in", 4, NSLOT)
            projections("nsa_in", 8, {3: (256, 1024), 4: (256, 1280)})
            act.wait_ge(gl_dve, 1)
            act.activation(gl, gl, ACT.Sigmoid).then_inc(gl_ready, 1)
            head_roots(4, 24, QH, 2 * GR)
            for gp in range(2):
                act.wait_ge(kz_psum, gp + 1)
                for o in range(2):
                    src = ps[gp][DH * o:DH * o + DH, 0:S]
                    act.activation(kz[0:DH, 0, 2 * gp + o], src, ACT.Copy).then_inc(kz_act, 1)
                    act.activation(kz[DH:P, 0, 2 * gp + o, 0:S - 1], src[:, 1:S], ACT.Copy).then_inc(kz_act, 1)
            act.wait_ge(heads_psum, 1)
            for k in range(2):
                act.activation(qcT[:, 4 * k:4 * k + 4, 0:P], ps[k][:, :].rearrange("p (h q) -> p h q", h=4), ACT.Copy).then_inc(heads_act, 1)
            for w in range(2):
                act.wait_ge(cmp_psum, w + 1)
                step.then(act.activation(pc[:, w:w + 1], ps[4 + w][:, 64:65], ACT.Copy))
                act.activation(hc[:, w], ps[4 + w][:, 0:GR * NCMP], ACT.Silu, bias=pc[:, w:w + 1]).then_inc(cmp_act, 1)
            act.wait_ge(heads_psum, 3)
            for t in range(NT):
                for o in range(2):
                    act.activation(kT[DH * o:DH * o + DH, 0, :, t * P:t * P + P],
                                   ps[t][0:DH, :].rearrange("p (g q) -> p g q", g=GR), ACT.Copy).then_inc(heads_act, 1)
            act.wait_ge(cmp_psum, 3)
            act.activation(kcm[0:GR * NCMP], ps[6][0:GR * NCMP, 0:DH], ACT.Square, accum_out=ss[0:GR * NCMP, 48:49]).then_inc(cmp_act, 1)
            act.wait_ge(cmp_act, 3)
            act.activation(rms[0:GR * NCMP, 48:49], ss[0:GR * NCMP, 48:49], ACT.Sqrt, bias=epsc[0:GR * NCMP, 0:1], scale=1.0 / DH).then_inc(rms_ready, 1)
            act.wait_ge(heads_psum, 5)
            for k in range(2):
                act.activation(qrT[:, 4 * k:4 * k + 4, 0:P], ps[k][:, :].rearrange("p (h q) -> p h q", h=4), ACT.Copy).then_inc(heads_act, 1)

            for i in range(NU + 4):
                if i < NU:
                    if i >= 3:
                        act.wait_ge(pT_psum, i - 2)
                    unit_exp(i, (i // 8 + 1) * P)
                u = i - 2
                if 0 <= u < NU:
                    n = u // 2
                    if u % 2:
                        act.wait_ge(pcT_psum, n + 1)
                        act.activation(pcT[0:NCMP, n % 2], ps[7][0:NCMP, :].rearrange("p (h q) -> p h q", h=4), ACT.Copy).then_inc(pcT_ready, 1)
                    act.wait_ge(pT_psum, u + 1)
                    act.activation(pT[u % 2][0], ps[4][:, :].rearrange("p (h q) -> p h q", h=4), ACT.Copy).then_inc(pT_act, 1)
                if i == 2:
                    act.wait_ge(cexp_dve, 1)
                    act.activation(csc, csc, ACT.Exp).then_inc(cexp_act, 1)
                u = i - 4
                if u >= 0 and u % 2:
                    n = u // 2
                    t, g = n // GR, n % GR
                    act.wait_ge(ot_psum, n + 1)
                    act.activation(mixT[:, 2 * g:2 * g + 2, t * P:t * P + P], ps[6][:, 0:S].rearrange("p (j q) -> p j q", j=2),
                                   ACT.Copy).then_inc(ot_ready, 1)

            def high(l, i, n):
                src = MSLOT[l][n % 4]
                wait_mlp_slab(act, l, i, n)
                if isinstance(i, int) and i * 4 + n < 2:
                    act.wait_ge(slabs_used, SLABS[f"mlp{l}"] - 1 + n)
                else:
                    wait_mlp_used(act, l, i, n - 2)
                act.activation(ring_r[:, HSLOT[l][n % 2]], ring[:, src], ACT.Copy).then_inc(hi_ready, 1)

            def mlp(l):
                high(l, 0, 0)
                norm2(4 + 2 * l, 3 + 2 * l, l, 1)
                high_h(1 + 2 * l, h_hi_r)
                high(l, 0, 1)

                def relu2(k, par, first=0):
                    for n in range(2):
                        act.wait_ge(slabs_used, k * 2 + (SLABS[f"mlp{l}"] + first))
                        o = hid[par][:, 2 * n:2 * n + 2]
                        act.activation(o, ps[4 + n][:, :].rearrange("p (m q) -> p m q", m=2), ACT.Relu).then_inc(relu_ready, 1)
                        act.wait_ge(relu_ready, k * 2 + (l * 2 * MC + n + 1))
                        act.activation(o, o, ACT.Square).then_inc(sq_ready, 1)

                relu2(0, 0, 1)
                high(l, 0, 2)
                gate_rows(1 + 2 * l, 6)
                if l == 0:
                    for k, name in enumerate(("diff_lq1_2", "diff_lk1_2", "diff_lq2_2", "diff_lk2_2")):
                        act.dma_start(lamv[:, k], bc(d[name], DH)).then_inc(diff_in_sem, 16)
                    for k, name in enumerate(("diff_q_gain_2", "diff_k_gain_2")):
                        act.dma_start(dgain[:, k], bc(d[name], DH)).then_inc(diff_in_sem, 16)
                with act.Fori(0, 3) as i:
                    relu2(i * 2 + 1, 1)
                    high(l, i, 3)
                    high(l, i, 4)
                    relu2(i * 2 + 2, 0)
                    high(l, i, 5)
                    high(l, i, 6)
                relu2(7, 1)
                high(l, 3, 3)

            mlp(0)
            high_in("diff_in", 0, DSLOT)
            norm2(5, 4, 1, 0)
            high_h(2, h_hi_r)
            high_in("diff_in", 1, DSLOT)
            projections("diff_in", 15, {0: (512, 0)})
            high_in("diff_in", 2, DSLOT)
            gate_rows(2, 4)
            act.wait_ge(lam_dve, 1)
            act.activation(lamv[:, 0, 0:2], lamv[:, 0, 0:2], ACT.Exp).then_inc(lam_act, 1)
            projections("diff_in", 15, {1: (512, 512)})
            high_in("diff_in", 3, DSLOT)
            head_roots(5, 32, 0, QH)
            for s in (2, 3):
                for t in range(NT):
                    src = ps[(s % 2) * 2 + t]
                    bank_done(act, "diff_in", s, t, 15 + s)
                    step.sig(act.activation(dsq[:, t, (s - 2) * NB:(s - 1) * NB], src[:, :], ACT.Square))
                    act.activation(proj[:, t, s * NB:(s + 1) * NB], src[:, :], ACT.Copy).then_inc(proj_act, 1)
                high_in("diff_in", s + 2, DSLOT)
            head_roots(6, 32, QH, QH)
            for w in range(2):
                act.wait_ge(heads_psum, 7 + 2 * w)
                for k in range(2):
                    act.activation(dqT[w][:, 4 * k:4 * k + 4, 0:P], ps[4 * w + k][:, :].rearrange("p (h q) -> p h q", h=4), ACT.Copy).then_inc(heads_act, 1)
            for i in range(NUD + 4):
                if i < NUD:
                    if i >= 3:
                        act.wait_ge(pT_psum, NU + i - 2)
                    unit_exp(NU + i, (i // 4 + 1) * P)
                u = i - 2
                if 0 <= u < NUD:
                    nk = (u // 4 + 1) * P
                    act.wait_ge(pT_psum, NU + u + 1)
                    act.activation(pT[u % 2][0][:, 0:2 * (u // 4 + 1)], ps[4 + u % 2][:, 0:2 * nk].rearrange("p (h q) -> p h q", q=P),
                                   ACT.Copy).then_inc(pT_act, 1)
                u = i - 4
                if u >= 0:
                    t = u // 4
                    act.wait_ge(ot_psum, 8 + u + 1)
                    act.activation(proj[:, t, (u % 4) * S:(u % 4) * S + S], ps[6 + u % 2][:, 0:S], ACT.Copy).then_inc(ot_ready, 1)
            act.wait_ge(ot_ready, 16)
            for t in range(NT):
                act.activation(work[:, t * D:(t + 1) * D], proj[:, t, 0:D], ACT.Square).then_inc(sq_act, 1)
            act.wait_ge(sum_ready, 7)
            act.activation(rms[:, 0:16], ss[:, 0:16], ACT.Sqrt, bias=epsc[:, 0:1], scale=1.0 / P).then_inc(rms_ready, 1)
            act.wait_ge(abT_psum, 8)
            for c in range(4, KC):
                act.activation(mixT[:, c], ps[c // 2][:, (c % 2) * S:(c % 2) * S + S], ACT.Copy, scale=lamv[:, 1, 0:1]).then_inc(mixT_act, 1)
            mlp(1)

        @block.vector
        def _(v):
            step = Steps(v, dve_step)

            def norm(i):
                v.wait_ge(rms_ready, RMS_NORM[i])
                step.then(v.reciprocal(rstd[:, 0:NT], rms[:, 0:NT]))
                for t in range(NT):
                    v.tensor_scalar(xn[:, t], x[:, t], rstd[:, t:t + 1], None, ALU.mult).then_inc(xn_ready, 1)

            def norm_out(i, gain, bias=None):
                for c in range(0, 4):
                    if c % 2 == 0:
                        v.wait_ge(xnT_psum, 4 * i + (1 if c == 0 else 3))
                    src = ps[4 + c // 2][:, (c % 2) * S:(c % 2) * S + S]
                    if bias is None:
                        ins = v.tensor_scalar(hT[:, c], src, gain(c), None, ALU.mult)
                    else:
                        ins = v.tensor_scalar(hT[:, c], src, gain(c), bias(c), ALU.mult, ALU.add)
                    ins.then_inc(hT_dve, 1)

            def head_sums(sq3, n):
                for t in range(NT):
                    step.sig(v.tensor_reduce(ss[:, n * t:n * t + n], sq3[:, t].rearrange("p (h e) -> p h e", e=P), AX, ALU.add))

            v.wait_ge(small_psum, 1)
            step.sig(v.tensor_copy(cols[:, :], ps[0][:, 0:NROWS]))
            v.tensor_copy(acol[:, :], ps[0][:, P:P + NADA]).then_inc(cols_ready, 1)
            v.wait_ge(cols_ready, 1)
            v.wait_ge(dve_step, step.n)
            step.sig(v.memset(wT[CH:P, :, 0:CH], 0.0))
            step.sig(v.tensor_copy(wT[0:CH], ps[1][0:CH, :].rearrange("p (h i) -> p h i", h=HA)))
            step.then(v.tensor_copy(wT[CH:P, :, CH:P], ps[1][CH:P, :].rearrange("p (h i) -> p h i", h=HA)[:, :, CH:P]))
            norm(0)
            norm_out(0, lambda c: cols[:, ROWS["norm1"] + c:ROWS["norm1"] + c + 1])
            v.wait_ge(small_in[1], 48)
            step.then(v.tensor_tensor(lb_bc, lb1_bc, lb_bc, ALU.subtract))
            v.sem_inc(lb_diff, 1)
            v.wait_ge(lb_exp, 1)
            step.then(v.tensor_scalar(lb_bc, lb_bc, 1.0, None, ALU.add))
            step.then(v.reciprocal(lb_bc, lb_bc))
            step.then(v.tensor_scalar(lb1_bc, lb_bc, -1.0, 1.0, ALU.mult, ALU.add))
            v.wait_ge(proj_act, 4)
            for t in range(NT):
                step.sig(v.tensor_tensor(sq[:, t], proj[:, t, NB:2 * NB], proj[:, t, NB:2 * NB], ALU.mult))
            v.wait_ge(dve_step, step.n)
            head_sums(sq, 4)
            v.wait_ge(dve_step, step.n)
            v.sem_inc(sum_ready, 1)
            v.wait_ge(proj_act, 8)
            for t in range(NT):
                f = proj[:, t, 3 * NB:4 * NB]
                step.then(v.tensor_tensor(f, f, lb1_bc, ALU.mult))
                step.then(v.tensor_tensor(f, f, lb_bc, ALU.add))
                step.then(v.tensor_scalar(hk[:, t], f, -1.0, 1.0, ALU.mult, ALU.add))
            v.sem_inc(f_ready, 1)
            for t in range(NT):
                bank_done(v, "w_in", 4, t, 4)
                v.tensor_copy(proj[:, t, 4 * NB:5 * NB], ps[t][:, :]).then_inc(proj_dve, 1)
            v.wait_ge(rms_ready, 2)
            step.then(v.reciprocal(rstd[:, 0:8], rms[:, 0:8]))
            for t in range(NT):
                vv = proj[:, t, NB:2 * NB].rearrange("p (h e) -> p h e", e=P)
                v.tensor_tensor(vv, vv, rstd[:, 4 * t:4 * t + 4].unsqueeze(2).to_broadcast([P, HA, P]),
                                ALU.mult).then_inc(vh_ready, 1)
            for t in range(NT):
                v.wait_ge(mixed_psum, t + 1)
                v.tensor_tensor(sq[:, t], ps[4 + t][:, :], vg_bc, ALU.mult).then_inc(mixed_taken, 1)
                v.wait_ge(mixed_taken, t + 1)
                for g in range(HA):
                    a = slice(g * P, g * P + P)
                    step.sig(v.scalar_tensor_tensor(proj[:, t, a], sq[:, t, a], cols[:, ROWS["bs"] + g:ROWS["bs"] + g + 1],
                                                    proj[:, t, a], ALU.add, ALU.mult))
            v.wait_ge(dve_step, step.n)
            step.then(v.memset(scT, 0.0))
            q, g = proj[:, :, 2 * NB:3 * NB], proj[:, :, 5 * NB:6 * NB]
            for t in range(NT):
                for j, m in enumerate((q[:, t], hk[:, t], q[:, t], hk[:, t])):
                    v.wait_ge(ex_act, 4 * t + j + 1)
                    v.tensor_tensor(ex[:, j, t], ex[:, j, t], m, ALU.mult).then_inc(ex_ready, 1)
            for j in range(3):
                v.wait_ge(exT_psum, 2 * j + 1)
                v.tensor_copy(exT[:, j, :, 0:P], ps[2 * j][:, :].rearrange("p (h c) -> p h c", h=HA)).then_inc(exT_dve, 1)
            for t in range(NT):
                v.wait_ge(sc_psum, t + 1)
                v.copy_predicated(scT[:, t].rearrange("p (h c) -> p h c", h=HA),
                                  cum[:, 0].bitcast(U32).unsqueeze(1).to_broadcast([P, HA, P]),
                                  ps[t][:, :].rearrange("p (h c) -> p h c", h=HA)).then_inc(sc_ready, 1)
            v.wait_ge(ex_act, 9)
            v.wait_ge(u_psum, 1)
            step.then(v.tensor_copy(st[:, 0], ps[2][:, :]))
            for n in (1, 2):
                for h in range(HA):
                    a = slice(h * P, h * P + P)
                    step.sig(v.scalar_tensor_tensor(st[:, n, a], st[:, n - 1, a], decay[:, 4 * n + h:4 * n + h + 1],
                                                    ps[2 + n][:, a], ALU.mult, ALU.add))
                v.wait_ge(dve_step, step.n)
            v.sem_inc(st_ready, 1)
            v.wait_ge(osq_ready, 2)
            head_sums(sq, 4)
            v.wait_ge(dve_step, step.n)
            v.sem_inc(sum_ready, 1)
            v.wait_ge(rms_ready, 3)
            step.then(v.reciprocal(rstd[:, 0:8], rms[:, 0:8]))
            for t in range(NT):
                gg = g[:, t].rearrange("p (h e) -> p h e", e=P)
                step.then(v.tensor_tensor(gg, gg, rstd[:, 4 * t:4 * t + 4].unsqueeze(2).to_broadcast([P, HA, P]), ALU.mult))
                v.tensor_tensor(g[:, t], g[:, t], ps[OBANK[t]][:, :], ALU.mult).then_inc(ab_ready, 1)
            for c in range(0, 4):
                v.wait_ge(abT_psum, c // 2 + 1)
                v.tensor_copy(mixT[:, c], ps[c // 2][:, (c % 2) * S:(c % 2) * S + S]).then_inc(mixT_dve, 1)
            v.wait_ge(ada_cols, ADA)
            v.tensor_tensor(mod[:, :], ps[6][:, 0:NADA], acol[:, :], ALU.add).then_inc(mod_ready, 1)
            for s in range(2):
                for t in range(NT):
                    bank_done(v, "w_out", s, t, 6 + s)
                    a = slice(s * NB, s * NB + NB)
                    v.tensor_tensor(x[:, t, a], x[:, t, a], ps[MIXBANK[2 * s + t]][:, :], ALU.add).then_inc(x_ready, 1)
            norm(1)
            norm_out(1, lambda c: cols[:, ROWS["norm2"] + c:ROWS["norm2"] + c + 1])

            def bcast(ap, n):
                return ap.unsqueeze(2).to_broadcast([P, ap.shape[1], n])

            step.sig(v.tensor_copy(iota[:, :], iotai[:, :]))
            step.then(v.tensor_scalar(desc[:, :], iotai[:, 0:NE], -1.0, float(NE), ALU.mult, ALU.add))
            v.wait_ge(small_in[3], 64)
            v.wait_ge(logit_psum, 1)
            step.then(v.tensor_tensor(lg, ps[0][:, 0:NT * (NG + NE)].rearrange("p (t n) -> p t n", t=NT),
                                      router_b[:, :].unsqueeze(1).to_broadcast([P, NT, NG + NE]), ALU.add))
            g_log, e_log = lg[:, :, 0:NG], lg[:, :, NG:]
            gmax, gprob, e2, w1, w2, key, v1, v2 = (sm[:, i] for i in (0, 1, 2, 3, 4, 5, 6, 7))

            def first(oh, vals, top, n):
                step.then(v.tensor_tensor(oh, vals, bcast(top, n), ALU.is_equal))
                step.then(v.tensor_tensor(oh, oh, desc[:, 0:n].unsqueeze(1).to_broadcast([P, NT, n]), ALU.mult))
                step.then(v.tensor_reduce(key, oh, AX, ALU.max))
                step.then(v.tensor_tensor(oh, oh, bcast(key, n), ALU.is_equal))

            step.then(v.tensor_reduce(gmax, g_log, AX, ALU.max))
            step.then(v.tensor_tensor(gtmp, g_log, bcast(gmax, NG), ALU.subtract))
            v.sem_inc(router_dve, 1)
            first(goh, g_log, gmax, NG)
            v.wait_ge(router_act, 1)
            step.then(v.tensor_reduce(gprob, gtmp, AX, ALU.add))
            step.then(v.reciprocal(gprob, gprob))
            step.then(v.tensor_scalar(gtmp, goh, -1.0, -NEG, ALU.add, ALU.mult))
            em4 = em.rearrange("p t (g e) -> p (t g) e", e=EPG)
            gtf = gtmp.rearrange("p t g -> p (t g)")
            for t in range(NT):
                step.sig(v.tensor_tensor(em[:, t].rearrange("p (g e) -> p g e", e=EPG), e_log[:, t].rearrange("p (g e) -> p g e", e=EPG),
                                         bcast(goh[:, t], EPG), ALU.mult))
            v.wait_ge(dve_step, step.n)
            step.then(v.tensor_tensor(em4, em4, bcast(gtf, EPG), ALU.add))
            step.then(v.tensor_reduce(v1, em, AX, ALU.max))
            first(oh1, em, v1, NE)
            step.then(v.scalar_tensor_tensor(em, oh1, NEG, em, ALU.mult, ALU.add))
            step.then(v.tensor_reduce(v2, em, AX, ALU.max))
            step.then(v.tensor_tensor(e2, v2, v1, ALU.subtract))
            v.sem_inc(router_dve, 1)
            first(oh2, em, v2, NE)
            step.then(v.tensor_tensor(chosen, oh1, oh2, ALU.add))
            v.sem_inc(chosen_ready, 1)
            v.wait_ge(router_act, 2)
            step.then(v.tensor_scalar(w1, e2, 1.0, None, ALU.add))
            step.then(v.reciprocal(w1, w1))
            step.then(v.tensor_tensor(w1, w1, gprob, ALU.mult))
            step.then(v.tensor_tensor(w2, w1, e2, ALU.mult))
            step.then(v.tensor_tensor(oh1, oh1, bcast(w1, NE), ALU.mult))
            step.then(v.tensor_tensor(oh2, oh2, bcast(w2, NE), ALU.mult))
            step.then(v.tensor_tensor(cwt, oh1, oh2, ALU.add))
            v.wait_ge(pos_psum, 1)
            step.then(v.tensor_scalar(pos1, ps[1][:, 0:NT * NE].rearrange("p (t e) -> p t e", e=NE), 1.0, None, ALU.add))
            step.then(v.tensor_tensor(pos1, pos1, chosen, ALU.mult))
            step.sig(v.tensor_copy(tot, ps[1][:, NT * NE:(NT + 1) * NE]))
            for t in range(NT):
                step.sig(v.tensor_scalar(posb[:, 0:NE, t], pos1[:, t], -1.0, None, ALU.add))
                step.sig(v.tensor_copy(cwb[:, 0:NE, t], cwt[:, t]))
            v.wait_ge(dve_step, step.n)
            v.sem_inc(blocks_ready, 1)

            def overflow_table():
                step.then(v.tensor_scalar(more, tot, float(BT), None, ALU.is_gt))
                for k in range(2, S // BT):
                    step.then(v.scalar_tensor_tensor(more, tot, float(k * BT), more, ALU.is_gt, ALU.add))
                step.then(v.tensor_tensor_scan(upto_e, ones[:, 0:NE], more, 0.0, ALU.mult, ALU.add))
                step.then(v.tensor_tensor(before_e, upto_e, more, ALU.subtract))

                def over_e(ap):
                    return ap.unsqueeze(1).to_broadcast([P, OVF, NE])

                j_of = bcast(iota[:, 0:OVF], NE)
                step.then(v.tensor_tensor(own, over_e(before_e), j_of, ALU.is_le))
                step.then(v.tensor_tensor(otmp, over_e(upto_e), j_of, ALU.is_gt))
                step.then(v.tensor_tensor(own, own, otmp, ALU.mult))
                step.then(v.tensor_tensor(otmp, j_of, over_e(before_e), ALU.subtract))
                step.then(v.scalar_tensor_tensor(otmp, otmp, 1.0, own, ALU.add, ALU.mult))
                step.then(v.tensor_reduce(obase, otmp, AX, ALU.add))
                step.then(v.tensor_scalar(obase, obase, float(BT), 1.0, ALU.mult, ALU.add))
                step.then(v.tensor_tensor(otmp, own, over_e(iota[:, 0:NE]), ALU.mult))
                step.then(v.tensor_reduce(oexp, otmp, AX, ALU.add))
                step.sig(v.tensor_copy(oexp_i[:, 0:OVF], oexp))
                step.then(v.tensor_copy(oexp_i[:, OVF:OVF + 1], upto_e[:, NE - 1:NE]))
                for t in range(NT):
                    step.then(v.tensor_tensor(otmp, own, over_e(pos1[:, t]), ALU.mult))
                    step.then(v.tensor_reduce(posb[:, NE:BLOCKS, t], otmp, AX, ALU.add))
                    step.then(v.tensor_tensor(posb[:, NE:BLOCKS, t], posb[:, NE:BLOCKS, t], obase, ALU.subtract))
                    step.then(v.tensor_tensor(otmp, own, over_e(cwt[:, t]), ALU.mult))
                    step.then(v.tensor_reduce(cwb[:, NE:BLOCKS, t], otmp, AX, ALU.add))
                v.sem_inc(overflow_ready, 1)

            def build_pick(m, q, weighted):
                for e in range(2):
                    for t in range(NT):
                        b = q * 2 + (m.block0 + e)
                        at = posb[:, bass.ds(b, 1), t]
                        dst = (pickw if weighted else pick)[:, t, e * BT:e * BT + BT]
                        if weighted:
                            ins = v.tensor_scalar(dst, iota[:, :], at, cwb[:, bass.ds(b, 1), t], ALU.is_equal, ALU.mult)
                        else:
                            ins = v.tensor_scalar(dst, iota[:, :], at, None, ALU.is_equal)
                ins.then_inc(m.pickw_ready if weighted else m.pick_ready, 1)

            def take_gathered(m, n):
                for k in range(2):
                    v.wait_ge(m.gathered, n + (k + 1))
                    c = 4 * k
                    v.tensor_tensor(xgT[:, c:c + 4], ps[6 + k][:, :].rearrange("p (c s) -> p c s", c=4),
                                    bcast(cols[:, ROWS["norm2"] + c:ROWS["norm2"] + c + 4], 2 * BT),
                                    ALU.mult).then_inc(m.xg_ready, 1)

            def pairs(m, n):
                v.sem_inc(m.pickT_ready, 1)
                v.sem_inc(m.o_dve, 1)
                build_pick(m, 0, False)
                take_gathered(m, 0)
                if m is main:
                    overflow_table()
                with v.Fori(0, n) as q:
                    v.wait_ge(m.gathered, q * 2 + 2)
                    build_pick(m, q + 1, False)
                    v.wait_ge(m.pickT_psum, q + 1)
                    build_pick(m, q, True)
                    v.wait_ge(m.sg_ready, q + 1)
                    v.tensor_tensor(eh, sg, ps[5][:, :], ALU.mult).then_inc(m.h_ready, 1)
                    take_gathered(m, q * 2 + 2)
                    v.wait_ge(m.pickT_psum, q + 2)
                    v.tensor_copy(pickT, ps[7][:, 0:NT * P]).then_inc(m.pickT_ready, 1)
                    m.wait_used(v, q, 6)
                    v.tensor_copy(eo[:, NB:D], ps[5][:, :]).then_inc(m.o_dve, 1)

            def low(l, i, n):
                slot = MSLOT[l][n % 4]
                v.wait_ge(hi_ready, i * 4 + (SPLIT[f"mlp{l}"] + n + 1))
                v.tensor_tensor(ring_r[:, slot], ring[:, slot], ring_r[:, HSLOT[l][n % 2]], ALU.subtract).then_inc(lo_ready, 1)

            def low_in(name, k, slots):
                slot = slots[k]
                v.wait_ge(hi_ready, SPLIT[name] + k + 1)
                v.tensor_tensor(ring_r[:, slot], ring[:, slot], high_place(name, k), ALU.subtract).then_inc(lo_ready, 1)

            def parts_of_h(j, dst):
                v.wait_ge(hT_dve, 4 * (3 + j))
                step.then(v.tensor_copy(dst[:, 0:4], hT[:, 0:4]))
                v.tensor_tensor(hT_r[:, 0:4], hT[:, 0:4], dst[:, 0:4], ALU.subtract).then_inc(h_lo_ready, 1)
                v.wait_ge(h_hi_ready, j + 1)
                v.tensor_tensor(hT_r[:, 4:KC], hT[:, 4:KC], dst[:, 4:KC], ALU.subtract).then_inc(h_lo_ready, 1)

            pairs(main, PAIRS)
            with v.If(any_overflow(v) > 0):
                pairs(ovf, OVF_PAIRS)
                v.wait_ge(ovf.scattered, OVF_PAIRS)
            low_in("nsa_in", 0, NSLOT)
            v.wait_ge(main.scattered, PAIRS)
            for s in range(2):
                for t in range(NT):
                    a = slice(s * NB, s * NB + NB)
                    v.tensor_tensor(x[:, t, a], x[:, t, a], ps[2 * t + s][:, :], ALU.add).then_inc(x_ready, 1)

            v.wait_ge(x_ready, 8)
            norm(2)
            v.wait_ge(xn_ready, 6)
            v.wait_ge(fg_in, 16)
            for t in range(NT):
                v.tensor_tensor(x[:, t], xn[:, t], fg_bc, ALU.mult).then_inc(x_ready, 2)
            v.wait_ge(mod_ready, 1)
            for l in range(2):
                for w, (name, part) in enumerate((("mix", 1), ("mlp", 4))):
                    sc = mod[:, (l * 6 + part) * KC:(l * 6 + part + 1) * KC]
                    g = cols[:, ROWS[name] + l * KC:ROWS[name] + (l + 1) * KC]
                    step.sig(v.scalar_tensor_tensor(gain_a[:, 2 * l + w], sc, 1.0, g, ALU.add, ALU.mult))
            cos = cossin[:, 0].rearrange("p (t i) -> p t i", t=NT)
            sin = cossin[:, 1].rearrange("p (t i) -> p t i", t=NT)

            def norm2(i, j, l, which):
                norm(i)
                norm_out(j, lambda c: gain_a[:, 2 * l + which, c:c + 1],
                         lambda c: mod[:, (l * 6 + 3 * which) * KC + c:(l * 6 + 3 * which) * KC + c + 1])

            def gate_cols(k, l, part):
                for c in range(KC):
                    ins = v.tensor_scalar(rep[:, c], ones[:, :], mod[:, (l * 6 + part) * KC + c:(l * 6 + part) * KC + c + 1],
                                          None, ALU.mult)
                ins.then_inc(rep_ready, 1)

            def rope(first, heads):
                h = proj[:, :, first:first + heads * DH].rearrange("p t (h e) -> p t h e", e=DH)
                a, b = h[:, :, :, 0:RD], h[:, :, :, RD:2 * RD]
                w = lambda i: rope_s[:, i, 0:NT * heads * RD].rearrange("p (t h i) -> p t h i", t=NT, i=RD)
                over = lambda ap: ap.unsqueeze(2).to_broadcast([P, NT, heads, RD])
                step.sig(v.tensor_tensor(w(0), a, over(cos), ALU.mult))
                step.sig(v.tensor_tensor(w(1), b, over(sin), ALU.mult))
                step.sig(v.tensor_tensor(w(2), b, over(cos), ALU.mult))
                step.then(v.tensor_tensor(w(3), a, over(sin), ALU.mult))
                step.sig(v.tensor_tensor(a, w(0), w(1), ALU.subtract))
                step.then(v.tensor_tensor(b, w(2), w(3), ALU.add))

            def query_sums(per, sq3):
                for t in range(NT):
                    step.sig(v.tensor_reduce(ss[:, per * t:per * t + QH], sq3[:, t, 0:QH * DH].rearrange("p (h e) -> p h e", e=DH), AX, ALU.add))
                v.wait_ge(dve_step, step.n)
                v.sem_inc(sum_ready, 1)

            def scaled(first, heads, r0, per, gain):
                for t in range(NT):
                    h = proj[:, t, first:first + heads * DH].rearrange("p (h e) -> p h e", e=DH)
                    step.then(v.tensor_tensor(h, h, bcast(rstd[:, r0 + per * t:r0 + per * t + heads], DH), ALU.mult))
                    step.then(v.tensor_tensor(h, h, gain.unsqueeze(1).to_broadcast([P, heads, DH]), ALU.mult))

            def unit_max(u, nk):
                v.wait_ge(sc2_psum, u + 1)
                v.wait_ge(e_ready, 4 * (u - 1)) if u > 1 else None
                for k in range(2):
                    b = ps[2 * (u % 2) + k][:, :].rearrange("p (h k) -> p h k", h=2)
                    dg = b[:, :, nk - P:nk]
                    step.sig(v.tensor_tensor(dg, dg, dmask.unsqueeze(1).to_broadcast([P, 2, P]), ALU.add))
                v.wait_ge(dve_step, step.n)
                for k in range(2):
                    b = ps[2 * (u % 2) + k][:, :].rearrange("p (h k) -> p h k", h=2)
                    step.sig(v.tensor_reduce(nm[:, u % 2, 2 * k:2 * k + 2], b[:, :, 0:nk], AX, ALU.max))
                v.wait_ge(dve_step, step.n)
                v.tensor_scalar(nm[:, u % 2], nm[:, u % 2], -SCALE, None, ALU.mult).then_inc(nm_ready, 1)

            def residual(name, half, gate, banks):
                v.wait_ge(gate_ready, 2 * gate + 2)
                for s, t in ((0, 0), (0, 1), (1, 0), (1, 1)) if name else ((0, 0), (1, 0), (0, 1), (1, 1)):
                    if name:
                        bank_done(v, name, s, t, half + s)
                    a = slice(s * NB, s * NB + NB)
                    step.then(v.tensor_tensor(res[:, s, t], ps[banks(s, t)][:, :], gbc[:, a], ALU.mult))
                    v.tensor_tensor(x[:, t, a], x[:, t, a], res[:, s, t], ALU.add).then_inc(x_ready, 1)

            norm2(3, 2, 0, 0)
            parts_of_h(0, h_hi_nsa)
            low_in("nsa_in", 1, NSLOT)
            gate_cols(0, 0, 2)
            step.sig(v.tensor_scalar(dmask, before[:, :], NEG, None, ALU.mult))
            step.sig(v.tensor_scalar(cadd, cm01[:, :, :], -1.0, -NEG, ALU.add, ALU.mult))
            v.wait_ge(nsa_in_sem, 9 * 16)
            step.then(v.tensor_copy(kk[:, 0, 0:NT], posi[:, :]))
            step.then(v.tensor_tensor(rt[:, 1].rearrange("p (t i) -> p t i", t=NT), bcast(kk[:, 0, 0:NT], RD),
                                      inv[:, :].unsqueeze(1).to_broadcast([P, NT, RD]), ALU.mult))
            step.then(v.tensor_scalar(kk[:, 0], rt[:, 1], 1.0 / TWO_PI, 0.25, ALU.mult, ALU.add))
            step.then(v.tensor_scalar(kk[:, 1], rt[:, 1], 1.0 / TWO_PI, None, ALU.mult))
            step.then(v.tensor_scalar(kk, kk, ROUND, None, ALU.add))
            step.then(v.tensor_scalar(kk, kk, ROUND, None, ALU.subtract))
            step.then(v.tensor_copy(rt[:, 0], rt[:, 1]))
            for part in (PI1, PI2, PI3):
                step.then(v.scalar_tensor_tensor(rt, kk, -part, rt, ALU.mult, ALU.add))
            step.then(v.tensor_scalar(rt[:, 0], rt[:, 0], math.pi / 2, None, ALU.add))
            step.then(v.tensor_scalar(rt, rt, 3.1415925, -3.1415925, ALU.min, ALU.max))
            v.sem_inc(rope_dve, 1)
            low_in("nsa_in", 2, NSLOT)
            v.wait_ge(proj_act, 10 + 4)
            query_sums(24, sqn)
            low_in("nsa_in", 3, NSLOT)
            v.wait_ge(rms_ready, 7)
            step.then(v.reciprocal(heads(rstd, 24, 0, QH), heads(rms, 24, 0, QH)))
            scaled(0, QH, 0, 24, qg)
            v.sem_inc(rows_ready, 1)
            for t in range(NT):
                bank_done(v, "nsa_in", 2, t, 10)
                v.tensor_copy(proj[:, t, 2 * NB:3 * NB], ps[t][:, :]).then_inc(proj_dve, 1)
            low_in("nsa_in", 4, NSLOT)
            v.wait_ge(gl_psum, 1)
            v.tensor_tensor(gl, ps[7][:, 0:NT * 3 * QH].rearrange("p (t n) -> p t n", t=NT),
                            bgl.unsqueeze(1).to_broadcast([P, NT, 3 * QH]), ALU.add).then_inc(gl_dve, 1)
            for gp in range(2):
                v.wait_ge(kz_psum, 3 + gp)
                for o in range(2):
                    src = ps[2 + gp][DH * o:DH * o + DH, 0:S]
                    v.tensor_copy(kz[0:DH, 1, 2 * gp + o], src).then_inc(kz_dve, 1)
                    v.tensor_copy(kz[DH:P, 1, 2 * gp + o, 0:S - 1], src[:, 1:S]).then_inc(kz_dve, 1)
            v.wait_ge(proj_act, 10 + 8)
            for t in range(NT):
                step.sig(v.tensor_reduce(ss[:, 24 * t + QH:24 * t + 24], sqn[:, t, QH * DH:].rearrange("p (h e) -> p h e", e=DH), AX, ALU.add))
            v.wait_ge(dve_step, step.n)
            v.sem_inc(sum_ready, 1)
            v.wait_ge(rms_ready, 8)
            step.then(v.reciprocal(heads(rstd, 24, QH, 2 * GR), heads(rms, 24, QH, 2 * GR)))
            v.wait_ge(heads_psum, 2)
            for k in range(2):
                v.tensor_copy(qcT[:, 4 * k:4 * k + 4, P:S], ps[2 + k][:, :].rearrange("p (h q) -> p h q", h=4)).then_inc(heads_dve, 1)
            scaled(1536, GR, 16, 24, kg[:, 1])
            v.wait_ge(rope_act, 1)
            rope_s = view(work, 0, 4, 256)
            rope(1536, GR)
            v.sem_inc(rows_ready, 1)
            scaled(2048, GR, 20, 24, kg[:, 2])
            rope(2048, GR)
            v.sem_inc(rows_ready, 1)
            rope(0, QH)
            v.sem_inc(rows_ready, 1)
            v.wait_ge(heads_psum, 4)
            for t in range(NT):
                for o in range(2):
                    v.tensor_copy(kT[DH * o:DH * o + DH, 1, :, t * P:t * P + P],
                                  ps[2 + t][0:DH, :].rearrange("p (g q) -> p g q", g=GR)).then_inc(heads_dve, 1)
            step.then(v.memset(kcT, 0.0))
            v.wait_ge(rms_ready, 9)
            G15 = GR * NCMP
            step.then(v.reciprocal(rstd[0:G15, 48:49], rms[0:G15, 48:49]))
            v.scalar_tensor_tensor(kcm[0:G15], ps[6][0:G15, 0:DH], rstd[0:G15, 48:49], kg[0:G15, 0], ALU.mult, ALU.mult).then_inc(cmp_dve, 1)
            v.wait_ge(cmp_psum, 4)
            v.tensor_copy(vcm[0:NCMP], ps[7][0:NCMP, 0:GR * DH].rearrange("p (g e) -> p g e", e=DH)).then_inc(cmp_dve, 1)
            v.wait_ge(heads_psum, 6)
            for k in range(2):
                v.tensor_copy(qrT[:, 4 * k:4 * k + 4, P:S], ps[2 + k][:, :].rearrange("p (h q) -> p h q", h=4)).then_inc(heads_dve, 1)
            v.wait_ge(cmp_psum, 5)
            for o in range(2):
                v.tensor_copy(kcT[DH * o:DH * o + DH, :, 16 * o:16 * o + NCMP],
                              ps[6][0:DH, 64:64 + G15].rearrange("p (g k) -> p g k", g=GR)).then_inc(cmp_dve, 1)

            def compressed_softmax():
                v.wait_ge(csc_psum, 1)
                c16 = lambda ap: ap.rearrange("p (h c) -> p h c", c=16)[:, :, 0:NCMP]
                step.then(v.memset(csc, 0.0))
                for o in range(2):
                    for t in range(NT):
                        step.sig(v.scalar_tensor_tensor(c16(csc[:, o, t]), ps[5][:, t * S:t * S + S].rearrange("p (c o k) -> p c o k", o=2, k=16)[:, :, o, 0:NCMP], SCALE,
                                                        cadd[:, t, 0:NCMP].unsqueeze(1).to_broadcast([P, 8, NCMP]), ALU.mult, ALU.add))
                v.wait_ge(dve_step, step.n)
                call = csc.rearrange("p o t n -> p (o t n)").rearrange("p (h c) -> p h c", c=16)[:, :, 0:NCMP]
                step.then(v.tensor_reduce(cmx[:, 0:32], call, AX, ALU.max))
                step.then(v.tensor_tensor(call, call, bcast(cmx[:, 0:32], NCMP), ALU.subtract))
                v.sem_inc(cexp_dve, 1)
                v.wait_ge(cexp_act, 1)
                step.then(v.tensor_reduce(csum[:, 0:32], call, AX, ALU.add))
                step.then(v.reciprocal(csum[:, 0:32], csum[:, 0:32]))
                v.wait_ge(gl_ready, 1)
                for o in range(2):
                    for t in range(NT):
                        gate = gl[:, t].rearrange("p (h w) -> p h w", w=6)[:, :, 3 * o]
                        at = (o * NT + t) * 8
                        step.then(v.tensor_tensor(csum[:, at:at + 8], csum[:, at:at + 8], gate, ALU.mult))
                        step.then(v.tensor_tensor(c16(csc[:, o, t]), c16(csc[:, o, t]),
                                                  cm01[:, t, 0:NCMP].unsqueeze(1).to_broadcast([P, 8, NCMP]), ALU.mult))
                        step.then(v.tensor_tensor(c16(csc[:, o, t]), c16(csc[:, o, t]), bcast(csum[:, at:at + 8], NCMP), ALU.mult))
                v.sem_inc(cw_ready, 1)

            def unit_weights(u, t, g, br):
                nk = (t + 1) * P
                v.wait_ge(e_ready, 4 * (u + 1))
                s4 = sums[:, u % 2]
                step.then(v.reciprocal(s4, s4))
                gate = gl[:, t, 12 * g:12 * g + 12].rearrange("p (j o w) -> p o j w", j=2, w=3)[:, :, :, 1 + br]
                s22 = s4.rearrange("p (o j) -> p o j", j=2)
                step.then(v.tensor_tensor(s22, s22, gate, ALU.mult))
                v.tensor_tensor(E[u % 3][:, :, 0:nk], E[u % 3][:, :, 0:nk], bcast(s4, nk), ALU.mult).then_inc(p_ready, 1)

            for i in range(NU + 2):
                if i < NU:
                    unit_max(i, (i // 8 + 1) * P)
                u = i - 1
                if 0 <= u < NU:
                    unit_weights(u, u // 8, (u // 2) % GR, u % 2)
                if i == 2:
                    compressed_softmax()
                u = i - 2
                if u >= 8:
                    v.wait_ge(pT_psum, u + 1)
                    v.tensor_copy(pT[u % 2][1], ps[5][:, :].rearrange("p (h q) -> p h q", h=4)).then_inc(pT_dve, 1)
            low(0, 0, 0)
            residual("nsa_out", 13, 0, lambda s, t: 2 * s + t)
            def mlp(l):
                norm2(4 + 2 * l, 3 + 2 * l, l, 1)
                parts_of_h(1 + 2 * l, h_hi_r)
                gate_cols(1 + 2 * l, l, 5)
                low(l, 0, 1)

                def hidden_parts(k, par):
                    for n in range(2):
                        v.wait_ge(sq_ready, k * 2 + (l * 2 * MC + n + 1))
                        a = slice(2 * n, 2 * n + 2)
                        v.tensor_copy(hid_hi_r[par][:, a], hid[par][:, a]).then_inc(hid_hi_ready, 1)
                        v.wait_ge(hid_hi_ready, k * 2 + (l * 2 * MC + n + 1))
                        v.tensor_tensor(hid_lo[par][:, a], hid[par][:, a], hid_hi_r[par][:, a], ALU.subtract).then_inc(hid_ready, 1)

                hidden_parts(0, 0)
                low(l, 0, 2)
                with v.Fori(0, 3) as i:
                    hidden_parts(i * 2 + 1, 1)
                    low(l, i, 3)
                    low(l, i, 4)
                    hidden_parts(i * 2 + 2, 0)
                    low(l, i, 5)
                    low(l, i, 6)
                hidden_parts(7, 1)
                low(l, 3, 3)
                if l == 0:
                    low_in("diff_in", 0, DSLOT)
                v.wait_ge(slabs_used, SLABS[f"mlp{l}"] + 16)
                residual(None, 0, 1 + 2 * l, lambda s, t: 2 * t + s)

            mlp(0)
            norm2(5, 4, 1, 0)
            parts_of_h(2, h_hi_r)
            low_in("diff_in", 1, DSLOT)
            gate_cols(2, 1, 2)
            v.wait_ge(diff_in_sem, 6 * 16)
            for k in range(2):
                step.then(v.tensor_tensor(lamv[:, 2 * k], lamv[:, 2 * k], lamv[:, 2 * k + 1], ALU.mult))
            for k in range(2):
                step.then(v.tensor_reduce(dl[:, k:k + 1], lamv[:, 2 * k], AX, ALU.add))
            step.then(v.tensor_copy(lamv[:, 0, 0:2], dl[:, 0:2]))
            v.sem_inc(lam_dve, 1)
            v.wait_ge(lam_act, 1)
            step.then(v.tensor_tensor(dl[:, 0:1], lamv[:, 0, 1:2], lamv[:, 0, 0:1], ALU.subtract))
            step.sig(v.tensor_scalar(dl[:, 0:1], dl[:, 0:1], -LAM0, None, ALU.add))
            step.then(v.tensor_scalar(lamv[:, 1, 0:1], cols[:, ROWS["subln"]:ROWS["subln"] + 1], 1.0 - LAM0, None, ALU.mult))
            rope_s = view(xn, 0, 4, 256)

            def scaled_rows(w):
                v.wait_ge(rms_ready, 12 + w)
                step.then(v.reciprocal(heads(rstd, 32, QH * w, QH), heads(rms, 32, QH * w, QH)))
                scaled(1024 * w, QH, 16 * w, 32, dgain[:, w])

            def rotated_rows(w):
                rope(1024 * w, QH)
                v.sem_inc(rows_ready, 1)

            low_in("diff_in", 2, DSLOT)
            v.wait_ge(proj_act, 18 + 4)
            query_sums(32, sqn)
            low_in("diff_in", 3, DSLOT)
            scaled_rows(0)
            low_in("diff_in", 4, DSLOT)
            v.wait_ge(gate_psum, 3)
            rotated_rows(0)
            v.wait_ge(proj_act, 18 + 8)
            for t in range(NT):
                step.sig(v.tensor_reduce(ss[:, 32 * t + 16:32 * t + 32], dsq[:, t, 0:1024].rearrange("p (h e) -> p h e", e=DH), AX, ALU.add))
            v.wait_ge(dve_step, step.n)
            v.sem_inc(sum_ready, 1)
            low_in("diff_in", 5, DSLOT)
            scaled_rows(1)
            rotated_rows(1)
            for s in (4, 5):
                for t in range(NT):
                    bank_done(v, "diff_in", s, t, 15 + s)
                    v.tensor_copy(proj[:, t, s * NB:(s + 1) * NB], ps[(s % 2) * 2 + t][:, :]).then_inc(proj_dve, 1)
            for w in range(2):
                v.wait_ge(heads_psum, 8 + 2 * w)
                for k in range(2):
                    v.tensor_copy(dqT[w][:, 4 * k:4 * k + 4, P:S], ps[4 * w + 2 + k][:, :].rearrange("p (h q) -> p h q", h=4)).then_inc(heads_dve, 1)

            def diff_weights(u, nk):
                v.wait_ge(e_ready, 4 * (u + 1))
                s4 = sums[:, u % 2]
                step.then(v.reciprocal(s4, s4))
                step.then(v.tensor_scalar(s4[:, 2:4], s4[:, 2:4], dl[:, 0:1], None, ALU.mult))
                for j in range(2):
                    step.sig(v.tensor_scalar(E[u % 3][:, 2 + j, 0:nk], E[u % 3][:, 2 + j, 0:nk], s4[:, 2 + j:3 + j], None, ALU.mult))
                v.wait_ge(dve_step, step.n)
                for j in range(2):
                    v.scalar_tensor_tensor(E[u % 3][:, j, 0:nk], E[u % 3][:, j, 0:nk], s4[:, j:j + 1], E[u % 3][:, 2 + j, 0:nk],
                                           ALU.mult, ALU.add).then_inc(p_ready, 1)

            for i in range(NUD + 1):
                if i < NUD:
                    unit_max(NU + i, (i // 4 + 1) * P)
                if i:
                    diff_weights(NU + i - 1, ((i - 1) // 4 + 1) * P)
            v.wait_ge(sq_act, 2)
            for t in range(NT):
                step.sig(v.tensor_reduce(ss[:, 8 * t:8 * t + 8], work[:, t * D:(t + 1) * D].rearrange("p (h e) -> p h e", e=P), AX, ALU.add))
            v.wait_ge(dve_step, step.n)
            v.sem_inc(sum_ready, 1)
            v.wait_ge(rms_ready, 14)
            step.then(v.reciprocal(rstd[:, 0:16], rms[:, 0:16]))
            for t in range(NT):
                o = proj[:, t, 0:D].rearrange("p (h e) -> p h e", e=P)
                v.tensor_tensor(o, o, bcast(rstd[:, 8 * t:8 * t + 8], P), ALU.mult).then_inc(orow_ready, 1)
            v.wait_ge(abT_psum, 6)
            for c in range(0, 4):
                v.tensor_scalar(mixT[:, c], ps[c // 2][:, (c % 2) * S:(c % 2) * S + S], lamv[:, 1, 0:1], None, ALU.mult).then_inc(mixT_dve, 1)
            low(1, 0, 0)
            residual("diff_out", 21, 2, lambda s, t: 4 + 2 * s + t)
            mlp(1)

        @block.tensor
        def _(pe):
            r = Ring()
            step = Steps(pe, pe_step)

            def arrived(slot):
                _, loads = r.take(slot)
                pe.wait_ge(landed[slot], 16 * loads)

            def norm_T(i):
                for t in range(NT):
                    pe.wait_ge(xn_ready, 2 * i + t + 1)
                    for c in (0, 1, 4, 5, 2, 3, 6, 7):
                        m = pe.transpose(ps[4 + c // 2][:, (c % 2) * S + t * P:(c % 2) * S + t * P + P],
                                         xn[:, t, c * P:c * P + P], ident[:, :])
                        if t == NT - 1 and c % 2:
                            m.then_inc(xnT_psum, 1)

            def product(bank, lhs, t, slot):
                w = slab(slot)
                for c in range(KC):
                    m = pe.matmul(bank[:, :], lhs[:, c, t * P:t * P + P], w[:, c, :], start=(c == 0), stop=(c == KC - 1))
                return m

            pe.wait_ge(const_ready, 1)
            pe.wait_ge(small_in[0], 16 * 11)
            pe.transpose(ps[0][:, 0:NROWS], rows[0:NROWS, :], ident[0:NROWS, 0:NROWS])
            pe.transpose(ps[0][:, P:P + NADA], arow[:, :], ident[0:NADA, 0:NADA])
            pe.wait_ge(small_in[2], 16)
            for g in range(HA):
                m = pe.transpose(ps[1][:, g * P:g * P + P], ws[:, g], ident[:, :])
            m.then_inc(small_psum, 1)
            norm_T(0)
            pe.wait_ge(hT_dve, 4)
            pe.wait_ge(hT_act, 4)
            pe.wait_ge(cols_ready, 1)
            pe.wait_ge(dve_step, 4)
            def ada_columns(n):
                pe.wait_ge(ada_rows, n + 1)
                for c in range(4):
                    m = pe.matmul(ps[6][:, 4 * n + c:4 * n + c + 1], ada_row[:, n % 2, c * P:c * P + P], sel4[:, :],
                                  start=True, stop=True)
                m.then_inc(ada_cols, 1)

            def ada(first, last):
                for n in range(first, last):
                    slot = ada_slab(n) % SLOTS
                    arrived(slot)
                    if n:
                        pe.wait_ge(ada_rows, n)
                    for c in range(KC):
                        j = c % 4
                        m = pe.matmul(ps[7][32 * j:32 * j + 32, :], crep[:, c], slab(slot)[:, c, :],
                                      start=(c < 4), stop=(c >= 4), skip_group_check=True)
                    m.then_inc(slabs_used, 1)
                    if n:
                        ada_columns(n - 1)

            for s in range(6):
                slot = in_slab(s) % SLOTS
                arrived(slot)
                for t in range(NT):
                    if s >= 2:
                        pe.wait_ge(proj_act, 2 * (s - 2) + t + 1)
                    product(ps[(s % 2) * 2 + t], hT, t, slot).then_inc(slabs_used if t else half_psum, 1)
                    if s + t == 0:
                        pe.wait_ge(crep_ready, KC)
                    ada(2 * s + t, 2 * s + t + 1)
            for t in range(NT):
                pe.wait_ge(vh_ready, t + 1)
                for g in range(HA):
                    m = pe.matmul(ps[4 + t][:, g * P:g * P + P], wT[:, g], proj[:, t, NB + g * P:NB + g * P + P],
                                  start=True, stop=True)
                m.then_inc(mixed_psum, 1)
            ada(12, 14)
            pe.wait_ge(mixed_taken, 2)
            pe.wait_ge(lf_ready, 1)
            for t in range(NT):
                for m_ in range(3):
                    m = pe.matmul(ps[3 * t + m_][:, :], cum[:, m_], lf[:, t], start=True, stop=True)
            m.then_inc(cum_psum, 1)
            ada(14, 16)
            pe.wait_ge(ex_act, 4)
            for t in range(NT):
                for h in range(HA):
                    m = pe.matmul(ps[0][:, 8 * t + h:8 * t + h + 5:4], lf[:, t, h * P:h * P + P], same[:, :], start=True, stop=True)
            m.then_inc(cum_psum, 1)
            for j in range(3):
                for t in range(NT):
                    pe.wait_ge(ex_act, 9)
                    pe.wait_ge(ex_ready, 4 * t + j + 1)
                    for h in range(HA):
                        m = pe.transpose(ps[2 * j + t][:, h * P:h * P + P], ex[:, j, t, h * P:h * P + P], ident[:, :])
                    m.then_inc(exT_psum, 1)
            ada(16, 18)
            pe.wait_ge(exT_dve, 3)
            pe.wait_ge(exT_ready, 3)
            for t in range(NT):
                a = slice(t * P, t * P + P)
                for h in range(HA):
                    m = pe.matmul(ps[t][:, h * P:h * P + P], exT[:, 1, h, a], exT[:, 0, h, a], start=True, stop=True)
                m.then_inc(sc_psum, 1)
            pe.wait_ge(ex_ready, 8)
            pe.wait_ge(proj_dve, 2)
            for n in range(3):
                t, b = n // 2, CH * (n % 2)
                for h in range(HA):
                    a = slice(h * P, h * P + P)
                    m = pe.matmul(ps[2 + n][:, a], ex[b:b + CH, 3, t, a], proj[b:b + CH, t, 4 * NB + h * P:4 * NB + h * P + P],
                                  start=True, stop=True)
            m.then_inc(u_psum, 1)
            ada(18, 20)
            for t in range(NT):
                pe.wait_ge(sc_ready, t + 1)
                for h in range(HA):
                    a = slice(h * P, h * P + P)
                    pe.matmul(ps[OBANK[t]][:, a], scT[:, t, a], proj[:, t, 4 * NB + h * P:4 * NB + h * P + P],
                              start=(h == 0), stop=False, skip_group_check=True)
            pe.wait_ge(st_ready, 1)
            for n in (1, 2, 3):
                t, b = n // 2, CH * (n % 2)
                for h in range(HA):
                    a = slice(h * P, h * P + P)
                    m = pe.matmul(ps[OBANK[t]][b:b + CH, a], exT[:, 2, h, n * CH:n * CH + CH], st[:, n - 1, a],
                                  start=False, stop=True, skip_group_check=True)
            m.then_inc(o_psum, 1)
            ada(20, ADA)
            pe.wait_ge(ab_ready, 2)
            for c in range(KC):
                for t in range(NT):
                    src = c * P if c < 4 else 5 * NB + (c - 4) * P
                    m = pe.transpose(ps[c // 2][:, (c % 2) * S + t * P:(c % 2) * S + t * P + P], proj[:, t, src:src + P], ident[:, :])
                if c % 2:
                    m.then_inc(abT_psum, 1)
            ada_columns(ADA - 1)
            pe.wait_ge(mixT_dve, 4)
            pe.wait_ge(mixT_act, 4)
            for s in range(2):
                arrived(s)
                for t in range(NT):
                    product(ps[MIXBANK[2 * s + t]], mixT, t, s).then_inc(slabs_used if t else half_psum, 1)
            norm_T(1)
            pe.wait_ge(hT_dve, 8)
            pe.wait_ge(hT_act, 8)
            pe.wait_ge(small_in[3], 64)
            for t in range(NT):
                for c in range(KC):
                    m = pe.matmul(ps[0][:, t * (NG + NE):(t + 1) * (NG + NE)], hT[:, c, t * P:t * P + P], wr[:, c, :],
                                  start=(c == 0), stop=(c == KC - 1))
            m.then_inc(logit_psum, 1)
            pe.wait_ge(chosen_ready, 1)
            for t in range(NT):
                for u in range(t + 1):
                    pe.matmul(ps[1][:, t * NE:(t + 1) * NE], before[:, :] if u == t else ones[:, :], chosen[:, u],
                              start=(u == 0), stop=(u == t))
            for u in range(NT):
                m = pe.matmul(ps[1][:, NT * NE:(NT + 1) * NE], ones[:, :], chosen[:, u], start=(u == 0), stop=(u == NT - 1))
            m.then_inc(pos_psum, 1)

            def gather(m):
                for k in range(2):
                    for c in range(4 * k, 4 * k + 4):
                        for t in range(NT):
                            ins = pe.matmul(ps[6 + k][:, (c % 4) * 2 * BT:(c % 4 + 1) * 2 * BT], xn[:, t, c * P:c * P + P],
                                            pick[:, t], start=(t == 0), stop=(t == NT - 1))
                    ins.then_inc(m.gathered, 1)

            def pair(m, q):
                pe.wait_ge(m.xg_ready, q * 2 + 2)
                pe.wait_ge(m.o_act, q + 1)
                pe.wait_ge(m.o_dve, q + 1)
                for part in range(2):
                    m.wait_landed(pe, q, 2 * part)
                    m.wait_landed(pe, q, 2 * part + 1)
                    for c in range(KC):
                        for e in range(2):
                            ins = pe.matmul(ps[4 + part][BT * e:BT * e + BT, :], xgT[:, c, BT * e:BT * e + BT],
                                            slab(ESLOT[2 * part + e])[:, c, :], start=(c == 0), stop=(c == KC - 1),
                                            skip_group_check=True)
                    ins.then_inc(m.used, 2)
                pe.wait_ge(m.pick_ready, q + 2)
                pe.wait_ge(m.hT_ready, q + 1)
                pe.wait_ge(m.pickT_ready, q + 1)
                gather(m)
                pe.wait_ge(m.h_ready, q + 1)
                pe.wait_ge(m.xg_ready, q * 2 + 3)
                for c in range(FE // P):
                    ins = pe.transpose(ps[6][:, c * P:c * P + P], eh[:, c * P:c * P + P], ident[:, :])
                ins.then_inc(m.hT_psum, 1)
                pe.wait_ge(m.pickw_ready, q + 1)
                pe.wait_ge(m.xg_ready, q * 2 + 4)
                for t in range(NT):
                    ins = pe.transpose(ps[7][:, t * P:t * P + P], pickw[:, t], ident[:, :])
                ins.then_inc(m.pickT_psum, 1)
                pe.wait_ge(m.hT_ready, q + 2)
                m.wait_landed(pe, q, 4)
                m.wait_landed(pe, q, 5)
                for n in range(2):
                    for c in range(FE // P):
                        for e in range(2):
                            w = ring[:, ESLOT[4 + e]].rearrange("p (c n) -> p c n", n=D)
                            ins = pe.matmul(ps[4 + n][BT * e:BT * e + BT, :], ehT[:, c, BT * e:BT * e + BT],
                                            w[:, c, n * NB:n * NB + NB], start=(c == 0), stop=(c == FE // P - 1),
                                            skip_group_check=True)
                    if n == 0:
                        ins.then_inc(m.down, 1)
                    else:
                        ins.then_inc(m.used, 2)
                pe.wait_ge(m.pickT_ready, q + 2)
                pe.wait_ge(m.o_act, q + 2)
                pe.wait_ge(m.o_dve, q + 2)
                for t in range(NT):
                    for n in range(2):
                        ins = pe.matmul(ps[2 * t + n][:, :], pickT[:, t * P:t * P + P], eo[:, n * NB:n * NB + NB],
                                        start=False, stop=True, skip_group_check=True)
                ins.then_inc(m.scattered, 1)

            pe.wait_ge(blocks_ready, 1)
            for i in range(4):
                pe.matmul(ps[i][:, :], zb[:, 0:P], zb[:, :], start=True, stop=True, skip_group_check=True)
            pe.wait_ge(main.pick_ready, 1)
            gather(main)
            pe.sem_inc(main.pickT_psum, 1)
            with pe.Fori(0, PAIRS) as q:
                pair(main, q)
            r.skip(ESLOT, PAIRS)
            pe.wait_ge(main.hT_ready, PAIRS + 1)
            pe.wait_ge(main.pickT_ready, PAIRS + 1)
            pe.wait_ge(main.xg_ready, 2 * PAIRS + 2)
            with pe.If(any_overflow(pe) > 0):
                pe.wait_ge(ovf.pick_ready, 1)
                gather(ovf)
                pe.sem_inc(ovf.pickT_psum, 1)
                with pe.Fori(0, OVF_PAIRS) as q:
                    pair(ovf, q)
            def norm2(i, j):
                norm_T(i)
                pe.wait_ge(hT_dve, 4 * (j + 1))
                pe.wait_ge(hT_act, 4 * (j + 1))

            def gate_rows(k, bank):
                pe.wait_ge(rep_ready, k + 1)
                for c in range(KC):
                    ins = pe.matmul(ps[bank + c // 4][:, (c % 4) * P:(c % 4) * P + P], rep[:, c], ident[:, :], start=True, stop=True)
                ins.then_inc(gate_psum, 1)

            def head_T(first, n, banks):
                def do(t):
                    for c in range(n):
                        ins = pe.transpose(ps[banks + c // 4][:, (c % 4) * P:(c % 4) * P + P],
                                           proj[:, t, first + c * P:first + c * P + P], ident[:, :])
                    ins.then_inc(heads_psum, 1)
                return do

            def in_parts(out, hi, lo, rhs_hi, rhs_lo, start, stop):
                pe.matmul(out, hi, rhs_hi, start=start, stop=False, skip_group_check=True)
                pe.matmul(out, hi, rhs_lo, start=False, stop=False, skip_group_check=True)
                return pe.matmul(out, lo, rhs_hi, start=False, stop=stop, skip_group_check=True)

            def product_in(name, s, bank, hi, t, slots):
                slot = slots[s]
                if t == 0:
                    r.take(slot)
                    pe.wait_ge(lo_ready, SPLIT[name] + s + 1)
                w_hi = high_place(name, s).rearrange("p (c n) -> p c n", n=NB)
                w_lo = ring_r[:, slot].rearrange("p (c n) -> p c n", n=NB)
                a = slice(t * P, t * P + P)
                for c in range(KC):
                    ins = in_parts(bank[:, :], hi[:, c, a], hT_r[:, c, a], w_hi[:, c], w_lo[:, c], c == 0, c == KC - 1)
                ins.then_inc(slabs_used if t else half_psum, 1)

            pe.wait_ge(x_ready, 8)
            norm2(3, 2)
            pe.wait_ge(h_lo_ready, 2)
            for s in range(5):
                for t in range(NT):
                    if s >= 2:
                        if s == 4:
                            pe.wait_ge(proj_dve, 2 + t + 1)
                        else:
                            pe.wait_ge(proj_act, 10 + 2 * (s - 2) + t + 1)
                    product_in("nsa_in", s, ps[(s % 2) * 2 + t], h_hi_nsa, t, NSLOT)
                if s == 0:
                    gate_rows(0, 4)
            pe.wait_ge(nsa_in_sem, 9 * 16)
            for t in range(NT):
                for c in range(KC):
                    for h in (h_hi_nsa, hT_r):
                        ins = pe.matmul(ps[7][:, t * 3 * QH:(t + 1) * 3 * QH], h[:, c, t * P:t * P + P].bitcast(F32), wgl[:, c],
                                        start=(c == 0 and h is h_hi_nsa), stop=(c == KC - 1 and h is hT_r))
            ins.then_inc(gl_psum, 1)
            pe.wait_ge(proj_dve, 4)
            pe.wait_ge(proj_act, 18)
            for w in range(2):
                for gp in range(2):
                    for t in range(NT):
                        at = 2 * NB + w * 256 + gp * P
                        ins = pe.transpose(ps[2 * w + gp][:, t * P:t * P + P], proj[:, t, at:at + P], ident[:, :])
                    ins.then_inc(kz_psum, 1)
            pe.wait_ge(rows_ready, 1)
            pe.wait_ge(kz_act, 8)
            pe.wait_ge(kz_dve, 8)
            for t in range(NT):
                head_T(0, 8, 2 * t)(t)
            arrived(NSLOT[5])
            pe.wait_ge(cv1_in, 16)
            cw1 = ring[:, NSLOT[5]].rearrange("p (w j m) -> p w j m", w=2, m=P)
            pe.wait_ge(gate_ready, 2)
            for w in range(2):
                pe.wait_ge(kz_dve if w else kz_act, 8)
                for j in range(16):
                    pe.matmul(ps[4 + w][:, 0:GR * NCMP], cw1[:, w, j], kz[:, w, :, 2 * j:2 * j + 16 * NCMP - 15:16],
                              start=(j == 0), stop=(j == 15))
                pe.wait_ge(pe_sum_ready, 1)
                pe.matmul(ps[4 + w][:, 64:65], pe_sum[:, w], ones[:, 0:1], start=True, stop=True).then_inc(cmp_psum, 1)
            for br in range(2):
                pe.wait_ge(rows_ready, 2 + br)
                if br:
                    pe.wait_ge(heads_dve, 2)
                else:
                    pe.wait_ge(heads_act, 2)
                for t in range(NT):
                    for g in range(GR):
                        at = 1536 + 512 * br + g * DH
                        ins = pe.transpose(ps[2 * br + t][0:DH, g * P:g * P + P], proj[:, t, at:at + DH], ident[:, :])
                ins.then_inc(heads_psum, 1)
            pe.wait_ge(cmp_act, 1)
            pe.matmul(ps[6][0:GR * NCMP, 0:DH], hc[:, 0], w2c[:, 0], start=True, stop=True).then_inc(cmp_psum, 1)
            pe.wait_ge(cmp_act, 2)
            pe.sem_inc(slabs_used, 1)
            pe.wait_ge(gl_dve, 1)
            for g in range(GR):
                ins = pe.matmul(ps[7][0:NCMP, g * DH:g * DH + DH], hc[:, 1, g * NCMP:(g + 1) * NCMP], w2c[:, 1], start=True, stop=True)
            ins.then_inc(cmp_psum, 1)
            pe.wait_ge(rows_ready, 4)
            pe.wait_ge(heads_act, 6)
            pe.wait_ge(heads_dve, 6)
            for t in range(NT):
                head_T(0, 8, 2 * t)(t)
            pe.wait_ge(cmp_dve, 1)
            pe.transpose(ps[6][0:DH, 64:64 + GR * NCMP], kcm[0:GR * NCMP], ident[0:GR * NCMP, 0:GR * NCMP]).then_inc(cmp_psum, 1)
            pe.wait_ge(heads_dve, 8)
            pe.wait_ge(heads_act, 8)

            def scores(u, t, g, br):
                if u >= 2:
                    pe.wait_ge(e_ready, 4 * (u - 1))
                nk = (t + 1) * P
                for j in range(2):
                    for o in range(2):
                        c = 2 * g + j
                        ins = pe.matmul(ps[2 * (u % 2) + o][:, j * S:j * S + nk], qrT[DH * o:DH * o + DH, c, t * P:t * P + P],
                                        kT[DH * o:DH * o + DH, br, g, 0:nk], start=True, stop=True)
                ins.then_inc(sc2_psum, 1)

            def transposes(u, t, g, br):
                n = u // 2
                if br:
                    if n:
                        pe.wait_ge(pcT_ready, n)
                    else:
                        pe.wait_ge(cw_ready, 1)
                    for o in range(2):
                        for j in range(2):
                            c = 2 * g + j
                            ins = pe.transpose(ps[7][0:NCMP, (2 * o + j) * P:(2 * o + j + 1) * P], csc[:, o, t, c * 16:c * 16 + NCMP], ident[:, :])
                    ins.then_inc(pcT_psum, 1)
                pe.wait_ge(p_ready, u + 1)
                if u >= 1:
                    pe.wait_ge(pT_act, u)
                    if u > 8:
                        pe.wait_ge(pT_dve, u - 8)
                for kb in range(t + 1):
                    for i in range(4):
                        ins = pe.transpose(ps[4 + kb][:, i * P:i * P + P], E[u % 3][:, i, kb * P:kb * P + P], ident[:, :])
                ins.then_inc(pT_psum, 1)

            def outputs(u, t, g, br):
                n = u // 2
                if br == 0 and n:
                    pe.wait_ge(ot_ready, n)
                pe.wait_ge(pT_act, u + 1)
                if t:
                    pe.wait_ge(pT_dve, u - 7)
                for kb in range(t + 1):
                    at = 1792 + 512 * br + g * DH
                    for o in range(2):
                        ins = pe.matmul(ps[6][DH * o:DH * o + DH, 0:S], proj[:, kb, at:at + DH], pT[u % 2][kb][:, 2 * o:2 * o + 2],
                                        start=(br == 0 and kb == 0), stop=False, skip_group_check=True)
                if br:
                    pe.wait_ge(pcT_ready, n + 1)
                    for o in range(2):
                        ins = pe.matmul(ps[6][DH * o:DH * o + DH, 0:S], vcm[0:NCMP, g], pcT[0:NCMP, n % 2, 2 * o:2 * o + 2],
                                        start=False, stop=True, skip_group_check=True)
                    ins.then_inc(ot_psum, 1)

            for i in range(NU + 3):
                for work_on, u in ((scores, i), (transposes, i - 2), (outputs, i - 3)):
                    if 0 <= u < NU:
                        work_on(u, u // 8, (u // 2) % GR, u % 2)
                if i == 2:
                    pe.wait_ge(cmp_dve, 4)
                    for t in range(NT):
                        for c in range(KC):
                            at = t * S + c * 32
                            ins = pe.matmul(ps[5][:, at:at + 32], qcT[:, c, t * P:t * P + P], kcT[:, c // 2], start=True, stop=True)
                    ins.then_inc(csc_psum, 1)
            pe.wait_ge(ot_ready, 8)
            pe.wait_ge(e_ready, 4 * NU)
            for s in range(2):
                arrived(NSLOT[s])
                for t in range(NT):
                    product(ps[2 * s + t], mixT, t, NSLOT[s]).then_inc(slabs_used if t else half_psum, 1)
            def mlp(l):
                norm2(4 + 2 * l, 3 + 2 * l)
                pe.wait_ge(x_ready, 16 + 8 * l)
                for i in range(4):
                    pe.matmul(ps[i][:, :], zb[:, 0:P], zb[:, :], start=True, stop=True, skip_group_check=True)

                def parts_of(n, wide):
                    return [ring_r[:, slot].rearrange("p (c n) -> p c n", n=wide) for slot in (HSLOT[l][n % 2], MSLOT[l][n % 4])]

                def hidden(k, i, n):
                    pe.wait_ge(lo_ready, i * 4 + (SPLIT[f"mlp{l}"] + n + 1))
                    if not isinstance(k, int) or k + l > 0:
                        pe.wait_ge(relu_ready, k * 2 + l * 2 * MC)
                    hi, lo = parts_of(n, NB)
                    for m in range(4):
                        for c in range(KC):
                            ins = in_parts(ps[4 + m // 2][:, (m % 2) * S:(m % 2) * S + S], hi[:, c, m * P:m * P + P],
                                           lo[:, c, m * P:m * P + P], h_hi_r[:, c], hT_r[:, c], c == 0, c == KC - 1)
                    ins.then_inc(slabs_used, 1)

                def output(k, par, i, n):
                    pe.wait_ge(hid_ready, k * 2 + (l * 2 * MC + 2))
                    pe.wait_ge(lo_ready, i * 4 + (SPLIT[f"mlp{l}"] + n + 1))
                    hi, lo = parts_of(n, D)
                    for t in range(NT):
                        for b in range(2):
                            a = slice(b * NB, b * NB + NB)
                            for c in range(4):
                                ins = in_parts(ps[2 * t + b][:, :], hid_hi_r[par][:, c, t * P:t * P + P], hid_lo[par][:, c, t * P:t * P + P],
                                               hi[:, c, a], lo[:, c, a], False, c == 3)
                    ins.then_inc(slabs_used, 1)

                pe.wait_ge(h_lo_ready, 4 * l + 4)
                hidden(0, 0, 0)
                gate_rows(1 + 2 * l, 6)
                with pe.Fori(0, 3) as i:
                    hidden(i * 2 + 1, i, 1)
                    output(i * 2, 0, i, 2)
                    hidden(i * 2 + 2, i, 3)
                    output(i * 2 + 1, 1, i, 4)
                hidden(7, 3, 1)
                output(6, 0, 3, 2)
                output(7, 1, 3, 3)
                r.skip(MSLOT[l], 4)

            mlp(0)
            norm2(5, 4)
            pe.wait_ge(h_lo_ready, 6)
            pe.wait_ge(x_ready, 20)
            for s in range(6):
                for t in range(NT):
                    if s >= 2:
                        pe.wait_ge(proj_act, 18 + 2 * (s - 2) + t + 1)
                    product_in("diff_in", s, ps[(s % 2) * 2 + t], h_hi_r, t, DSLOT)
                if s == 0:
                    gate_rows(2, 4)
            pe.wait_ge(proj_dve, 4 + 4)
            pe.wait_ge(proj_act, 26)
            pe.wait_ge(gate_ready, 6)
            for w in range(2):
                pe.wait_ge(rows_ready, 5 + w)
                for t in range(NT):
                    head_T(1024 * w, 8, (4 * w + 2 * t))(t)
            pe.wait_ge(heads_act, 12)
            pe.wait_ge(heads_dve, 12)

            def dscores(u):
                t, hp = u // 4, u % 4
                if u >= 2:
                    pe.wait_ge(e_ready, 4 * (NU + u - 1))
                nk = (t + 1) * P
                for j in range(2):
                    for o in range(2):
                        h = 2 * hp + j
                        ins = pe.matmul(ps[2 * (u % 2) + o][:, j * S:j * S + nk], dqT[0][DH * o:DH * o + DH, h, t * P:t * P + P],
                                        dqT[1][DH * o:DH * o + DH, h, 0:nk], start=True, stop=True)
                ins.then_inc(sc2_psum, 1)

            def dtransposes(u):
                pe.wait_ge(p_ready, NU + 2 * u + 2)
                for kb in range(u // 4 + 1):
                    for j in range(2):
                        ins = pe.transpose(ps[4 + u % 2][:, (2 * kb + j) * P:(2 * kb + j + 1) * P], E[(NU + u) % 3][:, j, kb * P:kb * P + P], ident[:, :])
                ins.then_inc(pT_psum, 1)

            def doutputs(u):
                t, hp = u // 4, u % 4
                pe.wait_ge(pT_act, NU + u + 1)
                if u >= 2:
                    pe.wait_ge(ot_ready, 8 + u - 1)
                for j in range(2):
                    h = 2 * hp + j
                    for kb in range(t + 1):
                        ins = pe.matmul(ps[6 + u % 2][:, j * P:j * P + P], pT[u % 2][0][:, 2 * kb + j], proj[:, kb, 2048 + h * P:2048 + h * P + P],
                                        start=(kb == 0), stop=(kb == t))
                ins.then_inc(ot_psum, 1)

            for i in range(NUD + 3):
                for work_on, u in ((dscores, i), (dtransposes, i - 2), (doutputs, i - 3)):
                    if 0 <= u < NUD:
                        work_on(u)
            pe.wait_ge(orow_ready, 2)
            for c in range(KC):
                for t in range(NT):
                    ins = pe.transpose(ps[c // 2][:, (c % 2) * S + t * P:(c % 2) * S + t * P + P], proj[:, t, c * P:c * P + P], ident[:, :])
                if c % 2:
                    ins.then_inc(abT_psum, 1)
            pe.wait_ge(mixT_dve, 8)
            pe.wait_ge(mixT_act, 8)
            for s in range(2):
                arrived(DSLOT[s])
                for t in range(NT):
                    product(ps[4 + 2 * s + t], mixT, t, DSLOT[s]).then_inc(slabs_used if t else half_psum, 1)
            mlp(1)


_INS = ["x", "norm1_gain", "w_in", "gmlp_v_gain", "gmlp_w_s", "gmlp_b_s", "hgrn_lower_bounds", "hgrn_out_gain",
        "w_out", "norm2_gain", "w_group_router", "b_group_router", "w_expert_router", "b_expert_router",
        "w_gate", "w_up", "w_down", "final_gain", "c_2", "positions_2", "ln_mix_g_2", "ln_mlp_g_2", "w_ada_2",
        "b_ada_2", "w_mlp_in_2", "w_mlp_out_2", "nsa_w_in_2", "nsa_b_gate_2", "nsa_q_gain_2", "nsa_k_gain_2",
        "nsa_pe_k_2", "nsa_w_ck1_2", "nsa_w_ck2_2", "nsa_pe_v_2", "nsa_w_cv1_2", "nsa_w_cv2_2", "nsa_w_out_2",
        "diff_w_in_2", "diff_q_gain_2", "diff_k_gain_2", "diff_lq1_2", "diff_lk1_2", "diff_lq2_2", "diff_lk2_2",
        "diff_subln_g_2", "diff_w_out_2"]
_KEEP = {"hgrn_lower_bounds", "final_gain", "ln_mix_g_2", "ln_mlp_g_2", "w_ada_2", "b_ada_2", "w_mlp_in_2",
         "w_mlp_out_2"}


def kernel(**inputs):
    import numpy as np
    import concourse.bacc as bacc
    from concourse.bass_utils import run_bass_kernel_spmd

    nc = bacc.Bacc("TRN2", target_bir_lowering=False, num_devices=1)
    arrays, d = {}, {}
    for name in _INS:
        a = np.ascontiguousarray(inputs[name])
        if name not in _KEEP:
            a = a[0]
        arrays[f"in_{name}"] = a
        d[name] = nc.dram_tensor(f"in_{name}", a.shape, mybir.dt.from_np(a.dtype), kind="ExternalInput").ap()
    out = nc.dram_tensor("out", (S, D), F32, kind="ExternalOutput").ap()
    build(nc, d, out)
    r = run_bass_kernel_spmd(nc, [arrays], core_ids=[0])
    return r.results[0]["out"].reshape(1, S, D)
```
